# Optimizing a Trainium2 kernel written in Bass

```python
import math
import jax, jax.numpy as jnp
from jax import lax
import numpy as np
import math, functools

D_MODEL = 1024
BATCH = 1
SEQ = 256
DEPTH = 1

RET_WIDTH = D_MODEL
RET_HEADS = 8
RET_HEAD_DIM = RET_WIDTH // RET_HEADS
RET_CHUNK = 128
ROPE_BASE = 10000.0
LRU_WIDTH = D_MODEL
LRU_BLOCKS = 8
LRU_BLOCK_DIM = LRU_WIDTH // LRU_BLOCKS
LRU_C = 8.0
CONV_WIDTH = 4
MIX_WIDTH = RET_WIDTH + LRU_WIDTH
IN_SPLITS = (RET_WIDTH, 2 * RET_WIDTH, 3 * RET_WIDTH, 4 * RET_WIDTH, 4 * RET_WIDTH + LRU_WIDTH)
IN_WIDTH = 4 * RET_WIDTH + 2 * LRU_WIDTH
NORM_EPS = 1e-6


def rms_norm(x, g):
    x32 = x.astype(jnp.float32)
    y = x32 * lax.rsqrt(jnp.mean(x32 * x32, axis=-1, keepdims=True) + NORM_EPS)
    return (y * g.astype(jnp.float32)).astype(x.dtype)

def rotary(x):
    T, d = x.shape[1], x.shape[-1]
    inv_freq = ROPE_BASE ** (-jnp.arange(0, d, 2, dtype=jnp.float32) / d)
    ang = jnp.arange(T, dtype=jnp.float32)[:, None] * inv_freq[None, :]
    cos = jnp.cos(ang)[None, :, None, :]
    sin = jnp.sin(ang)[None, :, None, :]
    x1, x2 = x[..., : d // 2], x[..., d // 2:]
    return jnp.concatenate([x1 * cos - x2 * sin, x1 * sin + x2 * cos], axis=-1)

def chunkwise_retention(q, k, v):
    B, T, H, d = q.shape
    C = RET_CHUNK
    nc = T // C
    log_g = jnp.log1p(-jnp.exp2(-5.0 - jnp.arange(H, dtype=jnp.float32)))
    idx = jnp.arange(C, dtype=jnp.float32)
    rel = idx[:, None] - idx[None, :]
    decay_mat = jnp.where(rel[None] >= 0,
                          jnp.exp(jnp.maximum(rel, 0.0)[None] * log_g[:, None, None]), 0.0)
    zeta = jnp.exp((C - 1 - idx)[None, :] * log_g[:, None])
    xi = jnp.exp((idx + 1)[None, :] * log_g[:, None])
    chunk_decay = jnp.exp(C * log_g)

    qc = q.reshape(B, nc, C, H, d)
    kc = k.reshape(B, nc, C, H, d)
    vc = v.reshape(B, nc, C, H, d)

    scores = jnp.einsum('bnqhd,bnkhd->bnhqk', qc, kc) * decay_mat[None, None]
    intra = jnp.einsum('bnhqk,bnkhe->bnqhe', scores, vc)

    kv = jnp.einsum('bnkhd,hk,bnkhe->nbhde', kc, zeta, vc)

    def step(state, kv_n):
        new_state = chunk_decay[None, :, None, None] * state + kv_n
        return new_state, state

    _, prev_states = lax.scan(step, jnp.zeros((B, H, d, d), jnp.float32), kv)
    prev_states = jnp.moveaxis(prev_states, 0, 1)
    cross = jnp.einsum('bnqhd,bnhde->bnqhe', qc, prev_states) * xi.T[None, None, :, :, None]
    return (intra + cross).reshape(B, T, H, d)

def group_norm_heads(o):
    mu = jnp.mean(o, axis=-1, keepdims=True)
    var = jnp.mean(jnp.square(o - mu), axis=-1, keepdims=True)
    return (o - mu) * lax.rsqrt(var + NORM_EPS)

def causal_depthwise_conv(x, w, b):
    T = x.shape[1]
    xp = jnp.pad(x, ((0, 0), (CONV_WIDTH - 1, 0), (0, 0)))
    out = b[None, None, :]
    for j in range(CONV_WIDTH):
        out = out + xp[:, j:j + T, :] * w[j][None, None, :]
    return out

def block_diag_linear(x, w, b):
    B, T, _ = x.shape
    xb = x.reshape(B, T, LRU_BLOCKS, LRU_BLOCK_DIM)
    y = jnp.einsum('btni,nio->btno', xb, w) + b[None, None]
    return y.reshape(B, T, LRU_WIDTH)

def rg_lru(x, gate_a_w, gate_a_b, gate_x_w, gate_x_b, lru_lambda):
    r = jax.nn.sigmoid(block_diag_linear(x, gate_a_w, gate_a_b))
    i = jax.nn.sigmoid(block_diag_linear(x, gate_x_w, gate_x_b))
    log_a = -LRU_C * r * jax.nn.softplus(-lru_lambda)[None, None, :]
    a = jnp.exp(log_a)
    mult = jnp.sqrt(jnp.maximum(1.0 - jnp.exp(2.0 * log_a), 0.0))
    b = mult * (i * x)

    def combine(left, right):
        a_l, b_l = left
        a_r, b_r = right
        return a_l * a_r, a_r * b_l + b_r

    _, h = lax.associative_scan(combine, (a, b), axis=1)
    return h

def first_inputs(seed: int = 0) -> dict:
    key = jax.random.key(seed)
    ks = jax.random.split(key, 14)
    f32 = jnp.float32
    x = jax.random.normal(ks[0], (BATCH, SEQ, D_MODEL), f32)
    norm_in_g = 1.0 + 0.05 * jax.random.normal(ks[1], (D_MODEL,), f32)
    w_in = jax.random.normal(ks[2], (D_MODEL, IN_WIDTH), f32) * D_MODEL ** -0.5
    conv_w = jax.random.normal(ks[3], (CONV_WIDTH, LRU_WIDTH), f32) * CONV_WIDTH ** -0.5
    conv_b = 0.01 * jax.random.normal(ks[4], (LRU_WIDTH,), f32)
    gate_a_w = jax.random.normal(ks[5], (LRU_BLOCKS, LRU_BLOCK_DIM, LRU_BLOCK_DIM), f32) * LRU_BLOCK_DIM ** -0.5
    gate_a_b = 0.01 * jax.random.normal(ks[6], (LRU_BLOCKS, LRU_BLOCK_DIM), f32)
    gate_x_w = jax.random.normal(ks[7], (LRU_BLOCKS, LRU_BLOCK_DIM, LRU_BLOCK_DIM), f32) * LRU_BLOCK_DIM ** -0.5
    gate_x_b = 0.01 * jax.random.normal(ks[8], (LRU_BLOCKS, LRU_BLOCK_DIM), f32)
    a_c = jax.random.uniform(ks[9], (LRU_WIDTH,), f32, minval=0.9, maxval=0.999)
    a0 = a_c ** (1.0 / LRU_C)
    lru_lambda = jnp.log(a0) - jnp.log1p(-a0)
    w_out = jax.random.normal(ks[10], (MIX_WIDTH, D_MODEL), f32) * MIX_WIDTH ** -0.5
    norm_out_g = 1.0 + 0.05 * jax.random.normal(ks[11], (D_MODEL,), f32)
    return {"x": x, "norm_in_g": norm_in_g, "w_in": w_in, "conv_w": conv_w, "conv_b": conv_b,
            "gate_a_w": gate_a_w, "gate_a_b": gate_a_b, "gate_x_w": gate_x_w, "gate_x_b": gate_x_b,
            "lru_lambda": lru_lambda, "w_out": w_out, "norm_out_g": norm_out_g}

def first_block(x, norm_in_g, w_in, conv_w, conv_b, gate_a_w, gate_a_b, gate_x_w, gate_x_b,
              lru_lambda, w_out, norm_out_g):
    B, T, _ = x.shape
    f32 = jnp.float32
    h = x
    for _layer in range(DEPTH):
        xn = rms_norm(h, norm_in_g)
        proj = jnp.einsum('btd,de->bte', xn, w_in).astype(f32)
        q, k, v, g_ret, x_lru, g_lru = jnp.split(proj, IN_SPLITS, axis=-1)

        q = rotary(q.reshape(B, T, RET_HEADS, RET_HEAD_DIM))
        k = rotary(k.reshape(B, T, RET_HEADS, RET_HEAD_DIM)) * RET_HEAD_DIM ** -0.5
        v = v.reshape(B, T, RET_HEADS, RET_HEAD_DIM)
        o_ret = group_norm_heads(chunkwise_retention(q, k, v)).reshape(B, T, RET_WIDTH)
        y_ret = o_ret * jax.nn.silu(g_ret)

        xc = causal_depthwise_conv(x_lru, conv_w.astype(f32), conv_b.astype(f32))
        o_lru = rg_lru(xc, gate_a_w.astype(f32), gate_a_b.astype(f32), gate_x_w.astype(f32),
                       gate_x_b.astype(f32), lru_lambda.astype(f32))
        y_lru = o_lru * jax.nn.silu(g_lru)

        mixed = jnp.concatenate([y_ret, y_lru], axis=-1).astype(x.dtype)
        h = h + jnp.einsum('bte,ed->btd', mixed, w_out)
    return rms_norm(h, norm_out_g)


D_MIX = D_MODEL
HEAD_DIM = 64
ATTN_WIDTH = D_MIX // 2
CONV_WIDTH_2 = D_MIX // 4
POOL_WIDTH = D_MIX - ATTN_WIDTH - CONV_WIDTH_2
N_ATTN_HEADS = ATTN_WIDTH // HEAD_DIM
POOL_WINDOWS = (2, 4, 8, 16)
N_POOL_GROUPS = len(POOL_WINDOWS)
POOL_GROUP = POOL_WIDTH // N_POOL_GROUPS
CONV_K = 3
MOBA_BLOCK = 256
MOBA_TOP_K = 3
NUM_BUCKETS = 32
MAX_DISTANCE = 1024
D_FF = ((8 * D_MODEL // 3 + 255) // 256) * 256
IN_COLS = 3 * ATTN_WIDTH + 3 * CONV_WIDTH_2 + POOL_WIDTH
DEEPNORM_ALPHA = (2.0 * DEPTH) ** 0.25
DEEPNORM_BETA = (8.0 * DEPTH) ** -0.25
LN_EPS = 1e-5
NEG_INF = -1e30


def layer_norm(x, g, b):
    xf = x.astype(jnp.float32)
    mu = xf.mean(-1, keepdims=True)
    var = jnp.square(xf - mu).mean(-1, keepdims=True)
    return ((xf - mu) * lax.rsqrt(var + LN_EPS)).astype(x.dtype) * g + b

def causal_dwconv(x, w):
    S = x.shape[1]
    xp = jnp.pad(x, ((0, 0), (CONV_K - 1, 0), (0, 0)))
    return sum(xp[:, j:j + S] * w[j] for j in range(CONV_K))

def t5_bucket(dist):
    n = jnp.maximum(dist, 0)
    max_exact = NUM_BUCKETS // 2
    nf = jnp.maximum(n, 1).astype(jnp.float32)
    large = max_exact + (jnp.log(nf / max_exact) / math.log(MAX_DISTANCE / max_exact)
                         * (NUM_BUCKETS - max_exact)).astype(jnp.int32)
    large = jnp.minimum(large, NUM_BUCKETS - 1)
    return jnp.where(n < max_exact, n, large)

def _moba_query_block(i, n_sel, args):
    qh, selh, kh, vh, tab = args
    L = MOBA_BLOCK
    scale = HEAD_DIM ** -0.5
    r = jnp.arange(L)
    rel = r[:, None] - r[None, :]
    own_logits = (jnp.einsum('qd,ld->ql', qh, kh[i]).astype(jnp.float32) * scale
                  + tab[t5_bucket(rel)].astype(jnp.float32))
    own_logits = jnp.where(rel >= 0, own_logits, NEG_INF)
    if n_sel == 0:
        p = jax.nn.softmax(own_logits, axis=-1).astype(vh.dtype)
        return jnp.einsum('ql,ld->qd', p, vh[i])
    k_sel = kh[selh]
    v_sel = vh[selh]
    dist = (i - selh)[:, :, None] * L + rel[:, None, :]
    sel_logits = (jnp.einsum('qd,qnld->qnl', qh, k_sel).astype(jnp.float32) * scale
                  + tab[t5_bucket(dist)].astype(jnp.float32))
    logits = jnp.concatenate([sel_logits.reshape(L, n_sel * L), own_logits], axis=-1)
    p = jax.nn.softmax(logits, axis=-1).astype(vh.dtype)
    p_sel = p[:, :n_sel * L].reshape(L, n_sel, L)
    p_own = p[:, n_sel * L:]
    return jnp.einsum('qnl,qnld->qd', p_sel, v_sel) + jnp.einsum('ql,ld->qd', p_own, vh[i])

def moba_attention(q, k, v, rel_bias):
    B, H, S, Dh = q.shape
    L = MOBA_BLOCK
    nb = -(-S // L)
    pad = nb * L - S
    if pad:
        cfg = ((0, 0), (0, 0), (0, pad), (0, 0))
        q, k, v = jnp.pad(q, cfg), jnp.pad(k, cfg), jnp.pad(v, cfg)
    qb = q.reshape(B, H, nb, L, Dh)
    kb = k.reshape(B, H, nb, L, Dh)
    vb = v.reshape(B, H, nb, L, Dh)
    k_mean = kb.astype(jnp.float32).mean(axis=3).astype(k.dtype)
    k_flat = kb.reshape(B * H, nb, L, Dh)
    v_flat = vb.reshape(B * H, nb, L, Dh)
    tab = jnp.broadcast_to(rel_bias[None], (B,) + rel_bias.shape).reshape(B * H, NUM_BUCKETS)
    outs = []
    for i in range(nb):
        q_i = qb[:, :, i]
        n_sel = min(MOBA_TOP_K, i)
        if n_sel:
            gate = jnp.einsum('bhqd,bhnd->bhqn', q_i, k_mean[:, :, :i]).astype(jnp.float32)
            _, sel = lax.top_k(gate, n_sel)
            sel = sel.reshape(B * H, L, n_sel)
        else:
            sel = jnp.zeros((B * H, L, 0), jnp.int32)
        step = functools.partial(_moba_query_block, i, n_sel)
        outs.append(lax.map(step, (q_i.reshape(B * H, L, Dh), sel, k_flat, v_flat, tab)))
    out = jnp.concatenate(outs, axis=1).reshape(B, H, nb * L, Dh)
    return out[:, :, :S]

def pool_mixer(p, w_pool, pool_scale):
    B, S, _ = p.shape
    pg = p.reshape(B, S, N_POOL_GROUPS, POOL_GROUP)
    pf = pg.astype(jnp.float32)
    c = jnp.cumsum(pf, axis=1)
    pos = jnp.arange(1, S + 1, dtype=jnp.float32)
    means = []
    for g, w in enumerate(POOL_WINDOWS):
        cg = c[:, :, g]
        lag = jnp.pad(cg, ((0, 0), (w, 0), (0, 0)))[:, :S]
        means.append((cg - lag) / jnp.minimum(pos, float(w))[None, :, None])
    pooled = (jnp.stack(means, axis=2) - pf).astype(p.dtype)
    y = jnp.einsum('bsgc,gcd->bsgd', pooled, w_pool)
    return y.reshape(B, S, POOL_WIDTH) * pool_scale

def to_heads(t):
    B, S, _ = t.shape
    return t.reshape(B, S, -1, HEAD_DIM).transpose(0, 2, 1, 3)

def hybrid_layer(x, w_in, conv_w, w_pool, pool_scale, w_out, ln1_g, ln1_b,
                 w_up, ffn_conv_w, ffn_conv_b, w_down, ln2_g, ln2_b, rel_bias):
    B, S, _ = x.shape
    h = x @ w_in
    sizes = [ATTN_WIDTH, ATTN_WIDTH, ATTN_WIDTH, CONV_WIDTH_2, CONV_WIDTH_2, CONV_WIDTH_2]
    q, k, v, cb, cc, cx, pin = jnp.split(h, list(np.cumsum(sizes)), axis=-1)
    attn = moba_attention(to_heads(q), to_heads(k), to_heads(v), rel_bias)
    attn = attn.transpose(0, 2, 1, 3).reshape(B, S, ATTN_WIDTH)
    conv = cb * causal_dwconv(cc * cx, conv_w)
    pool = pool_mixer(pin, w_pool, pool_scale)
    mix = jnp.concatenate([attn, conv, pool], axis=-1) @ w_out
    x = layer_norm(DEEPNORM_ALPHA * x + mix, ln1_g, ln1_b)
    up = causal_dwconv(x @ w_up, ffn_conv_w) + ffn_conv_b
    u, g = jnp.split(up, 2, axis=-1)
    ff = (u * jax.nn.silu(g)) @ w_down
    return layer_norm(DEEPNORM_ALPHA * x + ff, ln2_g, ln2_b)

def second_inputs(seed: int = 0) -> dict:
    key = jax.random.key(seed)
    ks = jax.random.split(key, 16)
    nrm = jax.random.normal
    return {
        'x': nrm(ks[0], (BATCH, SEQ, D_MODEL), jnp.float32),
        'w_in': nrm(ks[1], (DEPTH, D_MODEL, IN_COLS), jnp.float32) * D_MODEL ** -0.5,
        'conv_w': nrm(ks[2], (DEPTH, CONV_K, CONV_WIDTH_2), jnp.float32) * CONV_K ** -0.5,
        'w_pool': nrm(ks[3], (DEPTH, N_POOL_GROUPS, POOL_GROUP, POOL_GROUP), jnp.float32) * POOL_GROUP ** -0.5,
        'pool_scale': 1.0 + 0.02 * nrm(ks[4], (DEPTH, POOL_WIDTH), jnp.float32),
        'w_out': nrm(ks[5], (DEPTH, D_MIX, D_MODEL), jnp.float32) * (D_MIX ** -0.5 * DEEPNORM_BETA),
        'ln1_g': 1.0 + 0.02 * nrm(ks[6], (DEPTH, D_MODEL), jnp.float32),
        'ln1_b': 0.02 * nrm(ks[7], (DEPTH, D_MODEL), jnp.float32),
        'w_up': nrm(ks[8], (DEPTH, D_MODEL, 2 * D_FF), jnp.float32) * D_MODEL ** -0.5,
        'ffn_conv_w': nrm(ks[9], (DEPTH, CONV_K, 2 * D_FF), jnp.float32) * CONV_K ** -0.5,
        'ffn_conv_b': 0.02 * nrm(ks[10], (DEPTH, 2 * D_FF), jnp.float32),
        'w_down': nrm(ks[11], (DEPTH, D_FF, D_MODEL), jnp.float32) * (D_FF ** -0.5 * DEEPNORM_BETA),
        'ln2_g': 1.0 + 0.02 * nrm(ks[12], (DEPTH, D_MODEL), jnp.float32),
        'ln2_b': 0.02 * nrm(ks[13], (DEPTH, D_MODEL), jnp.float32),
        'rel_bias': 0.5 * nrm(ks[14], (N_ATTN_HEADS, NUM_BUCKETS), jnp.float32),
    }

def second_block(x, w_in, conv_w, w_pool, pool_scale, w_out, ln1_g, ln1_b,
              w_up, ffn_conv_w, ffn_conv_b, w_down, ln2_g, ln2_b, rel_bias):
    for l in range(DEPTH):
        x = hybrid_layer(x, w_in[l], conv_w[l], w_pool[l], pool_scale[l], w_out[l],
                         ln1_g[l], ln1_b[l], w_up[l], ffn_conv_w[l], ffn_conv_b[l],
                         w_down[l], ln2_g[l], ln2_b[l], rel_bias)
    return x


_first_inputs = second_inputs


def second_inputs(seed=0):
    import zlib

    import numpy as np

    out = dict(_first_inputs(seed))
    spreads = {}
    factors = {'pool_scale': 8.0, 'ln1_b': 2.784, 'ffn_conv_b': 7.017, 'ln2_g': 2.89, 'ln2_b': 2.747}
    for name, (base, spread) in spreads.items():
        noise = np.random.default_rng([zlib.crc32(name.encode()), seed]).standard_normal(out[name].shape)
        drawn = base * np.exp(spread * noise) if base else spread * noise
        out[name] = __import__('jax').numpy.asarray(drawn.astype(out[name].dtype))
    for name, factor in factors.items():
        out[name] = (out[name] * factor).astype(out[name].dtype)
    return out


_narrow_inputs = second_inputs


def second_inputs(seed=0):

    out = dict(_narrow_inputs(seed))
    wider = {'pool_scale': 3.68, 'ln2_g': 3.24, 'ln2_b': 3.25, 'rel_bias': 4.28}
    for name, times in wider.items():
        mean = out[name].mean()
        out[name] = (mean + times * (out[name] - mean)).astype(out[name].dtype)
    return out


DEPTH_3 = 2

N_MIXERS = 2
N_RWKV_LAYERS = (DEPTH_3 + 1) // 2
N_GMLP_LAYERS = DEPTH_3 // 2
N_MEM = 256

RWKV_HEAD = 64
RWKV_HEADS = D_MODEL // RWKV_HEAD
LORA_DECAY = 64
LORA_AAA = 64
LORA_GATE = 160
GN_EPS = 64e-5

GMLP_CHUNK = 128
GMLP_WIDTH = 2 * D_MODEL
GMLP_GROUP_DIM = 128
GMLP_GROUPS = GMLP_WIDTH // GMLP_GROUP_DIM

XATTN_HEADS = 4
XATTN_HEAD_DIM = D_MODEL // XATTN_HEADS

D_FF_3 = 2816
RMS_EPS = 1e-6


def rms_norm_3(x, g):
    x32 = x.astype(jnp.float32)
    y = x32 * lax.rsqrt(jnp.mean(x32 * x32, axis=-1, keepdims=True) + RMS_EPS)
    return (y * g.astype(jnp.float32)).astype(x.dtype)

def swiglu_ffn(h, w_in, w_out):
    gate, up = jnp.split(h @ w_in, 2, axis=-1)
    return (jax.nn.silu(gate) * up) @ w_out

def token_shift(x):
    return jnp.pad(x[:, :-1], ((0, 0), (1, 0), (0, 0)))

def rwkv7_time_mix(h, mu, w_rkv, w0, w1, w2, a0, a1, a2, g1, g2, k_k, k_a, r_k, ln_w, ln_b, w_o):
    B, S, C = h.shape
    H, N = RWKV_HEADS, RWKV_HEAD
    dx = token_shift(h) - h
    xr = h + dx * mu[0]
    xw = h + dx * mu[1]
    xk = h + dx * mu[2]
    xv = h + dx * mu[3]
    xa = h + dx * mu[4]
    xg = h + dx * mu[5]
    x3 = jnp.stack([xr, xk, xv], axis=0)
    rkv = jnp.einsum('nbsc,cnd->nbsd', x3, w_rkv.reshape(C, 3, C))
    r, k, v = rkv[0], rkv[1], rkv[2]
    w = -jax.nn.softplus(-(w0 + jnp.tanh(xw @ w1) @ w2)) - 0.5
    decay = jnp.exp(-jnp.exp(w.astype(jnp.float32)))
    a = jax.nn.sigmoid(a0 + (xa @ a1) @ a2)
    g = jax.nn.sigmoid(xg @ g1) @ g2
    kk = (k * k_k).reshape(B, S, H, N).astype(jnp.float32)
    kk = kk / jnp.maximum(jnp.linalg.norm(kk, axis=-1, keepdims=True), 1e-12)
    k = k * (1.0 + (a - 1.0) * k_a)

    def heads(t):
        return t.reshape(B, S, H, N).astype(jnp.float32)

    r_h, k_h, v_h, a_h = heads(r), heads(k), heads(v), heads(a)
    b_h = kk * a_h
    xs = tuple(jnp.moveaxis(t, 1, 0) for t in (r_h, heads(decay), k_h, v_h, kk, b_h))

    def step(state, inp):
        r_t, w_t, k_t, v_t, kk_t, b_t = inp
        sa = jnp.einsum('bhij,bhj->bhi', state, -kk_t)
        state = (state * w_t[:, :, None, :] + sa[..., None] * b_t[:, :, None, :]
                 + v_t[..., :, None] * k_t[:, :, None, :])
        y = jnp.einsum('bhij,bhj->bhi', state, r_t)
        return state, y

    s0 = jnp.zeros((B, H, N, N), jnp.float32)
    _, ys = lax.scan(step, s0, xs)
    y = jnp.moveaxis(ys, 0, 1)
    mean = jnp.mean(y, axis=-1, keepdims=True)
    var = jnp.mean(jnp.square(y - mean), axis=-1, keepdims=True)
    y = ((y - mean) * lax.rsqrt(var + GN_EPS)).reshape(B, S, C)
    y = y * ln_w.astype(jnp.float32) + ln_b.astype(jnp.float32)
    bonus = jnp.sum(r_h * k_h * r_k.astype(jnp.float32), axis=-1, keepdims=True) * v_h
    y = (y + bonus.reshape(B, S, C)).astype(h.dtype)
    return (y * g) @ w_o

def gmlp_chunk_mix(h, w_uv, v_norm, w_s, b_s, w_o):
    B, S, _ = h.shape
    z = jax.nn.gelu(h @ w_uv)
    u, v = jnp.split(z, 2, axis=-1)
    v = rms_norm_3(v, v_norm)
    v = v.reshape(B, S // GMLP_CHUNK, GMLP_CHUNK, GMLP_GROUPS, GMLP_GROUP_DIM)
    causal = jnp.tril(jnp.ones((GMLP_CHUNK, GMLP_CHUNK), dtype=bool))
    ws = jnp.where(causal[None], w_s, jnp.zeros_like(w_s))
    sv = jnp.einsum('gts,bcsgd->bctgd', ws, v) + jnp.transpose(b_s)[:, :, None]
    sv = sv.reshape(B, S, GMLP_WIDTH)
    return (u * sv) @ w_o

def memory_cross_attention(h, mem_k, mem_v, wq, wo):
    B, S, C = h.shape
    q = (h @ wq).reshape(B, S, XATTN_HEADS, XATTN_HEAD_DIM)
    s = jnp.einsum('bshd,bmhd->bhsm', q, mem_k).astype(jnp.float32) * (XATTN_HEAD_DIM ** -0.5)
    p = jax.nn.softmax(s, axis=-1).astype(h.dtype)
    o = jnp.einsum('bhsm,bmhd->bshd', p, mem_v).reshape(B, S, C)
    return o @ wo

def third_inputs(seed: int = 0) -> dict:
    key = jax.random.key(seed)
    ks = iter(jax.random.split(key, 48))
    C, F = D_MODEL, D_FF_3
    L, NA, NB = DEPTH_3, N_RWKV_LAYERS, N_GMLP_LAYERS

    def nrm(shape, scale):
        return jax.random.normal(next(ks), shape, jnp.float32) * scale

    def gain(shape):
        return 1.0 + 0.05 * jax.random.normal(next(ks), shape, jnp.float32)

    return {
        "x": jax.random.normal(next(ks), (BATCH, SEQ, C), jnp.float32),
        "mem": jax.random.normal(next(ks), (BATCH, N_MEM, C), jnp.float32),
        "mem_norm": gain((C,)),
        "mem_w_kv": nrm((C, 2 * C), C ** -0.5),
        "ffn1_norm": gain((L, C)),
        "ffn1_w_in": nrm((L, C, 2 * F), C ** -0.5),
        "ffn1_w_out": nrm((L, F, C), F ** -0.5),
        "mix_norm": gain((L, C)),
        "xattn_norm": gain((L, C)),
        "xattn_wq": nrm((L, C, C), C ** -0.5),
        "xattn_wo": nrm((L, C, C), C ** -0.5),
        "ffn2_norm": gain((L, C)),
        "ffn2_w_in": nrm((L, C, 2 * F), C ** -0.5),
        "ffn2_w_out": nrm((L, F, C), F ** -0.5),
        "rwkv_mu": jax.random.uniform(next(ks), (NA, 6, C), jnp.float32),
        "rwkv_w_rkv": nrm((NA, C, 3 * C), C ** -0.5),
        "rwkv_w0": jax.random.uniform(next(ks), (NA, C), jnp.float32, -6.0, -0.5),
        "rwkv_w1": nrm((NA, C, LORA_DECAY), C ** -0.5),
        "rwkv_w2": nrm((NA, LORA_DECAY, C), 0.5 * LORA_DECAY ** -0.5),
        "rwkv_a0": nrm((NA, C), 0.1),
        "rwkv_a1": nrm((NA, C, LORA_AAA), C ** -0.5),
        "rwkv_a2": nrm((NA, LORA_AAA, C), 0.5 * LORA_AAA ** -0.5),
        "rwkv_g1": nrm((NA, C, LORA_GATE), C ** -0.5),
        "rwkv_g2": nrm((NA, LORA_GATE, C), LORA_GATE ** -0.5),
        "rwkv_k_k": gain((NA, C)),
        "rwkv_k_a": gain((NA, C)),
        "rwkv_r_k": nrm((NA, RWKV_HEADS, RWKV_HEAD), 0.1),
        "rwkv_ln_w": gain((NA, C)),
        "rwkv_ln_b": nrm((NA, C), 0.01),
        "rwkv_w_o": nrm((NA, C, C), C ** -0.5),
        "gmlp_w_uv": nrm((NB, C, 2 * GMLP_WIDTH), C ** -0.5),
        "gmlp_v_norm": gain((NB, GMLP_WIDTH)),
        "gmlp_w_s": nrm((NB, GMLP_GROUPS, GMLP_CHUNK, GMLP_CHUNK), 0.5 * GMLP_CHUNK ** -0.5),
        "gmlp_b_s": gain((NB, GMLP_GROUPS, GMLP_CHUNK)),
        "gmlp_w_o": nrm((NB, GMLP_WIDTH, C), GMLP_WIDTH ** -0.5),
        "final_norm": gain((C,)),
    }

def third_block(x, mem, mem_norm, mem_w_kv,
              ffn1_norm, ffn1_w_in, ffn1_w_out, mix_norm, xattn_norm, xattn_wq, xattn_wo,
              ffn2_norm, ffn2_w_in, ffn2_w_out,
              rwkv_mu, rwkv_w_rkv, rwkv_w0, rwkv_w1, rwkv_w2, rwkv_a0, rwkv_a1, rwkv_a2,
              rwkv_g1, rwkv_g2, rwkv_k_k, rwkv_k_a, rwkv_r_k, rwkv_ln_w, rwkv_ln_b, rwkv_w_o,
              gmlp_w_uv, gmlp_v_norm, gmlp_w_s, gmlp_b_s, gmlp_w_o,
              final_norm):
    B = mem.shape[0]
    mem_k, mem_v = jnp.split(rms_norm_3(mem, mem_norm) @ mem_w_kv, 2, axis=-1)
    mem_k = mem_k.reshape(B, N_MEM, XATTN_HEADS, XATTN_HEAD_DIM)
    mem_v = mem_v.reshape(B, N_MEM, XATTN_HEADS, XATTN_HEAD_DIM)

    for i in range(DEPTH_3):
        x = x + 0.5 * swiglu_ffn(rms_norm_3(x, ffn1_norm[i]), ffn1_w_in[i], ffn1_w_out[i])
        h = rms_norm_3(x, mix_norm[i])
        j = i // N_MIXERS
        if i % N_MIXERS == 0:
            y = rwkv7_time_mix(h, rwkv_mu[j], rwkv_w_rkv[j], rwkv_w0[j], rwkv_w1[j], rwkv_w2[j],
                               rwkv_a0[j], rwkv_a1[j], rwkv_a2[j], rwkv_g1[j], rwkv_g2[j],
                               rwkv_k_k[j], rwkv_k_a[j], rwkv_r_k[j], rwkv_ln_w[j], rwkv_ln_b[j],
                               rwkv_w_o[j])
        else:
            y = gmlp_chunk_mix(h, gmlp_w_uv[j], gmlp_v_norm[j], gmlp_w_s[j], gmlp_b_s[j], gmlp_w_o[j])
        x = x + y
        x = x + memory_cross_attention(rms_norm_3(x, xattn_norm[i]), mem_k, mem_v,
                                       xattn_wq[i], xattn_wo[i])
        x = x + 0.5 * swiglu_ffn(rms_norm_3(x, ffn2_norm[i]), ffn2_w_in[i], ffn2_w_out[i])
    return rms_norm_3(x, final_norm)


def setup_inputs(seed=0):
    out = dict(first_inputs(seed))
    for name, value in second_inputs(seed + 1).items():
        if name != "x":
            out[name + "_2"] = value
    for name, value in third_inputs(seed + 2).items():
        if name != "x":
            out[name + "_3"] = value
    return out


def reference(
    x, norm_in_g, w_in, conv_w, conv_b, gate_a_w, gate_a_b, gate_x_w, gate_x_b, lru_lambda,
    w_out, norm_out_g, w_in_2, conv_w_2, w_pool_2, pool_scale_2, w_out_2, ln1_g_2, ln1_b_2,
    w_up_2, ffn_conv_w_2, ffn_conv_b_2, w_down_2, ln2_g_2, ln2_b_2, rel_bias_2, mem_3,
    mem_norm_3, mem_w_kv_3, ffn1_norm_3, ffn1_w_in_3, ffn1_w_out_3, mix_norm_3, xattn_norm_3,
    xattn_wq_3, xattn_wo_3, ffn2_norm_3, ffn2_w_in_3, ffn2_w_out_3, rwkv_mu_3, rwkv_w_rkv_3,
    rwkv_w0_3, rwkv_w1_3, rwkv_w2_3, rwkv_a0_3, rwkv_a1_3, rwkv_a2_3, rwkv_g1_3, rwkv_g2_3,
    rwkv_k_k_3, rwkv_k_a_3, rwkv_r_k_3, rwkv_ln_w_3, rwkv_ln_b_3, rwkv_w_o_3, gmlp_w_uv_3,
    gmlp_v_norm_3, gmlp_w_s_3, gmlp_b_s_3, gmlp_w_o_3, final_norm_3,
):
    x = first_block(
        x, norm_in_g, w_in, conv_w, conv_b, gate_a_w, gate_a_b, gate_x_w, gate_x_b, lru_lambda,
        w_out, norm_out_g,
    )
    x = second_block(
        x, w_in_2, conv_w_2, w_pool_2, pool_scale_2, w_out_2, ln1_g_2, ln1_b_2, w_up_2,
        ffn_conv_w_2, ffn_conv_b_2, w_down_2, ln2_g_2, ln2_b_2, rel_bias_2,
    )
    return third_block(
        x, mem_3, mem_norm_3, mem_w_kv_3, ffn1_norm_3, ffn1_w_in_3, ffn1_w_out_3, mix_norm_3,
        xattn_norm_3, xattn_wq_3, xattn_wo_3, ffn2_norm_3, ffn2_w_in_3, ffn2_w_out_3, rwkv_mu_3,
        rwkv_w_rkv_3, rwkv_w0_3, rwkv_w1_3, rwkv_w2_3, rwkv_a0_3, rwkv_a1_3, rwkv_a2_3,
        rwkv_g1_3, rwkv_g2_3, rwkv_k_k_3, rwkv_k_a_3, rwkv_r_k_3, rwkv_ln_w_3, rwkv_ln_b_3,
        rwkv_w_o_3, gmlp_w_uv_3, gmlp_v_norm_3, gmlp_w_s_3, gmlp_b_s_3, gmlp_w_o_3,
        final_norm_3,
    )


_drawn_inputs = setup_inputs


def setup_inputs(seed=0):
    import zlib

    import numpy as np

    out = dict(_drawn_inputs(seed))
    spreads = {}
    factors = {'conv_b': 3.721,
     'gate_a_b': 8.0,
     'gate_x_b': 8.0,
     'mem_norm_3': 8.0,
     'ffn1_norm_3': 5.315,
     'xattn_norm_3': 8.0,
     'ffn2_norm_3': 5.523,
     'rwkv_w1_3': 8.0,
     'rwkv_w2_3': 8.0,
     'rwkv_a0_3': 6.872,
     'rwkv_k_k_3': 8.0,
     'rwkv_k_a_3': 5.341,
     'rwkv_ln_w_3': 6.423,
     'rwkv_ln_b_3': 8.0,
     'gmlp_v_norm_3': 33.467,
     'gmlp_b_s_3': 5.336}
    for name, (base, spread) in spreads.items():
        noise = np.random.default_rng([zlib.crc32(name.encode()), seed]).standard_normal(out[name].shape)
        drawn = base * np.exp(spread * noise) if base else spread * noise
        out[name] = __import__('jax').numpy.asarray(drawn.astype(out[name].dtype))
    for name, factor in factors.items():
        out[name] = (out[name] * factor).astype(out[name].dtype)
    return out
```

```python
import math
from contextlib import ExitStack

import numpy as np
import concourse.bass as bass
from concourse import mybir

F32 = mybir.dt.float32
ALU = mybir.AluOpType
ACT = mybir.ActivationFunctionType
AX = mybir.AxisListType

P = 128
T = 256
C = 1024
KB = C // P
UNITS = 6
UNIT = 2048
BANKS = 4
FF = 2816
FFI = FF // 256
EPS = 1e-6


def plan():
    ffn = ("ffn", 2 * FFI, FFI)
    stages = [("b1_xlru", 4, 0), ("b1_q", 4, 0), ("b1_k", 4, 0), ("b1_v", 4, 0), ("b1_gret", 4, 0),
              ("b1_glru", 4, 0), ("b1_out", 0, 8),
              ("b2_q", 2, 0), ("b2_k", 2, 0), ("b2_v", 2, 0), ("b2_cb", 1, 0), ("b2_cc", 1, 0),
              ("b2_cx", 1, 0), ("b2_pin", 1, 0), ("b2_out", 0, 4), ("b2_ffn",) + ffn[1:],
              ("mem_k", 4, 0), ("mem_v", 4, 0), ("l0_ffn1",) + ffn[1:],
              ("rw_r", 4, 0), ("rw_k", 4, 0), ("rw_v", 4, 0), ("rw_out", 0, 4),
              ("l0_xq", 4, 0), ("l0_xo", 0, 4), ("l0_ffn2",) + ffn[1:],
              ("l1_ffn1",) + ffn[1:], ("gm_v", 8, 0), ("gm_u", 8, 0), ("gm_out", 0, 8),
              ("l1_xq", 4, 0), ("l1_xo", 0, 4), ("l1_ffn2",) + ffn[1:]]
    unit, bank, out = 0, 0, {}
    for name, np_, nd in stages:
        out[name] = (unit, bank)
        unit, bank = unit + np_ + nd, bank + np_
    out["end"] = (unit, bank)
    return out


PLAN = plan()
N_UNITS = -(-PLAN["end"][0] // UNITS) * UNITS


PARAMS = [("norm_in_g", 8), ("conv_w", 32), ("conv_b", 8), ("gate_a_b", 8), ("gate_x_b", 8),
          ("lru_lambda", 8), ("norm_out_g", 8),
          ("conv_w_2", 6), ("pool_scale_2", 2), ("ln1_g_2", 8), ("ln1_b_2", 8), ("ffn_conv_w_2", 132),
          ("ffn_conv_b_2", 44), ("ln2_g_2", 8), ("ln2_b_2", 8),
          ("mem_norm_3", 8), ("ffn1_norm_3", 16), ("mix_norm_3", 16), ("xattn_norm_3", 16),
          ("ffn2_norm_3", 16), ("rwkv_mu_3", 48), ("rwkv_w0_3", 8), ("rwkv_a0_3", 8), ("rwkv_k_k_3", 8),
          ("rwkv_k_a_3", 8), ("rwkv_r_k_3", 8), ("rwkv_ln_w_3", 8), ("rwkv_ln_b_3", 8),
          ("gmlp_v_norm_3", 16), ("final_norm_3", 8)]
PCOL, _n = {}, 0
for _name, _w in PARAMS:
    PCOL[_name] = _n
    _n += _w
N_PARAMS = _n


def constants():
    f = np.float32
    i = np.arange(P)
    out = {}
    out["ident"] = np.eye(P, dtype=f)
    out["mean_c"] = np.full((P, P), 1.0 / C, f)
    out["mean_p"] = np.full((P, P), 1.0 / P, f)
    half = (i[:, None] // 64 == i[None, :] // 64)
    out["sum_h"] = half.astype(f)
    out["mean_h"] = (half / 64.0).astype(f)
    rot = np.zeros((P, P), f)
    for d in range(64):
        rot[d + 64, d] = -1.0
        rot[d, d + 64] = 1.0
    out["rot"] = rot
    inv = (f(10000.0) ** (-np.arange(0, P, 2, dtype=f) / f(P))).astype(f)
    ang = np.arange(T, dtype=f)[None, :] * inv[:, None]
    ang = np.concatenate([ang, ang], 0)
    out["cos"] = np.tile(np.cos(ang).astype(f), (1, 2))
    out["sin"] = np.tile(np.sin(ang).astype(f), (1, 2))
    logg = np.log1p(-np.exp2(-5.0 - np.arange(8)))
    rel = np.arange(T)[None, :] - i[:, None]
    dec = np.where(rel[None] >= 0, np.exp(np.maximum(rel, 0)[None] * logg[:, None, None]), 0.0) * P ** -0.5
    dec = np.concatenate([dec, dec[:, :, :P]], 2)
    out["decay"] = dec.transpose(1, 0, 2).reshape(P, -1).astype(f)
    pos = np.arange(1, T + 1)
    win = np.repeat(np.array([2, 4, 8, 16]), 64).reshape(2, P)
    out["pool_inv"] = (1.0 / np.minimum(pos, win[:, :, None])).transpose(1, 0, 2).reshape(P, -1).astype(f)
    n = np.maximum(255 - np.arange(384), 0)
    nf = np.maximum(n, 1).astype(f)
    large = 16 + (np.log(nf / f(16)) / f(math.log(64.0)) * f(16)).astype(np.int32)
    bucket = np.where(n < 16, n, np.minimum(large, 31))
    hot = np.zeros((P, 384), f)
    hot[bucket[:256], np.arange(256)] = 1.0
    out["bucket_hot"] = hot
    out["future"] = np.tile(np.where(np.arange(384) > 255, f(-1e30), f(0)).astype(f), (P, 1))
    s_, t_ = i[:, None], i[None, :]
    same = s_ // CHUNK == t_ // CHUNK
    out["before"] = (same & (s_ < t_)).astype(f)
    out["upto"] = (same & (s_ <= t_)).astype(f)
    for m in LEVELS:
        out[f"level{m}"] = ((s_ // (2 * m) == t_ // (2 * m)) & (s_ % (2 * m) < m) & (t_ % (2 * m) >= m)).astype(f)
    reset = np.ones((P, T), f)
    reset[:, ::CHUNK] = 0.0
    out["reset"] = reset
    out["causal"] = (s_ <= t_).astype(f)
    return out


CHUNK = 64
LEVELS = (1, 2, 4, 8, 16, 32)
CONSTS = constants()
DECAY = CONSTS.pop("decay")
COMMON = ("ident", "mean_c")
EARLY = ("mean_p", "rot", "cos", "sin", "pool_inv", "bucket_hot", "future")
LATE = tuple(n for n in CONSTS if n not in COMMON + EARLY)
CCOL, N_COMMON = {}, 0
for _name in COMMON:
    CCOL[_name] = (N_COMMON, N_COMMON + CONSTS[_name].shape[1])
    N_COMMON += CONSTS[_name].shape[1]
N_CONSTS = 0
for _set in (EARLY, LATE):
    _n = N_COMMON
    for _name in _set:
        CCOL[_name] = (_n, _n + CONSTS[_name].shape[1])
        _n += CONSTS[_name].shape[1]
    N_CONSTS = max(N_CONSTS, _n)
N_LATE = _n - N_COMMON


class Sems(dict):

    def __init__(self, nc, ctx):
        self.nc, self.ctx = nc, ctx

    def __missing__(self, name):
        self[name] = self.ctx.enter_context(self.nc.semaphore(name))
        return self[name]


class Chain:

    def __init__(self, eng, sem):
        self.eng, self.sem, self.n = eng, sem, 0

    def step(self, ins):
        self.n += 1
        ins.then_inc(self.sem, 1)
        self.eng.wait_ge(self.sem, self.n)


class Ctx:

    def __init__(self, nc, ctx, io):
        self.nc, self.io = nc, io
        self.S = Sems(nc, ctx)

        def sb(name, shape):
            return ctx.enter_context(nc.sbuf_tensor("sb_" + name, shape, F32))

        self.ring = sb("ring", [P, UNITS, UNIT])
        self.par = sb("par", [P, N_PARAMS])
        self.con = sb("con", [P, N_CONSTS])
        self.h = sb("h", [P, KB, T])
        self.xn = sb("xn", [P, KB, T])
        self.sq = sb("sq", [P, KB, T])
        self.rstd = sb("rstd", [P, 512])
        self.std = sb("std", [P, 512])
        self.eps = sb("eps", [P, 4])
        self.th = sb("th", [P, 2, 512])
        self.t1 = sb("t1", [P, 2, 512])
        self.hid = sb("hid", [P, 2, 512])
        self.work = [sb(f"work{i}", [P, KB, T]) for i in range(NWORK)]
        self.small = sb("small", [P, 256])
        self.gates = self.work[9][:, :, :].rearrange("p a b -> p (a b)")\
            .rearrange("p (g n o) -> p g n o", g=2, n=8)
        self.pad = sb("pad", [P, KB, T + 4])
        self.relb = sb("relb", [P, 8])
        self.relg = sb("relg", [8, 384])
        self.table = sb("table", [P, 8, 384])
        self.wpool = sb("wpool", [P, 2, P])
        self.ps = ctx.enter_context(nc.psum_tensor("ps", [P, 8, 512], F32))

    def p(self, name, j=0, n=1):
        return self.par[:, PCOL[name] + j:PCOL[name] + j + n]

    def c(self, name):
        a, b = CCOL[name]
        return self.con[:, a:b]

    def wait_loaded(self, eng, n, j=None):
        v = 16 * (n // UNITS + 1)
        eng.wait_ge(self.S[f"unit_loaded{n % UNITS}"], v if j is None else j * 16 + v)

    def wait_done(self, eng, n, j=None):
        v = n // UNITS + 1
        eng.wait_ge(self.S[f"unit_done{n % UNITS}"], v if j is None else j + v)

    def wait_read(self, eng, q, j=None):
        v = q // BANKS + 1
        eng.wait_ge(self.S[f"bank_read{q % BANKS}"], v if j is None else j + v)

    def bank(self, q):
        return self.ps[:, q % BANKS, :]

    def read(self, ins, q):
        ins.then_inc(self.S[f"bank_read{q % BANKS}"], 1)


NWORK = 10


def p_unit(c, pe, n, q, x, j=None, token_major=False):
    c.wait_loaded(pe, n, j)
    if q >= BANKS:
        c.wait_read(pe, q - BANKS, j)
    w = c.ring[:, n % UNITS, :].rearrange("p (k n) -> p k n", k=KB)
    out = c.bank(q).rearrange("p (m t) -> p m t", m=2)
    for m in range(2):
        for k in range(KB):
            if token_major:
                mm = c.nc.tensor.matmul(out[:, m, :], x[:, k, m * P:m * P + P], w[:, k, :],
                                        start=k == 0, stop=k == KB - 1)
            else:
                mm = c.nc.tensor.matmul(out[:, m, :], w[:, k, m * P:m * P + P], x[:, k, :],
                                        start=k == 0, stop=k == KB - 1)
    mm.then_inc(c.S[f"unit_done{n % UNITS}"], 1)


def d_unit(c, pe, n, x2, first, last, j=None):
    c.wait_loaded(pe, n, j)
    w = c.ring[:, n % UNITS, :].rearrange("p (k n) -> p k n", k=2)
    for m in range(KB):
        for k in range(2):
            mm = c.nc.tensor.matmul(c.ps[:, 4 + m // 2, (m % 2) * T:(m % 2) * T + T],
                                    w[:, k, m * P:m * P + P], x2(k),
                                    start=first and k == 0 and m % 2 == 0, stop=last and k == 1,
                                    skip_group_check=True)
    mm.then_inc(c.S[f"unit_done{n % UNITS}"], 1)


def rms_scalar(c, act, k, src=None, ready=None):
    src = c.h if src is None else src
    act.wait_ge(c.S["h_ready"], k + 1) if ready is None else act.wait_ge(*ready)
    c.nc.scalar.activation(c.sq[:, :, :], src[:, :, :], ACT.Square).then_inc(c.S["sq_ready"], 1)
    act.wait_ge(c.S["mean_sq_ready"], k + 1)
    c.nc.scalar.activation(c.std[:, 0:T], c.ps[:, 4, 0:T], ACT.Sqrt, bias=c.eps[:, 0:1])\
        .then_inc(c.S["std_ready"], 1)


def rms_tensor(c, pe, k):
    pe.wait_ge(c.S["sq_ready"], k + 1)
    for b in range(KB):
        mm = c.nc.tensor.matmul(c.ps[:, 4, 0:T], c.c("mean_c"), c.sq[:, b, :], start=b == 0, stop=b == KB - 1)
    mm.then_inc(c.S["mean_sq_ready"], 1)


def rms_vector(c, dve, k, gain, out, src=None):
    src = c.h if src is None else src
    dve.wait_ge(c.S["std_ready"], k + 1)
    c.nc.vector.reciprocal(c.rstd[:, 0:T], c.std[:, 0:T]).then_inc(c.S["rstd_ready"], 1)
    dve.wait_ge(c.S["rstd_ready"], k + 1)
    for b in range(KB):
        c.nc.vector.scalar_tensor_tensor(out=out[:, b, :], in0=src[:, b, :], scalar=c.p(*gain(b)),
                                         in1=c.rstd[:, 0:T], op0=ALU.mult, op1=ALU.mult)\
            .then_inc(c.S["xn_ready"], 1)


def add_residual(c, dve, n, scale, ch, a=None):
    c.wait_done(dve, n)
    for b in range(4):
        ins = c.nc.vector.scalar_tensor_tensor(
            out=c.h[:, 2 * b:2 * b + 2, :], in0=c.ps[:, 4 + b, :].rearrange("p (m t) -> p m t", m=2),
            scalar=scale, in1=c.h[:, 2 * b:2 * b + 2, :], op0=ALU.mult, op1=ALU.add)
        if b < 3:
            ins.then_inc(ch.sem, 1)
            ch.n += 1
    dve.wait_ge(ch.sem, ch.n)
    ins.then_inc(c.S["h_ready"], 1)


def gu_unit(n0, i):
    if i < 2:
        return n0 + 2 * i
    return n0 + 5 + 6 * ((i - 2) // 2) + 3 * (i % 2)


def d_unit_of(n0, i):
    if i == 0:
        return n0 + 4
    if i == FFI - 1:
        return n0 + 3 * FFI - 1
    return n0 + 7 + 6 * ((i - 1) // 2) + 3 * ((i - 1) % 2)


def ffn_tensor(c, pe, name, x):
    n0, q0 = PLAN[name]

    def gu(i, j=None):
        n = gu_unit(n0, i)
        p_unit(c, pe, n, q0 + 2 * i, x, j)
        p_unit(c, pe, n + 1, q0 + 2 * i + 1, x, j)

    def d(i, j=None):
        c.wait_read(pe, q0 + 2 * i + 1, j)
        x = c.hid[:, i % 2, :].rearrange("p (m t) -> p m t", m=2)
        d_unit(c, pe, d_unit_of(n0, i), lambda k: x[:, k, :], i == 0, i == FFI - 1, j)

    gu(0)
    gu(1)
    d(0)
    with pe.Fori(0, (FFI - 3) // 2) as j:
        gu(2, j)
        d(1, j)
        gu(3, j)
        d(2, j)
    gu(FFI - 1)
    d(FFI - 2)
    d(FFI - 1)


def ffn_loop(eng, body):
    body(0, None)
    body(1, None)
    with eng.Fori(0, (FFI - 3) // 2) as j:
        body(2, j)
        body(3, j)
    body(FFI - 1, None)


def swiglu_scalar(c, act, name, f):
    n0, q0 = PLAN[name]

    def body(i, j):
        c.wait_done(act, gu_unit(n0, i), j)
        if i >= 2:
            c.wait_read(act, q0 + 2 * (i - 2) + 1, j)
        c.nc.scalar.activation(c.th[:, i % 2, :], c.bank(q0 + 2 * i), ACT.Tanh, scale=0.5)\
            .then_inc(c.S[f"tanh_ready{i % 2}"], 1)
    ffn_loop(act, body)


def tanh_count(f, i):
    return f * ((FFI + 1) // 2 if i % 2 == 0 else FFI // 2) + i // 2 + 1


def swiglu_vector(c, dve, name, f):
    n0, q0 = PLAN[name]

    def body(i, j):
        v = tanh_count(f, i)
        dve.wait_ge(c.S[f"tanh_ready{i % 2}"], v if j is None else j + v)
        c.read(c.nc.vector.scalar_tensor_tensor(
            out=c.t1[:, i % 2, :], in0=c.th[:, i % 2, :], scalar=1.0, in1=c.bank(q0 + 2 * i),
            op0=ALU.add, op1=ALU.mult), q0 + 2 * i)
        c.wait_done(dve, gu_unit(n0, i) + 1, j)
        if i >= 2:
            c.wait_done(dve, d_unit_of(n0, i - 2), j)
        c.wait_read(dve, q0 + 2 * i, j)
        c.read(c.nc.vector.scalar_tensor_tensor(
            out=c.hid[:, i % 2, :], in0=c.t1[:, i % 2, :], scalar=0.5, in1=c.bank(q0 + 2 * i + 1),
            op0=ALU.mult, op1=ALU.mult), q0 + 2 * i + 1)
    ffn_loop(dve, body)


NORMS = ["b1_in", "b1_out", "mem", "l0_ffn1", "l0_mix", "l0_x", "l0_ffn2",
         "l1_ffn1", "l1_mix", "l1_x", "l1_ffn2", "final"]
NK = {name: i for i, name in enumerate(NORMS)}
RESID = ["b1_out", "l0_ffn1", "rw_out", "l0_xo", "l0_ffn2",
         "l1_ffn1", "gm_out", "l1_xo", "l1_ffn2"]
HR = {name: i + 1 for i, name in enumerate(RESID)}


def b1_scalar(c, act):
    S, nc, W = c.S, c.nc, c.work
    rms_scalar(c, act, NK["b1_in"], ready=(S["x_loaded"], 16))
    n0, q0 = PLAN["b1_xlru"]
    act.wait_ge(S["b1_pad"], 1)
    for u in range(4):
        c.wait_done(act, n0 + u)
        c.read(nc.scalar.activation(c.pad[:, 2 * u:2 * u + 2, 3:3 + T],
                                    c.bank(q0 + u).rearrange("p (m t) -> p m t", m=2), ACT.Copy), q0 + u)
    act.wait_ge(S["b1_abs"], 1)
    nc.scalar.activation(c.small[:, 8:16], c.small[:, 0:8], ACT.Exp, scale=-1.0).then_inc(S["b1_exp"], 1)
    n0, q0 = PLAN["b1_q"]
    for u in range(8):
        c.wait_done(act, n0 + u)
        if u >= 2:
            act.wait_ge(S["b1_rotated"], u - 1)
        c.read(nc.scalar.activation(c.hid[:, u % 2, :], c.bank(q0 + u), ACT.Copy), q0 + u)
    n0, q0 = PLAN["b1_v"]
    v = W[2][:, :, :].rearrange("p a b -> p (a b)").rearrange("p (m n) -> p m n", m=2)
    for u in range(4):
        c.wait_done(act, n0 + u)
        c.read(nc.scalar.activation(v[:, :, u * 256:u * 256 + 256],
                                    c.bank(q0 + u).rearrange("p (m n) -> p m n", m=2), ACT.Copy), q0 + u)
    for n in range(8):
        tmp = c.sq if n % 2 == 0 else W[8]
        act.wait_ge(S["b1_gate_mm"], n + 1)
        if n >= 2:
            act.wait_ge(S["b1_gate_used"], n - 1)
        bank = c.ps[:, 6 + n % 2, :]
        nc.scalar.activation(tmp[:, 0, :], bank[:, 0:T], ACT.Tanh, scale=0.5,
                             bias=c.small[:, 64 + n:65 + n]).then_inc(S["b1_gate_r"], 1)
        nc.scalar.activation(tmp[:, 1, :], bank[:, T:2 * T], ACT.Tanh, scale=0.5,
                             bias=c.small[:, 72 + n:73 + n]).then_inc(S["b1_gate_i"], 1)
        act.wait_ge(S["b1_gate_r"], n + 1)
        for s, (col, f) in enumerate(((80, ACT.Exp), (88, ACT.Tanh), (80, ACT.Tanh), (96, ACT.Exp))):
            nc.scalar.activation(tmp[:, 2 + s, :], tmp[:, 0, :], f, scale=c.small[:, col + n:col + n + 1],
                                 bias=c.small[:, col + n:col + n + 1]).then_inc(S["b1_gate_ready"], 1)
    ng, qg = PLAN["b1_gret"]

    def gate(u):
        c.wait_done(act, ng + u)
        if u >= 2:
            c.wait_read(act, qg + u - 2)
        nc.scalar.activation(c.th[:, u % 2, :], c.bank(qg + u), ACT.Tanh, scale=0.5)\
            .then_inc(S["b1_gate_tanh"], 1)

    for p in range(5):
        if p < 4:
            gate(2 * p)
        if p > 0:
            act.wait_ge(S["b1_var"], p)
            nc.scalar.activation(W[9][:, 2 * p - 2:2 * p, :],
                                 c.ps[:, 6, :].rearrange("p (m t) -> p m t", m=2), ACT.Copy)\
                .then_inc(S["b1_var_read"], 1)
        if p < 4:
            gate(2 * p + 1)
            act.wait_ge(S["b1_o"], p + 1)
            nc.scalar.activation(c.t1[:, 0, :], c.ps[:, 6, :], ACT.Copy).then_inc(S["b1_o_read"], 1)
            act.wait_ge(S["b1_cen"], p + 1)
            nc.scalar.activation(c.t1[:, 1, :], W[0][:, 2 * p:2 * p + 2, :].rearrange("p a b -> p (a b)"),
                                 ACT.Square).then_inc(S["b1_cen_sq"], 1)
    act.wait_ge(S["b1_var_read"], 4)
    nc.scalar.activation(W[9][:, :, :], W[9][:, :, :], ACT.Sqrt, bias=c.eps[:, 0:1]).then_inc(S["b1_std"], 1)
    act.wait_ge(S["b1_m_ready"], 8)
    nc.scalar.activation(W[7][:, :, :], W[7][:, :, :], ACT.Sqrt).then_inc(S["b1_mult"], 1)
    rms_scalar(c, act, NK["b1_out"], ready=(S["h_ready"], HR["b1_out"]))


def b1_tensor(c, pe):
    S, nc, W = c.S, c.nc, c.work
    pe.wait_ge(S["con_loaded"], 16)
    rms_tensor(c, pe, NK["b1_in"])
    pe.wait_ge(S["xn_ready"], 8)
    for u in range(4):
        n0, q0 = PLAN["b1_xlru"]
        p_unit(c, pe, n0 + u, q0 + u, c.xn)
    n0, q0 = PLAN["b1_q"]

    def rotate(u):
        c.wait_read(pe, q0 + u)
        if u >= 2:
            pe.wait_ge(S["b1_rot_read"], u - 1)
        nc.tensor.matmul(c.ps[:, 4 + u % 2, :], c.c("rot"), c.hid[:, u % 2, :], start=True, stop=True)\
            .then_inc(S["b1_rot_mm"], 1)

    for u in range(8):
        p_unit(c, pe, n0 + u, q0 + u, c.xn)
        if u > 0:
            rotate(u - 1)
    n0, q1 = PLAN["b1_v"]
    p_unit(c, pe, n0, q1, c.xn, token_major=True)
    rotate(7)
    for u in range(1, 4):
        p_unit(c, pe, n0 + u, q1 + u, c.xn, token_major=True)
    pe.wait_ge(S["gates_loaded"], 16)
    for n in range(8):
        pe.wait_ge(S["b1_conv"], n + 1)
        if n >= 2:
            pe.wait_ge(S["b1_gate_i"], n - 1)
        for g in range(2):
            mm = nc.tensor.matmul(c.ps[:, 6 + n % 2, g * T:g * T + T], c.gates[:, g, n, :], W[5][:, n, :],
                                  start=True, stop=True)
        mm.then_inc(S["b1_gate_mm"], 1)
    ng, qg = PLAN["b1_gret"]
    v = W[2][:, :, :].rearrange("p a b -> p (a b)").rearrange("p (m n) -> p m n", m=2)
    prob = c.hid[:, :, :].rearrange("p a b -> p (a b)").rearrange("p (a b) -> p a b", a=2)
    pe.wait_ge(S["b1_rotated"], 8)
    pe.wait_ge(S["b1_gate_i"], 8)
    for p in range(5):
        if p < 4:
            if p > 0:
                pe.wait_ge(S["b1_prob"], 2 * p)
            for e in range(2):
                hd = 2 * p + e
                nc.tensor.matmul(c.ps[:, 4 + e, 0:T], W[1][:, hd, 0:P], W[0][:, hd, :], start=True, stop=True)
                nc.tensor.matmul(c.ps[:, 4 + e, T:T + P], W[1][:, hd, P:T], W[0][:, hd, P:T],
                                 start=True, stop=True).then_inc(S["b1_scores"], 1)
            p_unit(c, pe, ng + 2 * p, qg + 2 * p, c.xn)
        if p > 0:
            pe.wait_ge(S["b1_cen_sq"], p)
            nc.tensor.matmul(c.ps[:, 6, :], c.c("mean_p"), c.t1[:, 1, :], start=True, stop=True)\
                .then_inc(S["b1_var"], 1)
        if p < 4:
            p_unit(c, pe, ng + 2 * p + 1, qg + 2 * p + 1, c.xn)
            if p == 0:
                c.wait_read(pe, q1 + 3)
                c.wait_read(pe, q1 + 2)
            else:
                pe.wait_ge(S["b1_var_read"], p)
            for e in range(2):
                hd = 2 * p + e
                pe.wait_ge(S["b1_prob"], hd + 1)
                nc.tensor.matmul(c.ps[:, 6, e * T:e * T + T], v[:, 0, hd * P:hd * P + P],
                                 prob[:, e, 0:T], start=True, stop=False, skip_group_check=True)
                mm = nc.tensor.matmul(c.ps[:, 6, e * T + P:e * T + T], v[:, 1, hd * P:hd * P + P],
                                      prob[:, e, T:T + P], start=False, stop=True, skip_group_check=True)
            mm.then_inc(S["b1_o"], 1)
            pe.wait_ge(S["b1_o_read"], p + 1)
            if p > 0:
                pe.wait_ge(S["b1_cen"], p)
            nc.tensor.matmul(c.ps[:, 7, :], c.c("mean_p"), c.t1[:, 0, :], start=True, stop=True)\
                .then_inc(S["b1_mean"], 1)
    n0, _ = PLAN["b1_out"]
    pe.wait_ge(S["b1_cen"], 4)
    pe.wait_ge(S["b1_var_read"], 4)
    for u in range(8):
        pe.wait_ge(S["b1_y"], u + 1)
        src = W[0] if u < 4 else W[7]
        d_unit(c, pe, n0 + u, lambda k: src[:, 2 * (u % 4) + k, :], u == 0, u == 7)
    rms_tensor(c, pe, NK["b1_out"])


def b1_vector(c, dve, ch):
    S, nc, W = c.S, c.nc, c.work
    v = nc.vector
    for i, e in enumerate((EPS, 1e-5, 64e-5)):
        ch.step(v.memset(c.eps[:, i:i + 1], e))
    v.memset(c.pad[:, :, 0:4], 0.0).then_inc(S["b1_pad"], 1)
    dve.wait_ge(S["par_loaded"], 16)
    dve.wait_ge(S["x_loaded"], 16)
    rms_vector(c, dve, NK["b1_in"], lambda b: ("norm_in_g", b), c.xn)
    s = c.small
    ch.step(v.tensor_scalar(s[:, 16:24], c.p("lru_lambda", 0, 8), -1.0, None, ALU.mult))
    v.tensor_tensor(s[:, 0:8], s[:, 16:24], c.p("lru_lambda", 0, 8), ALU.max).then_inc(S["b1_abs"], 1)
    ch.step(v.tensor_scalar(s[:, 16:24], s[:, 16:24], 0.0, None, ALU.max))
    dve.wait_ge(S["b1_exp"], 1)
    ch.step(v.tensor_scalar(s[:, 24:32], s[:, 8:16], 2.0, None, ALU.add))
    ch.step(v.reciprocal(s[:, 24:32], s[:, 24:32]))
    ch.step(v.tensor_tensor(s[:, 24:32], s[:, 24:32], s[:, 8:16], ALU.mult))
    ch.step(v.tensor_tensor(s[:, 32:40], s[:, 24:32], s[:, 24:32], ALU.mult))
    ch.step(v.tensor_scalar(s[:, 40:48], s[:, 32:40], 1 / 17, 1 / 15, ALU.mult, ALU.add))
    for d in (13, 11, 9, 7, 5, 3, 1):
        ch.step(v.tensor_tensor(s[:, 40:48], s[:, 40:48], s[:, 32:40], ALU.mult))
        ch.step(v.tensor_scalar(s[:, 40:48], s[:, 40:48], 1 / d, None, ALU.add))
    ch.step(v.tensor_tensor(s[:, 40:48], s[:, 40:48], s[:, 24:32], ALU.mult))
    ch.step(v.scalar_tensor_tensor(out=s[:, 40:48], in0=s[:, 40:48], scalar=2.0, in1=s[:, 16:24],
                                   op0=ALU.mult, op1=ALU.add))
    ch.step(v.tensor_scalar(s[:, 80:88], s[:, 40:48], -4.0, None, ALU.mult))
    ch.step(v.tensor_scalar(s[:, 88:96], s[:, 40:48], -2.0, None, ALU.mult))
    ch.step(v.tensor_scalar(s[:, 96:104], s[:, 40:48], -8.0, None, ALU.mult))
    ch.step(v.tensor_scalar(s[:, 64:72], c.p("gate_a_b", 0, 8), 0.5, None, ALU.mult))
    ch.step(v.tensor_scalar(s[:, 72:80], c.p("gate_x_b", 0, 8), 0.5, None, ALU.mult))
    dve.wait_ge(S["con_loaded"], 16)

    def conv(b):
        _, q0 = PLAN["b1_xlru"]
        c.wait_read(dve, q0 + b // 2)
        ch.step(v.tensor_scalar(W[5][:, b, :], c.pad[:, b, 0:T], c.p("conv_w", b), c.p("conv_b", b),
                                ALU.mult, ALU.add))
        for tap in range(1, 4):
            ins = v.scalar_tensor_tensor(out=W[5][:, b, :], in0=c.pad[:, b, tap:tap + T],
                                         scalar=c.p("conv_w", 8 * tap + b), in1=W[5][:, b, :],
                                         op0=ALU.mult, op1=ALU.add)
            if tap < 3:
                ch.step(ins)
        ins.then_inc(S["b1_conv"], 1)

    def rotate(u):
        _, q0 = PLAN["b1_q"]
        dst = W[u // 4][:, 2 * (u % 4):2 * (u % 4) + 2, :].rearrange("p a b -> p (a b)")
        c.wait_read(dve, q0 + u)
        ch.step(v.tensor_tensor(dst, c.hid[:, u % 2, :], c.c("cos"), ALU.mult))
        dve.wait_ge(S["b1_rot_mm"], u + 1)
        v.tensor_tensor(c.t1[:, u % 2, :], c.ps[:, 4 + u % 2, :], c.c("sin"), ALU.mult)\
            .then_inc(S["b1_rot_read"], 1)
        dve.wait_ge(S["b1_rot_read"], u + 1)
        v.tensor_tensor(dst, dst, c.t1[:, u % 2, :], ALU.add).then_inc(S["b1_rotated"], 1)

    for b in range(8):
        conv(b)
    for u in range(8):
        rotate(u)
    for n in range(8):
        tmp = c.sq if n % 2 == 0 else W[8]
        e1, th, tf, e2 = (tmp[:, 2 + k, :] for k in range(4))
        dve.wait_ge(S["b1_gate_i"], n + 1)
        v.scalar_tensor_tensor(out=W[5][:, n, :], in0=tmp[:, 1, :], scalar=1.0, in1=W[5][:, n, :],
                               op0=ALU.add, op1=ALU.mult).then_inc(S["b1_ix"], 1)
        dve.wait_ge(S["b1_gate_ready"], 4 * n + 4)
        ch.step(v.scalar_tensor_tensor(out=W[6][:, n, :], in0=e1, scalar=1.0, in1=th,
                                       op0=ALU.add, op1=ALU.mult))
        ch.step(v.tensor_scalar(W[6][:, n, :], W[6][:, n, :], 1.0, None, ALU.add))
        v.scalar_tensor_tensor(out=W[7][:, n, :], in0=e2, scalar=1.0, in1=tf,
                               op0=ALU.add, op1=ALU.mult).then_inc(S["b1_gate_used"], 1)
        dve.wait_ge(S["b1_gate_used"], n + 1)
        v.tensor_scalar(W[7][:, n, :], W[7][:, n, :], -1.0, 0.0, ALU.mult, ALU.max)\
            .then_inc(S["b1_m_ready"], 1)
    prob = c.hid[:, :, :].rearrange("p a b -> p (a b)").rearrange("p (a b) -> p a b", a=2)
    dec = c.table
    dve.wait_ge(S["decay_loaded"], 16)
    _, qg = PLAN["b1_gret"]

    def gate(u):
        dst = W[3 + u // 4][:, 2 * (u % 4):2 * (u % 4) + 2, :].rearrange("p a b -> p (a b)")
        dve.wait_ge(S["b1_gate_tanh"], u + 1)
        c.read(v.scalar_tensor_tensor(out=dst, in0=c.th[:, u % 2, :], scalar=1.0, in1=c.bank(qg + u),
                                      op0=ALU.add, op1=ALU.mult), qg + u)

    for p in range(4):
        for e in range(2):
            hd = 2 * p + e
            dve.wait_ge(S["b1_scores"], hd + 1)
            if p > 0:
                dve.wait_ge(S["b1_o"], p)
            v.tensor_tensor(prob[:, e, 0:T + P], c.ps[:, 4 + e, 0:T + P], dec[:, hd, :], ALU.mult)\
                .then_inc(S["b1_prob"], 1)
        gate(2 * p)
        gate(2 * p + 1)
        dve.wait_ge(S["b1_mean"], p + 1)
        v.tensor_tensor(W[0][:, 2 * p:2 * p + 2, :].rearrange("p a b -> p (a b)"), c.t1[:, 0, :],
                        c.ps[:, 7, :], ALU.subtract).then_inc(S["b1_cen"], 1)
    dve.wait_ge(S["b1_std"], 1)
    ch.step(v.reciprocal(W[9][:, :, :], W[9][:, :, :]))
    dve.wait_ge(S["b1_cen_sq"], 4)
    for u in range(4):
        sl = (slice(None), slice(2 * u, 2 * u + 2), slice(None))
        ch.step(v.scalar_tensor_tensor(out=W[0][sl], in0=W[0][sl], scalar=0.5, in1=W[9][sl],
                                       op0=ALU.mult, op1=ALU.mult))
        if u == 0:
            for k in range(4):
                c.wait_read(dve, qg + k)
        v.tensor_tensor(W[0][sl], W[0][sl], W[3][sl], ALU.mult).then_inc(S["b1_y"], 1)
    dve.wait_ge(S["b1_mult"], 1)
    dve.wait_ge(S["b1_ix"], 8)
    for k in range(4):
        c.wait_read(dve, qg + 4 + k)
    for n in range(8):
        ch.step(v.scalar_tensor_tensor(out=W[7][:, n, :], in0=W[7][:, n, :], scalar=0.5, in1=W[5][:, n, :],
                                       op0=ALU.mult, op1=ALU.mult))
        ch.step(v.tensor_tensor_scan(W[5][:, n, :], W[6][:, n, :], W[7][:, n, :], 0.0, ALU.mult, ALU.add))
        ins = v.scalar_tensor_tensor(out=W[7][:, n, :], in0=W[5][:, n, :], scalar=0.5, in1=W[4][:, n, :],
                                     op0=ALU.mult, op1=ALU.mult)
        if n % 2 == 0:
            ch.step(ins)
        else:
            ins.then_inc(S["b1_y"], 1)
    add_residual(c, dve, PLAN["b1_out"][0] + 7, 1.0, ch)
    dve.wait_ge(S["h_ready"], HR["b1_out"])
    rms_vector(c, dve, NK["b1_out"], lambda b: ("norm_out_g", b), c.h)


ALPHA = 2.0 ** 0.25


def at(v, step, j):
    return v if j is None else j * step + v


def ln_tensor(c, pe, k):
    S, mm = c.S, c.nc.tensor.matmul
    pe.wait_ge(S["ln_x"], k + 1)
    for b in range(KB):
        ins = mm(c.ps[:, 4, 0:T], c.c("mean_c"), c.h[:, b, :], start=b == 0, stop=b == KB - 1)
    ins.then_inc(S["ln_mean"], 1)
    pe.wait_ge(S["ln_sq"], k + 1)
    for b in range(KB):
        ins = mm(c.ps[:, 5, 0:T], c.c("mean_c"), c.sq[:, b, :], start=b == 0, stop=b == KB - 1)
    ins.then_inc(S["ln_var"], 1)


def ln_scalar(c, act, k):
    S = c.S
    act.wait_ge(S["ln_centred"], 8 * k + 8)
    c.nc.scalar.activation(c.sq[:, :, :], c.h[:, :, :], ACT.Square).then_inc(S["ln_sq"], 1)
    act.wait_ge(S["ln_var"], k + 1)
    c.nc.scalar.activation(c.std[:, 0:T], c.ps[:, 5, 0:T], ACT.Sqrt, bias=c.eps[:, 1:2])\
        .then_inc(S["ln_std"], 1)


def ln_vector(c, dve, k, n, gain, bias, ch):
    S, v = c.S, c.nc.vector
    c.wait_done(dve, n)
    for b in range(4):
        ins = v.scalar_tensor_tensor(
            out=c.h[:, 2 * b:2 * b + 2, :], in0=c.h[:, 2 * b:2 * b + 2, :], scalar=ALPHA,
            in1=c.ps[:, 4 + b, :].rearrange("p (m t) -> p m t", m=2), op0=ALU.mult, op1=ALU.add)
        if b < 3:
            ins.then_inc(ch.sem, 1)
            ch.n += 1
    dve.wait_ge(ch.sem, ch.n)
    ins.then_inc(S["ln_x"], 1)
    dve.wait_ge(S["ln_mean"], k + 1)
    for b in range(KB):
        v.tensor_tensor(c.h[:, b, :], c.h[:, b, :], c.ps[:, 4, 0:T], ALU.subtract)\
            .then_inc(S["ln_centred"], 1)
    dve.wait_ge(S["ln_std"], k + 1)
    ch.step(v.reciprocal(c.rstd[:, 0:T], c.std[:, 0:T]))
    for b in range(KB):
        dve.wait_ge(S["ln_sq"], k + 1)
        ch.step(v.scalar_tensor_tensor(out=c.h[:, b, :], in0=c.h[:, b, :], scalar=c.p(gain, b),
                                       in1=c.rstd[:, 0:T], op0=ALU.mult, op1=ALU.mult))
        v.tensor_scalar(c.h[:, b, :], c.h[:, b, :], c.p(bias, b), None, ALU.add).then_inc(S["ln_out"], 1)


def b2_views(c):
    W = c.work

    class V:
        q = W[0][:, 0:4, :]
        k = W[0][:, 4:8, :]
        v = W[1][:, 0:4, :].rearrange("p a b -> p (a b)").rearrange("p (m n) -> p m n", m=2)
        cb, cc, cx, pin = (W[2][:, i:i + 2, :] for i in (0, 2, 4, 6))
        mix = W[3]
        logit = [W[6][:, 2 * i:2 * i + 2, :].rearrange("p a b -> p (a b)")[:, 0:384] for i in range(4)]
        pt = [W[8][:, 2 * i:2 * i + 2, :].rearrange("p a b -> p (a b)")[:, 0:384] for i in range(2)]
        sums = [W[5][:, 2 * i:2 * i + 2, :] for i in range(4)]
        pooled = W[1][:, 4:6, :]
        conv = W[1][:, 6:8, :]
        cv = [W[4][:, 2 * i:2 * i + 2, :] for i in range(4)]
    return V


B2_UNITS = ["b2_cb", "b2_cc", "b2_cx", "b2_pin"]


def b2_tensor(c, pe):
    S, nc, V, mm = c.S, c.nc, b2_views(c), c.nc.tensor.matmul
    pe.wait_ge(S["relb_loaded"], 16)
    pe.wait_ge(S["rstd_ready"], NK["b1_out"] + 1)
    mm(c.ps[0:8, 5, 0:384], c.relb[0:32, :], c.c("bucket_hot")[0:32, :], start=True, stop=True)\
        .then_inc(S["b2_bias_mm"], 1)
    pe.wait_ge(S["xn_ready"], 8 * NK["b1_out"] + 8)
    for name in ("b2_q", "b2_k", "b2_v"):
        n0, q0 = PLAN[name]
        for u in range(2):
            p_unit(c, pe, n0 + u, q0 + u, c.h, token_major=name == "b2_v")
    _, qq = PLAN["b2_q"]
    pe.wait_ge(S["b2_bias_read"], 1)
    for s in range(11):
        if s < 8:
            b, e = s // 2, 64 * (s % 2)
            if s == 0:
                for u in range(4):
                    c.wait_read(pe, qq + u)
            if s >= 2:
                pe.wait_ge(S["b2_logit"], s - 1)
            mm(c.ps[:, 4 + s % 2, 0:P], V.q[e:e + 64, b, 0:P], V.k[e:e + 64, b, 0:P], start=True, stop=True)
            mm(c.ps[:, 4 + s % 2, P:P + T], V.q[e:e + 64, b, P:T], V.k[e:e + 64, b, :],
               start=True, stop=True).then_inc(S["b2_scores"], 1)
        if 1 <= s < 5:
            n0, q0 = PLAN[B2_UNITS[s - 1]]
            p_unit(c, pe, n0, q0, c.h)
        if 2 <= s < 10:
            hd = s - 2
            pr = V.logit[hd % 4]
            pe.wait_ge(S["b2_prob"], hd + 1)
            if hd >= 1:
                pe.wait_ge(S["b2_pt"], hd)
            for k in range(3):
                ins = nc.tensor.transpose(c.ps[:, 6, k * P:k * P + P], pr[:, k * P:k * P + P], c.c("ident"))
            ins.then_inc(S["b2_turned"], 1)
        if s >= 3:
            hd = s - 3
            e = 64 * (hd % 2)
            col = 256 * (hd // 2 % 2)
            pe.wait_ge(S["b2_pt"], hd + 1)
            if hd == 0:
                for u in range(4, 6):
                    c.wait_read(pe, qq + u)
            if hd >= 2 and hd % 2 == 0:
                pe.wait_ge(S["b2_o_read"], hd // 2)
            pt = V.pt[hd % 2]
            mm(c.ps[e:e + 64, 7, col:col + T], V.v[:, 0, 64 * hd:64 * hd + 64], pt[:, 0:T],
               start=True, stop=False, skip_group_check=True)
            mm(c.ps[e:e + 64, 7, col + P:col + T], V.v[:, 1, 64 * hd:64 * hd + 64], pt[:, T:T + P],
               start=False, stop=True, skip_group_check=True).then_inc(S["b2_o"], 1)
    pe.wait_ge(S["wpool_loaded"], 16)
    pe.wait_ge(S["b2_pooled"], 1)
    for b in range(2):
        ins = mm(c.ps[:, 5, b * T:b * T + T], c.wpool[:, b, :], V.pooled[:, b, :], start=True, stop=True)
    ins.then_inc(S["b2_pool_mm"], 1)
    n0, _ = PLAN["b2_out"]
    pe.wait_ge(S["b2_o_read"], 4)
    pe.wait_ge(S["b2_conv"], 1)
    pe.wait_ge(S["b2_pool"], 1)
    for u in range(4):
        d_unit(c, pe, n0 + u, lambda k: V.mix[:, 2 * u + k, :], u == 0, u == 3)
    ln_tensor(c, pe, 0)
    pe.wait_ge(S["ln_out"], 8)
    ffn_tensor(c, pe, "b2_ffn", c.h)
    ln_tensor(c, pe, 1)


def b2_scalar(c, act):
    S, nc, V = c.S, c.nc, b2_views(c)
    _, q0 = PLAN["b2_q"]
    n0, _ = PLAN["b2_q"]
    for u in range(6):
        c.wait_done(act, n0 + u)
        if u < 4:
            dst = (V.q if u < 2 else V.k)[:, 2 * (u % 2):2 * (u % 2) + 2, :]
            src = c.bank(q0 + u).rearrange("p (m t) -> p m t", m=2)
        else:
            dst = V.v[:, :, (u - 4) * 256:(u - 4) * 256 + 256]
            src = c.bank(q0 + u).rearrange("p (m n) -> p m n", m=2)
        c.read(nc.scalar.activation(dst, src, ACT.Copy), q0 + u)
    for s in range(11):
        if s < 8:
            act.wait_ge(S["b2_max"], s + 1)
            lg = V.logit[s % 4]
            nc.scalar.activation(lg[:, 0:P], lg[:, 0:P], ACT.Exp, bias=c.small[:, 2 * s:2 * s + 1],
                                 accum_out=c.small[:, 32 + 2 * s:33 + 2 * s]).then_inc(S["b2_exp"], 1)
            nc.scalar.activation(lg[:, P:384], lg[:, P:384], ACT.Exp, bias=c.small[:, 2 * s + 1:2 * s + 2],
                                 accum_out=c.small[:, 33 + 2 * s:34 + 2 * s]).then_inc(S["b2_exp"], 1)
        if 1 <= s < 5:
            n, q = PLAN[B2_UNITS[s - 1]]
            dst = (V.cb, V.cc, V.cx, V.pin)[s - 1]
            c.wait_done(act, n)
            c.read(nc.scalar.activation(dst, c.bank(q).rearrange("p (m t) -> p m t", m=2), ACT.Copy), q)
        if 2 <= s < 10:
            hd = s - 2
            act.wait_ge(S["b2_turned"], hd + 1)
            if hd >= 2:
                act.wait_ge(S["b2_o"], hd - 1)
            nc.scalar.activation(V.pt[hd % 2], c.ps[:, 6, 0:384], ACT.Copy).then_inc(S["b2_pt"], 1)
        if s >= 4 and s % 2 == 0:
            b = s // 2 - 2
            act.wait_ge(S["b2_o"], 2 * b + 2)
            nc.scalar.activation(V.mix[:, b, :], c.ps[:, 7, 256 * (b % 2):256 * (b % 2) + 256], ACT.Copy)\
                .then_inc(S["b2_o_read"], 1)
    ln_scalar(c, act, 0)
    n0, q0 = PLAN["b2_ffn"]

    def body(i, j):
        for g in range(2):
            q = q0 + 2 * i + g
            c.wait_done(act, gu_unit(n0, i) + g, j)
            if i >= 2 and g == 0:
                c.wait_read(act, q0 + 2 * (i - 2) + 1, j)
            for m in range(2):
                blk = 2 * i + m + (22 if g == 0 else 0)
                col = lambda name, k: c.par[:, at(PCOL[name] + k, 4, j):at(PCOL[name] + k, 4, j) + 1] \
                    if j is None else c.par[:, bass.ds(at(PCOL[name] + k, 4, j), 1)]
                nc.scalar.activation(V.cv[2 * g + i % 2][:, m, :],
                                     c.bank(q)[:, m * T:m * T + T], ACT.Identity,
                                     scale=col("ffn_conv_w_2", 88 + blk), bias=col("ffn_conv_b_2", blk))\
                    .then_inc(S["b2_tap0"], 1)
        c.wait_read(act, q0 + 2 * i, j)
        nc.scalar.activation(c.th[:, i % 2, :], V.cv[i % 2].rearrange("p m t -> p (m t)"),
                             ACT.Tanh, scale=0.5).then_inc(S["b2_tanh"], 1)
    ffn_loop(act, body)
    ln_scalar(c, act, 1)


def b2_vector(c, dve, ch):
    S, nc, V = c.S, c.nc, b2_views(c)
    v = nc.vector
    dve.wait_ge(S["b2_bias_mm"], 1)
    v.tensor_tensor(c.relg[0:8, :], c.ps[0:8, 5, 0:384], c.c("future")[0:8, :], ALU.add)\
        .then_inc(S["b2_bias_read"], 1)
    _, qq = PLAN["b2_q"]
    bias = c.table
    dve.wait_ge(S["bias_loaded"], 32)
    m = c.small
    for s in range(9):
        if s < 8:
            lg = V.logit[s % 4]
            dve.wait_ge(S["b2_scores"], s + 1)
            if s >= 4:
                dve.wait_ge(S["b2_turned"], s - 3)
            v.scalar_tensor_tensor(out=lg, in0=c.ps[:, 4 + s % 2, 0:384], scalar=0.125, in1=bias[:, s, :],
                                   op0=ALU.mult, op1=ALU.add).then_inc(S["b2_logit"], 1)
            dve.wait_ge(S["b2_logit"], s + 1)
            v.tensor_reduce(m[:, 64:65], lg[:, 0:P], AX.X, ALU.max).then_inc(S["b2_rowmax"], 1)
            v.tensor_reduce(m[:, 65:66], lg[:, P:384], AX.X, ALU.max).then_inc(S["b2_rowmax"], 1)
            dve.wait_ge(S["b2_rowmax"], 2 * s + 2)
            v.tensor_scalar(m[:, 2 * s:2 * s + 2], m[:, 64:66], -1.0, None, ALU.mult).then_inc(S["b2_max"], 1)
            dve.wait_ge(S["b2_max"], s + 1)
        if s >= 1:
            hd = s - 1
            lg = V.logit[hd % 4]
            dve.wait_ge(S["b2_exp"], 2 * hd + 2)
            ch.step(v.reciprocal(m[:, 66:68], m[:, 32 + 2 * hd:34 + 2 * hd]))
            ch.step(v.tensor_scalar(lg[:, 0:P], lg[:, 0:P], m[:, 66:67], None, ALU.mult))
            v.tensor_scalar(lg[:, P:384], lg[:, P:384], m[:, 67:68], None, ALU.mult)\
                .then_inc(S["b2_prob"], 1)
            dve.wait_ge(S["b2_prob"], hd + 1)
    for name in B2_UNITS:
        c.wait_read(dve, PLAN[name][1])
    ch.step(v.tensor_tensor(c.pad[:, 0:2, 3:3 + T], V.cc, V.cx, ALU.mult))
    for b in range(2):
        ch.step(v.tensor_scalar(V.conv[:, b, :], c.pad[:, b, 1:1 + T], c.p("conv_w_2", b), None, ALU.mult))
        for tap in (1, 2):
            ch.step(v.scalar_tensor_tensor(out=V.conv[:, b, :], in0=c.pad[:, b, 1 + tap:1 + tap + T],
                                           scalar=c.p("conv_w_2", 2 * tap + b), in1=V.conv[:, b, :],
                                           op0=ALU.mult, op1=ALU.add))
    v.tensor_tensor(V.mix[:, 4:6, :], V.conv, V.cb, ALU.mult).then_inc(S["b2_conv"], 1)
    src = V.pin
    for i, sh in enumerate((1, 2, 4, 8)):
        ch.step(v.tensor_copy(V.sums[i][:, :, 0:sh], src[:, :, 0:sh]))
        ch.step(v.tensor_tensor(V.sums[i][:, :, sh:T], src[:, :, sh:T], src[:, :, 0:T - sh], ALU.add))
        src = V.sums[i]
    inv = c.c("pool_inv").rearrange("p (m t) -> p m t", m=2)
    for i in range(4):
        e = 64 * (i % 2)
        ch.step(v.tensor_tensor(V.pooled[e:e + 64, i // 2, :], V.sums[i][e:e + 64, i // 2, :],
                                inv[e:e + 64, i // 2, :], ALU.mult))
    v.tensor_tensor(V.pooled, V.pooled, V.pin, ALU.subtract).then_inc(S["b2_pooled"], 1)
    dve.wait_ge(S["b2_pool_mm"], 1)
    for b in range(2):
        ins = v.tensor_scalar(V.mix[:, 6 + b, :], c.ps[:, 5, b * T:b * T + T], c.p("pool_scale_2", b), None,
                              ALU.mult)
        ch.step(ins) if b == 0 else ins.then_inc(S["b2_pool"], 1)
    ln_vector(c, dve, 0, PLAN["b2_out"][0] + 3, "ln1_g_2", "ln1_b_2", ch)

    n0, q0 = PLAN["b2_ffn"]

    def body(i, j):
        for g in range(2):
            q = q0 + 2 * i + g
            for tap in (1, 2):
                for m in range(2):
                    blk = 2 * i + m + (22 if g == 0 else 0)
                    k = PCOL["ffn_conv_w_2"] + 44 * (2 - tap) + blk
                    w = c.par[:, k:k + 1] if j is None else c.par[:, bass.ds(at(k, 4, j), 1)]
                    cv = V.cv[2 * g + i % 2][:, m, tap:T]
                    if tap == 1:
                        dve.wait_ge(S["b2_tap0"], at(4 * i + 2 * g + 2, 8, j))
                    else:
                        dve.wait_ge(S["b2_tap"], at(7 * i + (4 if g else 0) + m + 1, 14, j))
                    ins = v.scalar_tensor_tensor(out=cv, in0=c.bank(q)[:, m * T:m * T + T - tap], scalar=w,
                                                 in1=cv, op0=ALU.mult, op1=ALU.add)
                    if g == 0 and tap == 2 and m == 1:
                        c.read(ins, q)
                    else:
                        ins.then_inc(S["b2_tap"], 1)
        dve.wait_ge(S["b2_tanh"], at(i + 1, 2, j))
        c.wait_read(dve, q0 + 2 * i, j)
        v.scalar_tensor_tensor(out=c.t1[:, i % 2, :], in0=c.th[:, i % 2, :], scalar=1.0,
                               in1=V.cv[i % 2].rearrange("p m t -> p (m t)"), op0=ALU.add, op1=ALU.mult)\
            .then_inc(S["b2_half"], 1)
        if i >= 2:
            c.wait_done(dve, d_unit_of(n0, i - 2), j)
        dve.wait_ge(S["b2_tap"], at(7 * i + 7, 14, j))
        dve.wait_ge(S["b2_half"], at(i + 1, 2, j))
        c.read(v.scalar_tensor_tensor(out=c.hid[:, i % 2, :], in0=c.t1[:, i % 2, :], scalar=0.5,
                                      in1=V.cv[2 + i % 2].rearrange("p m t -> p (m t)"),
                                      op0=ALU.mult, op1=ALU.mult), q0 + 2 * i + 1)
    dve.wait_ge(S["b2_o_read"], 4)
    ffn_loop(dve, body)
    ln_vector(c, dve, 1, PLAN["b2_ffn"][0] + 3 * FFI - 1, "ln2_g_2", "ln2_b_2", ch)


def mem_scalar(c, act):
    S, nc, W = c.S, c.nc, c.work
    act.wait_ge(S["ln_out"], 16)
    rms_scalar(c, act, NK["mem"], src=W[0], ready=(S["mem_loaded"], 16))
    n0, q0 = PLAN["mem_k"]
    for u in range(8):
        c.wait_done(act, n0 + u)
        if u < 4:
            dst = W[8][:, 2 * u:2 * u + 2, :]
        else:
            dst = token_view(W[9])[:, :, (u - 4) * 256:(u - 4) * 256 + 256]
        c.read(nc.scalar.activation(dst, c.bank(q0 + u).rearrange("p (m t) -> p m t", m=2), ACT.Copy), q0 + u)


def token_view(w):
    return w[:, :, :].rearrange("p a b -> p (a b)").rearrange("p (m n) -> p m n", m=2)


def mem_tensor(c, pe):
    rms_tensor(c, pe, NK["mem"])
    pe.wait_ge(c.S["xn_ready"], 8 * NK["mem"] + 8)
    n0, q0 = PLAN["mem_k"]
    for u in range(8):
        p_unit(c, pe, n0 + u, q0 + u, c.work[1], token_major=u >= 4)


def mem_vector(c, dve):
    rms_vector(c, dve, NK["mem"], lambda b: ("mem_norm_3", b), c.work[1], src=c.work[0])


def ffn3(c, name, norm, f):
    k = NK[name]
    last = PLAN[name][0] + 3 * FFI - 1

    def scalar(act, ready):
        rms_scalar(c, act, k, ready=ready)
        swiglu_scalar(c, act, name, f)

    def tensor(pe):
        rms_tensor(c, pe, k)
        pe.wait_ge(c.S["xn_ready"], 8 * k + 8)
        ffn_tensor(c, pe, name, c.xn)

    def vector(dve, ch):
        rms_vector(c, dve, k, lambda b: (norm[0], norm[1] * 8 + b), c.xn)
        swiglu_vector(c, dve, name, f)
        add_residual(c, dve, last, 0.5, ch)
    return scalar, tensor, vector


def xattn_tensor(c, pe, i):
    S, nc, W, mm = c.S, c.nc, c.work, c.nc.tensor.matmul
    name = f"l{i}_x"
    rms_tensor(c, pe, NK[name])
    pe.wait_ge(S["xn_ready"], 8 * NK[name] + 8)
    n0, q0 = PLAN[f"l{i}_xq"]
    for u in range(4):
        p_unit(c, pe, n0 + u, q0 + u, c.xn)
    if i == 0:
        for u in range(8):
            c.wait_read(pe, PLAN["mem_k"][1] + u)
    v = token_view(W[9])
    for s in range(6):
        if s < 4:
            c.wait_read(pe, q0 + s)
            if s >= 2:
                pe.wait_ge(S["x_max"], 4 * i + s - 1)
                pe.wait_ge(S["x_exp"], 8 * i + 2 * s - 2)
            for n in range(2):
                for k in range(2):
                    ins = mm(c.ps[:, 4 + s % 2, n * T:n * T + T], W[0][:, 2 * s + k, n * P:n * P + P],
                             W[8][:, 2 * s + k, :], start=k == 0, stop=k == 1)
            ins.then_inc(S["x_scores"], 1)
        if 1 <= s < 5:
            hd = s - 1
            pe.wait_ge(S["x_prob"], 4 * i + hd + 1)
            if hd >= 1:
                pe.wait_ge(S["x_pt"], 4 * i + hd)
            for k in range(2):
                for n in range(2):
                    col = (2 * k + n) * P
                    ins = nc.tensor.transpose(c.ps[:, 6, col:col + P],
                                              W[2 + hd % 2][:, n, k * P:k * P + P], c.c("ident"))
            ins.then_inc(S["x_turned"], 1)
        if s >= 2:
            hd = s - 2
            pe.wait_ge(S["x_pt"], 4 * i + hd + 1)
            if hd >= 1:
                pe.wait_ge(S["x_o_read"], 4 * i + hd)
            for d in range(2):
                for k in range(2):
                    ins = mm(c.ps[:, 7, d * T:d * T + T], v[:, k, (2 * hd + d) * P:(2 * hd + d) * P + P],
                             W[4][:, 2 * (hd % 2) + k, :], start=k == 0, stop=k == 1)
            ins.then_inc(S["x_o"], 1)
    n0, _ = PLAN[f"l{i}_xo"]
    pe.wait_ge(S["x_o_read"], 4 * i + 4)
    for u in range(4):
        d_unit(c, pe, n0 + u, lambda k: W[1][:, 2 * u + k, :], u == 0, u == 3)


def xattn_scalar(c, act, i, ready):
    S, nc, W = c.S, c.nc, c.work
    rms_scalar(c, act, NK[f"l{i}_x"], ready=ready)
    n0, q0 = PLAN[f"l{i}_xq"]
    for u in range(4):
        c.wait_done(act, n0 + u)
        c.read(nc.scalar.activation(W[0][:, 2 * u:2 * u + 2, :],
                                    c.bank(q0 + u).rearrange("p (m t) -> p m t", m=2), ACT.Copy), q0 + u)
    for s in range(6):
        if s < 4:
            act.wait_ge(S["x_max"], 4 * i + s + 1)
            if s >= 2:
                act.wait_ge(S["x_turned"], 4 * i + s - 1)
            for n in range(2):
                nc.scalar.activation(W[2 + s % 2][:, n, :], c.ps[:, 4 + s % 2, n * T:n * T + T], ACT.Exp,
                                     scale=1.0 / 16, bias=c.small[:, 4 * s + n:4 * s + n + 1],
                                     accum_out=c.small[:, 32 + 4 * s + n:33 + 4 * s + n])\
                    .then_inc(S["x_exp"], 1)
        if 1 <= s < 5:
            hd = s - 1
            act.wait_ge(S["x_turned"], 4 * i + hd + 1)
            if hd >= 2:
                act.wait_ge(S["x_o"], 4 * i + hd - 1)
            nc.scalar.activation(W[4][:, 2 * (hd % 2):2 * (hd % 2) + 2, :],
                                 c.ps[:, 6, :].rearrange("p (k q) -> p k q", k=2), ACT.Copy)\
                .then_inc(S["x_pt"], 1)
        if s >= 2:
            hd = s - 2
            act.wait_ge(S["x_o"], 4 * i + hd + 1)
            nc.scalar.activation(W[1][:, 2 * hd:2 * hd + 2, :],
                                 c.ps[:, 7, :].rearrange("p (d q) -> p d q", d=2), ACT.Copy)\
                .then_inc(S["x_o_read"], 1)


def xattn_vector(c, dve, i, ch):
    S, W, v, m = c.S, c.work, c.nc.vector, c.small
    rms_vector(c, dve, NK[f"l{i}_x"], lambda b: ("xattn_norm_3", i * 8 + b), c.xn)
    for s in range(5):
        if s < 4:
            dve.wait_ge(S["x_scores"], 4 * i + s + 1)
            ch.step(v.tensor_reduce(m[:, 64:66], c.ps[:, 4 + s % 2, :].rearrange("p (n k) -> p n k", n=2),
                                    AX.X, ALU.max))
            v.tensor_scalar(m[:, 4 * s:4 * s + 2], m[:, 64:66], -1.0 / 16, None, ALU.mult)\
                .then_inc(S["x_max"], 1)
            dve.wait_ge(S["x_max"], 4 * i + s + 1)
        if s >= 1:
            hd = s - 1
            dve.wait_ge(S["x_exp"], 8 * i + 2 * hd + 2)
            ch.step(v.reciprocal(m[:, 66:68], m[:, 32 + 4 * hd:34 + 4 * hd]))
            pr = W[2 + hd % 2]
            ch.step(v.tensor_scalar(pr[:, 0, :], pr[:, 0, :], m[:, 66:67], None, ALU.mult))
            v.tensor_scalar(pr[:, 1, :], pr[:, 1, :], m[:, 67:68], None, ALU.mult).then_inc(S["x_prob"], 1)
            dve.wait_ge(S["x_prob"], 4 * i + hd + 1)
    add_residual(c, dve, PLAN[f"l{i}_xo"][0] + 3, 1.0, ch)


def gmlp_tensor(c, pe):
    S, W, mm = c.S, c.work, c.nc.tensor.matmul
    k = NK["l1_mix"]
    rms_tensor(c, pe, k)
    pe.wait_ge(S["xn_ready"], 8 * k + 8)
    n0, q0 = PLAN["gm_v"]
    for u in range(8):
        p_unit(c, pe, n0 + u, q0 + u, c.xn, token_major=True)
    n1, q1 = PLAN["gm_u"]
    for u in range(8):
        p_unit(c, pe, n1 + u, q1 + u, c.xn)
    pe.wait_ge(S["gm_vn"], 2)
    pe.wait_ge(S["gm_ws"], 1)
    for g in range(16):
        if g >= 8:
            pe.wait_ge(S["gm_sv_read"], 2 * (g // 2 - 4) + 2)
        if g == 0:
            pe.wait_ge(S["h_ready"], HR["l1_ffn1"])
            for u in range(4, 8):
                c.wait_read(pe, q1 + u)
        for n in range(2):
            mm(c.ps[:, g // 2 % 8, 256 * (g % 2) + n * P:256 * (g % 2) + n * P + P],
               W[n][:, :, :].rearrange("p a b -> p (a b)")[:, g * P:g * P + P],
               W[2][:, :, :].rearrange("p a b -> p (a b)")[:, g * P:g * P + P],
               start=True, stop=True).then_inc(S["gm_sv"], 1)
    n0, _ = PLAN["gm_out"]
    pe.wait_ge(S["gm_sv_read"], 16)
    for u in range(8):
        pe.wait_ge(S["gm_y"], 2 * u + 2)
        d_unit(c, pe, n0 + u, lambda k: W[4 + u // 4][:, 2 * (u % 4) + k, :], u == 0, u == 7)


def gmlp_scalar(c, act, ready):
    S, nc, W = c.S, c.nc, c.work
    rms_scalar(c, act, NK["l1_mix"], ready=ready)
    n0, q0 = PLAN["gm_v"]
    for u in range(8):
        c.wait_done(act, n0 + u)
        bank = c.bank(q0 + u).rearrange("p (m n) -> p m n", m=2)
        dst = [W[n][:, :, :].rearrange("p a b -> p (a b)")[:, u * 256:u * 256 + 256] for n in range(2)]
        nc.scalar.activation(dst[0], bank[:, 0, :], ACT.Gelu_apprx_tanh).then_inc(S["gm_v0"], 1)
        c.read(nc.scalar.activation(dst[1], bank[:, 1, :], ACT.Gelu_apprx_tanh), q0 + u)
    act.wait_ge(S["gm_v0"], 8)
    for u in range(4, 8):
        c.wait_read(act, q0 + u)
    for n in range(2):
        nc.scalar.activation(W[6 + n][:, :, :], W[n][:, :, :], ACT.Square,
                             accum_out=c.small[:, n:n + 1]).then_inc(S["gm_sq"], 1)
    act.wait_ge(S["gm_ms"], 1)
    nc.scalar.activation(c.small[:, 4:6], c.small[:, 2:4], ACT.Sqrt).then_inc(S["gm_std"], 1)
    n1, q1 = PLAN["gm_u"]
    for u in range(8):
        c.wait_done(act, n1 + u)
        dst = W[4 + u // 4][:, 2 * (u % 4):2 * (u % 4) + 2, :]
        c.read(nc.scalar.activation(dst, c.bank(q1 + u).rearrange("p (m t) -> p m t", m=2),
                                    ACT.Gelu_apprx_tanh), q1 + u)


def gmlp_vector(c, dve, ch):
    S, W, v, m = c.S, c.work, c.nc.vector, c.small
    rms_vector(c, dve, NK["l1_mix"], lambda b: ("mix_norm_3", 8 + b), c.xn)
    dve.wait_ge(S["gm_loaded"], 32)
    ws = W[2][:, :, :].rearrange("p a b -> p (a b)").rearrange("p (g t) -> p g t", g=16)
    causal = c.c("causal").rearrange("p (a t) -> p a t", a=1).to_broadcast([P, 16, P])
    v.tensor_tensor(ws, ws, causal, ALU.mult).then_inc(S["gm_ws"], 1)
    dve.wait_ge(S["gm_sq"], 2)
    v.tensor_scalar(m[:, 2:4], m[:, 0:2], 1.0 / 2048, EPS, ALU.mult, ALU.add).then_inc(S["gm_ms"], 1)
    dve.wait_ge(S["gm_std"], 1)
    ch.step(v.reciprocal(m[:, 6:8], m[:, 4:6]))
    for n in range(2):
        v.tensor_scalar(W[n][:, :, :], W[n][:, :, :], m[:, 6 + n:7 + n], None, ALU.mult)\
            .then_inc(S["gm_vn"], 1)
    bs = W[3][:, :, :].rearrange("p a b -> p (a b)").rearrange("p (g t) -> p g t", g=16)
    for g in range(16):
        dve.wait_ge(S["gm_sv"], 2 * (g // 2 * 2 + 2))
        if g == 0:
            _, q1 = PLAN["gm_u"]
        c.wait_read(dve, q1 + g // 2)
        sv = W[6 + g // 8][:, g % 8, :]
        v.scalar_tensor_tensor(out=sv.rearrange("p (n t) -> p n t", n=2),
                               in0=c.ps[:, g // 2 % 8, 256 * (g % 2):256 * (g % 2) + 256]
                               .rearrange("p (n t) -> p n t", n=2),
                               scalar=c.p("gmlp_v_norm_3", g),
                               in1=bs[:, g:g + 1, :].to_broadcast([P, 2, P]),
                               op0=ALU.mult, op1=ALU.add).then_inc(S["gm_sv_read"], 1)
        dve.wait_ge(S["gm_sv_read"], g + 1)
        v.tensor_tensor(W[4 + g // 8][:, g % 8, :], W[4 + g // 8][:, g % 8, :], sv, ALU.mult)\
            .then_inc(S["gm_y"], 1)
    add_residual(c, dve, PLAN["gm_out"][0] + 7, 1.0, ch)


DECAY_SCALE = math.exp(-0.5) / 2


def rw_views(c):
    W = c.work

    class V:
        bonus = c.pad[:, :, 0:T]
        vt, kt, bt = (token_view(w) for w in (c.sq, c.xn, W[3]))
        lora1 = c.table[:, :, 0:288]
        lora_wa = c.t1[:, :, :].rearrange("p a b -> p (a b)")
        lora_g = c.hid[:, :, :].rearrange("p a b -> p (a b)")
        lora_gt = c.th[:, :, :].rearrange("p a b -> p (a b)")[0:32, :]
        low = W[2][:, :, :].rearrange("p a b -> p (a b)").rearrange("p (i t) -> p i t", i=16)
        inv = W[6][:, :, :].rearrange("p a b -> p (a b)").rearrange("p (i t) -> p i t", i=16)
        tab = c.table[:, :, :].rearrange("p a b -> p (a b)")
        invt = tab[:, 0:2048].rearrange("p (i t) -> p i t", i=16)
        x0 = tab[:, 2048:3072].rearrange("p (h n) -> p h n", h=2)
        zed = [c.th[:, :, :].rearrange("p a b -> p (a b)").rearrange("p (i t) -> p i t", i=8),
               c.t1[:, :, :].rearrange("p a b -> p (a b)").rearrange("p (i t) -> p i t", i=8)]
        sa = [c.std, c.rstd]
        state = c.hid[:, 0, :].rearrange("p (b i) -> p b i", b=8)
        pend = c.small[:, 160:192].rearrange("p (b n) -> p b n", b=8)
        gk = low
        rb = invt
        rk = zed
    return V


def rw_head(i):
    g, r = i // 4, i % 4
    half, blk = g % 2, 4 * (g // 2) + r
    return 2 * blk + half, half, blk


def rw_z(V, i):
    return V.zed[i // 8][:, i % 8, :]


def rw_z4(V, g):
    return V.zed[g // 2][:, 4 * (g % 2):4 * (g % 2) + 4, :]


RW_PE, RW_VEC = 64, 68


def pe_step(n, kind, l, g):
    if l == 0:
        k = {"z": g, "zt": 4 + g}[kind]
    elif l < 5:
        k = 8 + 12 * (l - 1) + {"z": g, "q": 4 + 2 * g, "x": 5 + 2 * g}[kind]
    else:
        k = 8 + 12 * 4 + {"z": g, "q": 4 + g}[kind]
    return RW_PE * n + k + 1


def vec_step(n, kind, l, g):
    if l == 0:
        k = {"z": g, "q": 4 + g, "x": 8 + g}[kind]
    elif l < 5:
        k = 12 + 12 * (l - 1) + {"z": g, "q": 4 + 2 * g, "x": 5 + 2 * g}[kind]
    else:
        k = 12 + 12 * 4 + {"z": g, "q": 4 + g}[kind]
    return RW_VEC * n + k + 1


def rw_tensor(c, pe):
    S, nc, W, V, mm = c.S, c.nc, c.work, rw_views(c), c.nc.tensor.matmul
    tr = nc.tensor.transpose
    rms_tensor(c, pe, NK["l0_mix"])
    for i, name in enumerate(("rw_r", "rw_k", "rw_v")):
        pe.wait_ge(S["rw_mix"], 8 * i + 8)
        n0, q0 = PLAN[name]
        for u in range(4):
            p_unit(c, pe, n0 + u, q0 + u, W[1 + i])
    pe.wait_ge(S["lora_loaded"], 64)
    pe.wait_ge(S["rw_mix"], 48)
    for out, cols, x in ((c.ps[0:64, 4, 0:T], (0, 64), W[4]), (c.ps[64:128, 4, 0:T], (64, 128), W[5]),
                         (c.ps[:, 5, 0:T], (128, 256), W[6]), (c.ps[0:32, 6, 0:T], (256, 288), W[6])):
        for k in range(KB):
            ins = mm(out, V.lora1[:, k, cols[0]:cols[1]], x[:, k, :], start=k == 0, stop=k == KB - 1)
    ins.then_inc(S["rw_lora_mm"], 1)
    pe.wait_ge(S["rw_lora_act"], 4)
    for b in range(KB):
        o = slice(b * P, b * P + P)
        if b:
            pe.wait_ge(S["rw_z_read"], 3 * b)
        mm(c.ps[:, 4, 0:T], V.lora_wa[0:64, o], c.sq[0:64, 0, :], start=True, stop=True)
        mm(c.ps[:, 5, 0:T], V.lora_wa[64:128, o], c.sq[64:128, 0, :], start=True, stop=True)
        mm(c.ps[:, 6, 0:T], V.lora_g[:, o], c.sq[:, 1, :], start=True, stop=False)
        mm(c.ps[:, 6, 0:T], V.lora_gt[:, o], c.sq[0:32, 2, :], start=False, stop=True)\
            .then_inc(S["rw_z_mm"], 1)
    pe.wait_ge(S["rw_z_read"], 24)
    pe.wait_ge(S["rw_kk_sq"], 1)
    for b in range(KB):
        ins = mm(c.ps[:, 4 + b // 2, (b % 2) * T:(b % 2) * T + T], c.c("sum_h"), c.xn[:, b, :],
                 start=True, stop=True)
    ins.then_inc(S["rw_kk_sum"], 1)
    pe.wait_ge(S["rw_norm"], 4)
    pe.wait_ge(S["rw_rk"], 1)
    for b in range(KB):
        ins = mm(c.ps[:, 4 + b // 2, (b % 2) * T:(b % 2) * T + T], c.c("sum_h"), W[6][:, b, :],
                 start=True, stop=True)
    ins.then_inc(S["rw_rk_sum"], 1)
    _, qv = PLAN["rw_v"]
    for u in range(4):
        c.wait_read(pe, qv + u)
    turn = 0
    for src, ready in ((W[2], ("rw_vready", 1)), (W[1], ("rw_kt_ready", 1)), (W[4], ("rw_bt_ready", 1))):
        pe.wait_ge(S[ready[0]], ready[1])
        for g in range(4):
            if turn >= 4:
                pe.wait_ge(S["rw_turn_read"], turn - 3)
            for r in range(4):
                b, n = 4 * (g % 2) + r, g // 2
                ins = tr(c.ps[:, turn % 4, r * P:r * P + P], src[:, b, n * P:n * P + P], c.c("ident"))
            ins.then_inc(S["rw_turned"], 1)
            turn += 1
    pe.wait_ge(S["rw_turn_read"], 12)
    pe.wait_ge(S["rw_tilde"], 4)
    pe.wait_ge(S["rw_bonus"], 4)
    for n in range(2):
        tok = slice(n * P, n * P + P)
        if n:
            pe.wait_ge(S["rw_x0_read"], 2)
            pe.wait_ge(S["rw_sa_read"], 4)
            pe.wait_ge(S["rw_y_add"], 4)
            pe.wait_ge(S["rw_y_read"], 2)
            pe.wait_ge(S["rw_state"], 2)
        for g in range(4):
            for r in range(4):
                _, e, b = rw_head(4 * g + r)
                rows = slice(64 * e, 64 * e + 64)
                ins = mm(c.ps[:, g, r * P:r * P + P], W[0][rows, b, tok], W[4][rows, b, tok],
                         start=True, stop=True)
            ins.then_inc(S["rw_low_mm"], 1)
        for g in range(4):
            pe.wait_ge(S["rw_low"], 4 * n + g + 1)
            for r in range(4):
                ins = tr(c.ps[:, 4 + g, r * P:r * P + P], V.low[:, 4 * g + r, :], c.c("ident"))
            ins.then_inc(S["rw_inv_mm"], 1)
        for g in range(4):
            pe.wait_ge(S["rw_inv"], vec_step(n, "z", 0, g))
            for r in range(4):
                ins = tr(c.ps[:, g, r * P:r * P + P], rw_z(V, 4 * g + r), c.c("ident"))
            ins.then_inc(S["rw_inv_mm"], 1)
        for l in range(1, 6):
            for g in range(4):
                pe.wait_ge(S["rw_inv"], vec_step(n, "x", l - 1, g))
                for r in range(4):
                    ins = mm(c.ps[:, 4 + g, r * P:r * P + P], V.low[:, 4 * g + r, :], V.inv[:, 4 * g + r, :],
                             start=True, stop=True)
                ins.then_inc(S["rw_inv_mm"], 1)
            for g in range(4):
                pe.wait_ge(S["rw_inv"], vec_step(n, "z", l, g))
                for r in range(4):
                    ins = mm(c.ps[:, g, r * P:r * P + P], V.invt[:, 4 * g + r, :], rw_z(V, 4 * g + r),
                             start=True, stop=True)
                ins.then_inc(S["rw_inv_mm"], 1)
                if l < 5:
                    for r in range(4):
                        ins = mm(c.ps[:, 4 + g, r * P:r * P + P], rw_z(V, 4 * g + r),
                                 V.invt[:, 4 * g + r, :], start=True, stop=True)
                    ins.then_inc(S["rw_inv_mm"], 1)
        for j, (x, y) in enumerate(((1, 0), (4, 7), (1, 7))):
            for g in range(4):
                bank = (4 + g) if j == 1 else g
                if j == 0:
                    pe.wait_ge(S["rw_inv"], vec_step(n, "q", 5, g))
                elif j == 1:
                    pe.wait_ge(S["rw_inv"], vec_step(n, "z", 5, g))
                else:
                    pe.wait_ge(S["rw_mat"], 12 * n + g + 1)
                for r in range(4):
                    _, e, b = rw_head(4 * g + r)
                    rows = slice(64 * e, 64 * e + 64)
                    ins = mm(c.ps[:, bank, r * P:r * P + P], W[x][rows, b, tok], W[y][rows, b, tok],
                             start=True, stop=True)
                ins.then_inc(S["rw_mat_mm"], 1)
        pe.wait_ge(S["rw_mat"], 12 * n + 12)
        for i in range(16):
            hd, e, b = rw_head(i)
            mm(c.ps[:, e, b * 64:b * 64 + 64], V.gk[:, i, :], V.vt[:, n, hd * 64:hd * 64 + 64],
               start=b == 0, stop=False, skip_group_check=True)
        for cc in range(2):
            ci = 2 * n + cc
            rows = slice(64 * cc, 64 * cc + 64)
            tk = slice(ci * 64, ci * 64 + 64)
            if ci:
                pe.wait_ge(S["rw_state"], ci)
            if cc:
                pe.wait_ge(S["rw_x0_read"], ci)
            for i in range(16):
                hd, e, b = rw_head(i)
                half = slice(64 * e, 64 * e + 64)
                ins = mm(c.ps[rows, e, b * 64:b * 64 + 64], W[0][half, b, tk],
                         V.state[half, b, :], start=False, stop=True, skip_group_check=True)
            ins.then_inc(S["rw_x0"], 1)
            if ci:
                pe.wait_ge(S["rw_y_add"], 2 * ci)
            for i in range(16):
                hd, e, b = rw_head(i)
                half = slice(64 * e, 64 * e + 64)
                ins = mm(c.ps[half, 7 - 2 * e, b * 64:b * 64 + 64], V.state[half, b, :], W[7][half, b, tk],
                         start=True, stop=True)
            ins.then_inc(S["rw_ys"], 1)
            pe.wait_ge(S["rw_x0_read"], ci + 1)
            if ci:
                pe.wait_ge(S["rw_sa_read"], 2 * ci)
            for i in range(16):
                hd, e, b = rw_head(i)
                ins = mm(c.ps[rows, 2 + e, b * 64:b * 64 + 64], V.inv[rows, i, rows],
                         V.x0[rows, e, b * 64:b * 64 + 64], start=True, stop=True)
            ins.then_inc(S["rw_sa"], 1)
            pe.wait_ge(S["rw_sa_read"], 2 * ci + 2)
            if ci < 3:
                for i in range(16):
                    hd, e, b = rw_head(i)
                    half = slice(64 * e, 64 * e + 64)
                    mm(c.ps[half, 6, b * 64:b * 64 + 64], V.bt[rows, n, hd * 64:hd * 64 + 64],
                       V.sa[e][rows, b * 64:b * 64 + 64], start=True, stop=False, skip_group_check=True)
                    ins = mm(c.ps[half, 6, b * 64:b * 64 + 64], V.kt[rows, n, hd * 64:hd * 64 + 64],
                             V.vt[rows, n, hd * 64:hd * 64 + 64], start=False, stop=True,
                             skip_group_check=True)
                ins.then_inc(S["rw_s"], 1)
            if ci:
                pe.wait_ge(S["rw_y_read"], ci)
            for i in range(16):
                hd, e, b = rw_head(i)
                half = slice(64 * e, 64 * e + 64)
                mm(c.ps[half, 4, b * 64:b * 64 + 64], V.vt[rows, n, hd * 64:hd * 64 + 64],
                   V.rk[i // 8][rows, i % 8, rows], start=True, stop=False, skip_group_check=True)
                ins = mm(c.ps[half, 4, b * 64:b * 64 + 64], V.sa[e][rows, b * 64:b * 64 + 64],
                         V.rb[rows, i, rows], start=False, stop=True, skip_group_check=True)
            ins.then_inc(S["rw_y"], 1)
    pe.wait_ge(S["rw_y_add"], 8)
    pe.wait_ge(S["rw_sa_read"], 8)
    pe.wait_ge(S["rw_x0_read"], 4)
    for b in range(KB):
        ins = mm(c.ps[:, b // 2, (b % 2) * T:(b % 2) * T + T], c.c("mean_h"), W[7][:, b, :],
                 start=True, stop=True)
    ins.then_inc(S["rw_mean"], 1)
    pe.wait_ge(S["rw_cen_sq"], 1)
    pe.wait_ge(S["rw_y_read"], 4)
    for b in range(KB):
        ins = mm(c.ps[:, 4 + b // 2, (b % 2) * T:(b % 2) * T + T], c.c("mean_h"), W[6][:, b, :],
                 start=True, stop=True)
    ins.then_inc(S["rw_var"], 1)
    n0, _ = PLAN["rw_out"]
    pe.wait_ge(S["rw_gn_std"], 4)
    for u in range(4):
        pe.wait_ge(S["rw_out"], u + 1)
        d_unit(c, pe, n0 + u, lambda k: W[7][:, 2 * u + k, :], u == 0, u == 3)


def rw_scalar(c, act, ready):
    S, nc, W, V = c.S, c.nc, c.work, rw_views(c)
    A = nc.scalar.activation
    rms_scalar(c, act, NK["l0_mix"], ready=ready)
    for i, name in enumerate(("rw_r", "rw_k", "rw_v")):
        n0, q0 = PLAN[name]
        dst = (W[7], W[1], W[2])[i]
        for u in range(4):
            c.wait_done(act, n0 + u)
            if i and u == 0:
                for k in range(4):
                    c.wait_done(act, PLAN[("rw_r", "rw_k")[i - 1]][0] + k)
            c.read(A(dst[:, 2 * u:2 * u + 2, :], c.bank(q0 + u).rearrange("p (m t) -> p m t", m=2),
                     ACT.Copy), q0 + u)
    act.wait_ge(S["rw_lora_mm"], 1)
    A(c.sq[0:64, 0, :], c.ps[0:64, 4, 0:T], ACT.Tanh).then_inc(S["rw_lora_act"], 1)
    A(c.sq[64:128, 0, :], c.ps[64:128, 4, 0:T], ACT.Copy).then_inc(S["rw_lora_act"], 1)
    A(c.sq[:, 3, :], c.ps[:, 5, 0:T], ACT.Tanh, scale=0.5).then_inc(S["rw_lora_g"], 1)
    A(c.sq[0:32, 4, :], c.ps[0:32, 6, 0:T], ACT.Tanh, scale=0.5).then_inc(S["rw_lora_g"], 1)
    act.wait_ge(S["rw_half_bias"], 2)
    for b in range(KB):
        act.wait_ge(S["rw_z_mm"], b + 1)
        A(W[3][:, b, :], c.ps[:, 4, 0:T], ACT.Tanh, scale=0.5, bias=c.small[:, 128 + b:129 + b])\
            .then_inc(S["rw_z_read"], 1)
        A(W[4][:, b, :], c.ps[:, 5, 0:T], ACT.Tanh, scale=0.5, bias=c.small[:, 136 + b:137 + b])\
            .then_inc(S["rw_z_read"], 1)
        A(W[5][:, b, :], c.ps[:, 6, 0:T], ACT.Copy).then_inc(S["rw_z_read"], 1)
    act.wait_ge(S["rw_kk"], 8)
    A(c.xn[:, :, :], W[0][:, :, :], ACT.Square).then_inc(S["rw_kk_sq"], 1)
    act.wait_ge(S["rw_kk_sum"], 1)
    for g in range(4):
        A(W[6][:, 2 * g:2 * g + 2, :], c.ps[:, 4 + g, :].rearrange("p (m t) -> p m t", m=2), ACT.Sqrt)\
            .then_inc(S["rw_norm"], 1)
    act.wait_ge(S["rw_before"], 1)
    A(W[3][:, :, :], W[3][:, :, :], ACT.Exp).then_inc(S["rw_exp"], 1)
    act.wait_ge(S["rw_rk_sum"], 1)
    A(W[6][:, :, :], c.xn[:, :, :], ACT.Exp).then_inc(S["rw_exp"], 1)
    act.wait_ge(S["rw_tilde"], 1)
    A(W[3][:, :, :], c.xn[:, :, :], ACT.Exp, scale=-1.0).then_inc(S["rw_exp"], 1)
    for turn in range(12):
        n, h = turn // 2 % 2, turn % 2
        dst = (V.vt, V.kt, V.bt)[turn // 4]
        act.wait_ge(S["rw_turned"], turn + 1)
        if turn == 4:
            act.wait_ge(S["rw_exp"], 3)
        if turn == 8:
            act.wait_ge(S["rw_tilde"], 4)
        A(dst[:, n, h * 512:h * 512 + 512], c.ps[:, turn % 4, :], ACT.Copy).then_inc(S["rw_turn_read"], 1)
    for n in range(2):
        for g in range(4):
            act.wait_ge(S["rw_low_mm"], 4 * n + g + 1)
            A(V.low[:, 4 * g:4 * g + 4, :], c.ps[:, g, :].rearrange("p (r t) -> p r t", r=4), ACT.Copy)\
                .then_inc(S["rw_low"], 1)
        for cc in range(2):
            ci = 2 * n + cc
            rows = slice(64 * cc, 64 * cc + 64)
            act.wait_ge(S["rw_x0"], ci + 1)
            A(V.x0[rows, :, :], c.ps[rows, 0:2, :], ACT.Copy).then_inc(S["rw_x0_read"], 1)
            act.wait_ge(S["rw_sa"], ci + 1)
            for e in range(2):
                A(V.sa[e][rows, :], c.ps[rows, 2 + e, :], ACT.Copy, scale=-1.0).then_inc(S["rw_sa_read"], 1)
            act.wait_ge(S["rw_y"], ci + 1)
            A(W[7][:, :, ci * 64:ci * 64 + 64], c.ps[:, 4, :].rearrange("p (b t) -> p b t", b=8), ACT.Copy)\
                .then_inc(S["rw_y_read"], 1)
    act.wait_ge(S["rw_cen"], 4)
    A(W[6][:, :, :], W[7][:, :, :], ACT.Square).then_inc(S["rw_cen_sq"], 1)
    act.wait_ge(S["rw_var"], 1)
    for g in range(4):
        A(W[2][:, 2 * g:2 * g + 2, :], c.ps[:, 4 + g, :].rearrange("p (m t) -> p m t", m=2), ACT.Sqrt,
          bias=c.eps[:, 2:3]).then_inc(S["rw_gn_std"], 1)


def rw_vector(c, dve, ch):
    S, W, V, v = c.S, c.work, rw_views(c), c.nc.vector
    rms_vector(c, dve, NK["l0_mix"], lambda b: ("mix_norm_3", b), c.xn)
    dve.wait_ge(S["xn_ready"], 8 * NK["l0_mix"] + 8)
    v.tensor_scalar(c.small[:, 128:136], c.p("rwkv_w0_3", 0, 8), 0.5, None, ALU.mult)\
        .then_inc(S["rw_half_bias"], 1)
    v.tensor_scalar(c.small[:, 136:144], c.p("rwkv_a0_3", 0, 8), 0.5, None, ALU.mult)\
        .then_inc(S["rw_half_bias"], 1)
    ch.step(v.tensor_scalar(W[0][:, :, 0:1], c.xn[:, :, 0:1], -1.0, None, ALU.mult))
    ch.step(v.tensor_tensor(W[0][:, :, 1:T], c.xn[:, :, 0:T - 1], c.xn[:, :, 1:T], ALU.subtract))
    for i, m in enumerate((0, 2, 3, 1, 4, 5)):
        for b in range(KB):
            v.scalar_tensor_tensor(out=W[1 + i][:, b, :], in0=W[0][:, b, :],
                                   scalar=c.p("rwkv_mu_3", 8 * m + b), in1=c.xn[:, b, :],
                                   op0=ALU.mult, op1=ALU.add).then_inc(S["rw_mix"], 1)
    dve.wait_ge(S["rw_lora_g"], 2)
    v.tensor_scalar(c.sq[:, 1, :], c.sq[:, 3, :], 1.0, 0.5, ALU.add, ALU.mult).then_inc(S["rw_lora_act"], 1)
    v.tensor_scalar(c.sq[0:32, 2, :], c.sq[0:32, 4, :], 1.0, 0.5, ALU.add, ALU.mult)\
        .then_inc(S["rw_lora_act"], 1)
    _, qk = PLAN["rw_k"]
    for u in range(4):
        c.wait_read(dve, qk + u)
    dve.wait_ge(S["rw_mix"], 48)
    for b in range(KB):
        v.tensor_scalar(W[0][:, b, :], W[1][:, b, :], c.p("rwkv_k_k_3", b), None, ALU.mult)\
            .then_inc(S["rw_kk"], 1)
    dve.wait_ge(S["rw_z_read"], 24)
    ch.step(v.tensor_scalar(W[3][:, :, :], W[3][:, :, :], 1.0, -DECAY_SCALE, ALU.add, ALU.mult))
    ch.step(v.tensor_scalar(W[4][:, :, :], W[4][:, :, :], 1.0, 0.5, ALU.add, ALU.mult))
    dve.wait_ge(S["rw_norm"], 4)
    ch.step(v.tensor_scalar(W[6][:, :, :], W[6][:, :, :], 1e-12, None, ALU.max))
    ch.step(v.reciprocal(W[6][:, :, :], W[6][:, :, :]))
    ch.step(v.tensor_tensor(W[0][:, :, :], W[0][:, :, :], W[6][:, :, :], ALU.mult))
    for b in range(KB):
        ch.step(v.tensor_scalar(W[6][:, b, :], W[4][:, b, :], -1.0, c.p("rwkv_k_a_3", b), ALU.add, ALU.mult))
        ch.step(v.scalar_tensor_tensor(out=W[1][:, b, :], in0=W[6][:, b, :], scalar=1.0,
                                       in1=W[1][:, b, :], op0=ALU.add, op1=ALU.mult))
    ch.step(v.tensor_tensor(W[4][:, :, :], W[4][:, :, :], W[0][:, :, :], ALU.mult))
    _, qr = PLAN["rw_r"]
    for u in range(4):
        c.wait_read(dve, qr + u)
    for b in range(KB):
        ins = v.scalar_tensor_tensor(out=W[6][:, b, :], in0=W[7][:, b, :], scalar=c.p("rwkv_r_k_3", b),
                                     in1=W[1][:, b, :], op0=ALU.mult, op1=ALU.mult)
        if b < KB - 1:
            ch.step(ins)
    ins.then_inc(S["rw_rk"], 1)
    dve.wait_ge(S["rw_kk_sum"], 1)
    for b in range(KB):
        ch.step(v.tensor_tensor_scan(c.xn[:, b, :], c.c("reset"), W[3][:, b, :], 0.0, ALU.mult, ALU.add))
    v.tensor_tensor(W[3][:, :, :], c.xn[:, :, :], W[3][:, :, :], ALU.subtract).then_inc(S["rw_before"], 1)
    _, qv = PLAN["rw_v"]
    for u in range(4):
        c.wait_read(dve, qv + u)
    dve.wait_ge(S["rw_rk_sum"], 1)
    for g in range(4):
        v.tensor_tensor(V.bonus[:, 2 * g:2 * g + 2, :], c.ps[:, 4 + g, :].rearrange("p (m t) -> p m t", m=2),
                        W[2][:, 2 * g:2 * g + 2, :], ALU.mult).then_inc(S["rw_bonus"], 1)
    dve.wait_ge(S["rw_bonus"], 4)
    v.tensor_copy(c.small[:, 200:201], c.small[:, 128:129]).then_inc(S["rw_vready"], 1)
    dve.wait_ge(S["rw_exp"], 1)
    v.tensor_tensor(W[0][:, :, :], W[0][:, :, :], W[3][:, :, :], ALU.mult).then_inc(S["rw_tilde"], 1)
    dve.wait_ge(S["rw_exp"], 2)
    ch.step(v.tensor_copy(V.pend, W[6][:, :, CHUNK - 1:T:CHUNK]))
    v.tensor_tensor(W[7][:, :, :], W[7][:, :, :], W[6][:, :, :], ALU.mult).then_inc(S["rw_tilde"], 1)
    dve.wait_ge(S["rw_exp"], 3)
    v.tensor_tensor(W[1][:, :, :], W[1][:, :, :], W[3][:, :, :], ALU.mult).then_inc(S["rw_kt_ready"], 1)
    dve.wait_ge(S["rw_kt_ready"], 1)
    v.tensor_tensor(W[4][:, :, :], W[4][:, :, :], W[3][:, :, :], ALU.mult).then_inc(S["rw_tilde"], 1)
    dve.wait_ge(S["rw_tilde"], 3)
    v.memset(V.state, 0.0).then_inc(S["rw_tilde"], 1)
    v.tensor_copy(c.small[:, 200:201], c.small[:, 128:129]).then_inc(S["rw_bt_ready"], 1)

    def four(name):
        return c.c(name).rearrange("p (a t) -> p a t", a=1).to_broadcast([P, 4, P])

    def bank(g):
        return c.ps[:, g, :].rearrange("p (r t) -> p r t", r=4)

    dve.wait_ge(S["rw_turn_read"], 12)
    dve.wait_ge(S["rw_tilde"], 4)
    for n in range(2):
        if n:
            dve.wait_ge(S["rw_y"], 2)
        for g in range(4):
            dve.wait_ge(S["rw_inv_mm"], pe_step(n, "z", 0, g))
            v.tensor_tensor(rw_z4(V, g), bank(4 + g), four("level1"), ALU.mult).then_inc(S["rw_inv"], 1)
        for g in range(4):
            dve.wait_ge(S["rw_inv"], vec_step(n, "z", 0, g))
            v.tensor_tensor(V.inv[:, 4 * g:4 * g + 4, :], four("ident"), rw_z4(V, g), ALU.subtract)\
                .then_inc(S["rw_inv"], 1)
        for g in range(4):
            dve.wait_ge(S["rw_inv_mm"], pe_step(n, "zt", 0, g))
            v.tensor_tensor(V.invt[:, 4 * g:4 * g + 4, :], four("ident"), bank(g), ALU.subtract)\
                .then_inc(S["rw_inv"], 1)
        for l in range(1, 6):
            for g in range(4):
                dve.wait_ge(S["rw_inv_mm"], pe_step(n, "z", l, g))
                v.tensor_tensor(rw_z4(V, g), bank(4 + g), four(f"level{LEVELS[l]}"), ALU.mult)\
                    .then_inc(S["rw_inv"], 1)
            for g in range(4):
                q4, x4 = V.inv[:, 4 * g:4 * g + 4, :], V.invt[:, 4 * g:4 * g + 4, :]
                dve.wait_ge(S["rw_inv_mm"], pe_step(n, "q", l, g))
                v.tensor_tensor(q4, q4, bank(g), ALU.subtract).then_inc(S["rw_inv"], 1)
                if l < 5:
                    dve.wait_ge(S["rw_inv_mm"], pe_step(n, "x", l, g))
                    v.tensor_tensor(x4, x4, bank(4 + g), ALU.subtract).then_inc(S["rw_inv"], 1)
        dve.wait_ge(S["rw_inv_mm"], pe_step(n, "q", 5, 3))
        for j, (mask, dst) in enumerate((("before", None), ("upto", None), ("upto", None))):
            for g in range(4):
                dve.wait_ge(S["rw_mat_mm"], 12 * n + 4 * j + g + 1)
                dst = (V.gk[:, 4 * g:4 * g + 4, :], V.rb[:, 4 * g:4 * g + 4, :], rw_z4(V, g))[j]
                v.tensor_tensor(dst, bank((4 + g) if j == 1 else g), four(mask), ALU.mult)\
                    .then_inc(S["rw_mat"], 1)
        for cc in range(2):
            ci = 2 * n + cc
            if ci < 3:
                dve.wait_ge(S["rw_s"], ci + 1)
                end = V.pend[:, :, ci:ci + 1].to_broadcast([P, 8, 64])
                ch.step(v.tensor_tensor(V.state, V.state, c.ps[:, 6, :].rearrange("p (b i) -> p b i", b=8),
                                        ALU.add))
                v.tensor_tensor(V.state, V.state, end, ALU.mult).then_inc(S["rw_state"], 1)
                dve.wait_ge(S["rw_state"], ci + 1)
            dve.wait_ge(S["rw_y_read"], ci + 1)
            for e in range(2):
                half = slice(64 * e, 64 * e + 64)
                y = W[7][half, :, ci * 64:ci * 64 + 64]
                v.tensor_tensor(y, y, c.ps[half, 7 - 2 * e, :].rearrange("p (b t) -> p b t", b=8), ALU.add)\
                    .then_inc(S["rw_y_add"], 1)
    dve.wait_ge(S["rw_mean"], 1)
    dve.wait_ge(S["rw_y_add"], 8)
    for g in range(4):
        y = W[7][:, 2 * g:2 * g + 2, :]
        v.tensor_tensor(y, y, c.ps[:, g, :].rearrange("p (m t) -> p m t", m=2), ALU.subtract)\
            .then_inc(S["rw_cen"], 1)
    dve.wait_ge(S["rw_cen_sq"], 1)
    for g in range(4):
        sl = (slice(None), slice(2 * g, 2 * g + 2), slice(None))
        dve.wait_ge(S["rw_gn_std"], g + 1)
        ch.step(v.reciprocal(W[2][sl], W[2][sl]))
        for b in (2 * g, 2 * g + 1):
            ch.step(v.scalar_tensor_tensor(out=W[7][:, b, :], in0=W[7][:, b, :], scalar=c.p("rwkv_ln_w_3", b),
                                           in1=W[2][:, b, :], op0=ALU.mult, op1=ALU.mult))
            ch.step(v.scalar_tensor_tensor(out=W[7][:, b, :], in0=W[7][:, b, :], scalar=c.p("rwkv_ln_b_3", b),
                                           in1=V.bonus[:, b, :], op0=ALU.add, op1=ALU.add))
        v.tensor_tensor(W[7][sl], W[7][sl], W[5][sl], ALU.mult).then_inc(S["rw_out"], 1)
    add_residual(c, dve, PLAN["rw_out"][0] + 3, 1.0, ch)


def b3_scalar(c, act):
    S = c.S
    mem_scalar(c, act)
    ffn3(c, "l0_ffn1", ("ffn1_norm_3", 0), 0)[0](act, (S["ln_out"], 16))
    rw_scalar(c, act, (S["h_ready"], HR3("l0_ffn1")))
    xattn_scalar(c, act, 0, (S["h_ready"], HR3("rw_out")))
    ffn3(c, "l0_ffn2", ("ffn2_norm_3", 0), 1)[0](act, (S["h_ready"], HR3("l0_xo")))
    ffn3(c, "l1_ffn1", ("ffn1_norm_3", 1), 2)[0](act, (S["h_ready"], HR3("l0_ffn2")))
    gmlp_scalar(c, act, (S["h_ready"], HR3("l1_ffn1")))
    xattn_scalar(c, act, 1, (S["h_ready"], HR3("gm_out")))
    ffn3(c, "l1_ffn2", ("ffn2_norm_3", 1), 3)[0](act, (S["h_ready"], HR3("l1_xo")))
    rms_scalar(c, act, NK["final"], ready=(S["h_ready"], HR3("l1_ffn2")))


def b3_tensor(c, pe):
    pe.wait_ge(c.S["late_loaded"], 16)
    mem_tensor(c, pe)
    ffn3(c, "l0_ffn1", ("ffn1_norm_3", 0), 0)[1](pe)
    rw_tensor(c, pe)
    xattn_tensor(c, pe, 0)
    ffn3(c, "l0_ffn2", ("ffn2_norm_3", 0), 1)[1](pe)
    ffn3(c, "l1_ffn1", ("ffn1_norm_3", 1), 2)[1](pe)
    gmlp_tensor(c, pe)
    xattn_tensor(c, pe, 1)
    ffn3(c, "l1_ffn2", ("ffn2_norm_3", 1), 3)[1](pe)
    rms_tensor(c, pe, NK["final"])


def b3_vector(c, dve, ch):
    dve.wait_ge(c.S["late_loaded"], 16)
    mem_vector(c, dve)
    ffn3(c, "l0_ffn1", ("ffn1_norm_3", 0), 0)[2](dve, ch)
    rw_vector(c, dve, ch)
    xattn_vector(c, dve, 0, ch)
    ffn3(c, "l0_ffn2", ("ffn2_norm_3", 0), 1)[2](dve, ch)
    ffn3(c, "l1_ffn1", ("ffn1_norm_3", 1), 2)[2](dve, ch)
    gmlp_vector(c, dve, ch)
    xattn_vector(c, dve, 1, ch)
    ffn3(c, "l1_ffn2", ("ffn2_norm_3", 1), 3)[2](dve, ch)
    rms_vector(c, dve, NK["final"], lambda b: ("final_norm_3", b), c.h)


def HR3(name):
    return HR[name]


STOP = 3


def skewed(flat, offset, n):
    return bass.AP(tensor=flat.tensor, offset=flat.offset + offset,
                   ap=[[383, P], [P * 384, 8], [1, n]])


def build(nc, x, params, consts, late_consts, stream, decay, gates, rel_bias, w_pool, bias_rows, mem, lora1,
          lora_wa, lora_g, spatial, spatial_b, out):
    with ExitStack() as ctx:
        c = Ctx(nc, ctx, None)
        S = c.S
        block = ctx.enter_context(nc.Block())

        @block.sync
        def _(sp):
            for s in range(UNITS):
                sp.dma_start(c.ring[:, s, :], stream[s]).then_inc(S[f"unit_loaded{s}"], 16)
            last = {1: PLAN["b2_q"][0], 2: PLAN["mem_k"][0], 3: PLAN["end"][0]}[STOP]
            with sp.Fori(1, -(-last // UNITS)) as r:
                for s in range(UNITS):
                    unit = sp.snap(r * UNITS + s)
                    sp.wait_ge(S[f"unit_done{s}"], r)
                    sp.dma_start(c.ring[:, s, :], stream[bass.ds(unit, 1)].rearrange("a p n -> (a p) n"))\
                        .then_inc(S[f"unit_loaded{s}"], 16)
            sp.wait_ge(*{1: (S["xn_ready"], 16), 2: (S["ln_out"], 16), 3: (S["xn_ready"], 8 * len(NORMS))}[STOP])
            sp.dma_start(out, c.h[:, :, :]).then_inc(S["out_stored"], 16)
            sp.wait_ge(S["out_stored"], 16)

        @block.scalar
        def _(act):
            act.dma_start(c.h[:, :, :], x).then_inc(S["x_loaded"], 16)
            act.dma_start(c.par[:, :], params).then_inc(S["par_loaded"], 16)
            act.dma_start(c.con[:, 0:consts.shape[1]], consts).then_inc(S["con_loaded"], 16)
            act.dma_start(c.table[:, :, :], decay).then_inc(S["decay_loaded"], 16)
            act.dma_start(c.gates[:, :, :, :], gates).then_inc(S["gates_loaded"], 16)
            act.wait_ge(S["b1_pad"], 1)
            b1_scalar(c, act)
            if STOP > 1:
                b2_scalar(c, act)
            if STOP > 2:
                b3_scalar(c, act)

        @block.tensor
        def _(pe):
            b1_tensor(c, pe)
            if STOP > 1:
                b2_tensor(c, pe)
            if STOP > 2:
                b3_tensor(c, pe)

        @block.vector
        def _(dve):
            ch = Chain(dve, S["vector_step"])
            b1_vector(c, dve, ch)
            if STOP > 1:
                b2_vector(c, dve, ch)
            if STOP > 2:
                b3_vector(c, dve, ch)

        @block.gpsimd
        def _(pool):
            pool.dma_start(c.relb[0:32, :], rel_bias).then_inc(S["relb_loaded"], 16)
            pool.dma_start(c.wpool[:, :, :], w_pool).then_inc(S["wpool_loaded"], 16)
            if STOP > 1:
                pool.wait_ge(S["b2_bias_read"], 1)
                pool.dma_start(bias_rows.rearrange("h p y -> h p y"),
                               c.relg[0:8, :].rearrange("h (a y) -> h a y", a=1).to_broadcast([8, P, 384]))\
                    .then_inc(S["bias_stored"], 16)
                pool.wait_ge(S["bias_stored"], 16)
                pool.wait_ge(S["b1_prob"], 8)
                flat = bias_rows.rearrange("h p y -> (h p y)")
                pool.dma_start(c.table[:, :, P:384], skewed(flat, 127, T)).then_inc(S["bias_loaded"], 16)
                pool.dma_start(c.table[:, :, 0:P], skewed(flat, 127 + P, P)).then_inc(S["bias_loaded"], 16)
            if STOP > 2:
                pool.wait_ge(S["b2_bias_read"], 1)
                pool.wait_ge(S["b2_pooled"], 1)
                pool.dma_start(c.con[:, N_COMMON:N_COMMON + N_LATE], late_consts).then_inc(S["late_loaded"], 16)
                pool.wait_ge(S["b2_scores"], 8)
                pool.dma_start(c.work[0][:, :, :], mem).then_inc(S["mem_loaded"], 16)
                V = rw_views(c)
                pool.wait_ge(S["h_ready"], HR["l0_ffn1"])
                pool.dma_start(V.lora1, lora1).then_inc(S["lora_loaded"], 16)
                pool.dma_start(V.lora_wa, lora_wa).then_inc(S["lora_loaded"], 16)
                pool.dma_start(V.lora_g, lora_g[0:P, :]).then_inc(S["lora_loaded"], 16)
                pool.dma_start(V.lora_gt, lora_g[P:160, :]).then_inc(S["lora_loaded"], 16)
                pool.wait_ge(S["h_ready"], HR["l0_xo"])
                pool.dma_start(c.work[2][:, :, :], spatial).then_inc(S["gm_loaded"], 16)
                pool.dma_start(c.work[3][:, :, :].rearrange("p a b -> p (a b)"),
                               spatial_b.rearrange("(a n) -> a n", a=1).to_broadcast([P, 2048]))\
                    .then_inc(S["gm_loaded"], 16)


def feature_major(a):
    a = np.asarray(a).reshape(-1, np.asarray(a).shape[-1] // P, P)
    return np.ascontiguousarray(a.transpose(2, 0, 1))


def p_units(w):
    n = w.shape[1] // 256
    return [u for u in w.reshape(KB, P, n, 256).transpose(2, 1, 0, 3).reshape(n, P, UNIT)]


def d_units(w):
    n = w.shape[0] // 256
    return [u for u in w.reshape(n, 2, P, C).transpose(0, 2, 1, 3).reshape(n, P, UNIT)]


def ffn_units(w_in, w_out, gate_first=True):
    g, u, d = p_units(w_in[:, :FF]), p_units(w_in[:, FF:]), d_units(w_out)
    if not gate_first:
        g, u = u, g
    out = [g[0], u[0], g[1], u[1], d[0]]
    for j in range((FFI - 3) // 2):
        i = 2 * j + 2
        out += [g[i], u[i], d[i - 1], g[i + 1], u[i + 1], d[i]]
    return out + [g[FFI - 1], u[FFI - 1], d[FFI - 2], d[FFI - 1]]


def kernel(**inputs):
    import concourse.bacc as bacc
    from concourse.bass_utils import run_bass_kernel_spmd as run

    a = {k: np.asarray(v) for k, v in inputs.items()}
    w1 = a["w_in"]
    cut = [w1[:, i * C:(i + 1) * C] for i in range(6)]
    units = []
    for i in (4, 0, 1, 2, 3, 5):
        units += p_units(cut[i])
    units += d_units(a["w_out"])
    w2 = a["w_in_2"][0]
    units += p_units(w2) + d_units(a["w_out_2"][0])
    units += ffn_units(a["w_up_2"][0], a["w_down_2"][0], False)
    units += p_units(a["mem_w_kv_3"])
    for i in range(2):
        units += ffn_units(a["ffn1_w_in_3"][i], a["ffn1_w_out_3"][i])
        if i == 0:
            units += p_units(a["rwkv_w_rkv_3"][0]) + d_units(a["rwkv_w_o_3"][0])
        else:
            uv = a["gmlp_w_uv_3"][0]
            units += p_units(uv[:, 2 * C:]) + p_units(uv[:, :2 * C]) + d_units(a["gmlp_w_o_3"][0])
        units += p_units(a["xattn_wq_3"][i]) + d_units(a["xattn_wo_3"][i])
        units += ffn_units(a["ffn2_w_in_3"][i], a["ffn2_w_out_3"][i])
    while len(units) < N_UNITS:
        units.append(np.zeros((P, UNIT), np.float32))
    arrays = {"stream": np.stack(units)}
    cols = []
    for name, width in PARAMS:
        v = a[name].reshape(-1, P)
        assert v.shape[0] == width, name
        cols.append(v.T)
    arrays["params"] = np.ascontiguousarray(np.concatenate(cols, 1))
    arrays["consts"] = np.concatenate([CONSTS[n] for n in COMMON + EARLY], 1)
    arrays["late_consts"] = np.concatenate([CONSTS[n] for n in LATE], 1)
    arrays["decay"] = DECAY.reshape(P, 8, 384)
    arrays["x"] = np.ascontiguousarray(a["x"][0].T.reshape(KB, P, T).transpose(1, 0, 2))
    arrays["gates"] = np.ascontiguousarray(
        np.stack([a["gate_a_w"], a["gate_x_w"]]).transpose(2, 0, 1, 3))
    arrays["rel_bias"] = np.ascontiguousarray(a["rel_bias_2"].T)
    pool = np.zeros((P, 2, P), np.float32)
    for g in range(4):
        e = 64 * (g % 2)
        pool[e:e + 64, g // 2, e:e + 64] = a["w_pool_2"][0, g]
    arrays["w_pool"] = pool
    arrays["mem"] = np.ascontiguousarray(a["mem_3"][0].T.reshape(KB, P, T).transpose(1, 0, 2))
    lora = np.concatenate([a["rwkv_w1_3"][0], a["rwkv_a1_3"][0], a["rwkv_g1_3"][0]], 1)
    arrays["lora1"] = np.ascontiguousarray(lora.reshape(KB, P, -1).transpose(1, 0, 2))
    arrays["lora_wa"] = np.concatenate([a["rwkv_w2_3"][0], a["rwkv_a2_3"][0]], 0)
    arrays["lora_g"] = np.ascontiguousarray(a["rwkv_g2_3"][0])
    arrays["spatial"] = np.ascontiguousarray(a["gmlp_w_s_3"][0].transpose(2, 0, 1)).reshape(P, KB, T)
    arrays["spatial_b"] = a["gmlp_b_s_3"].reshape(-1)
    nc = bacc.Bacc("TRN2", target_bir_lowering=False, num_devices=1)
    args = {n: nc.dram_tensor(n, v.shape, F32, kind="ExternalInput").ap() for n, v in arrays.items()}
    args["bias_rows"] = nc.dram_tensor("bias_rows", (8, P, 384), F32, kind="Internal").ap()
    args["out"] = nc.dram_tensor("out", (P, KB, T), F32, kind="ExternalOutput").ap()
    build(nc, **args)
    r = run(nc, [arrays], core_ids=[0])
    o = np.asarray(r.results[0]["out"])
    return np.ascontiguousarray(o.transpose(1, 0, 2).reshape(C, T).T)[None]
```

```python
import math
from contextlib import ExitStack

import numpy as np
import concourse.bass as bass
from concourse import mybir

F32 = mybir.dt.float32
ALU = mybir.AluOpType
ACT = mybir.ActivationFunctionType
AX = mybir.AxisListType

P = 128
T = 256
C = 1024
KB = C // P
UNITS = 6
UNIT = 2048
BANKS = 4
FF = 2816
FFI = FF // 256
EPS = 1e-6


def plan():
    ffn = ("ffn", 2 * FFI, FFI)
    stages = [("b1_xlru", 4, 0), ("b1_q", 4, 0), ("b1_k", 4, 0), ("b1_v", 4, 0), ("b1_gret", 4, 0),
              ("b1_glru", 4, 0), ("b1_out", 0, 8),
              ("b2_q", 2, 0), ("b2_k", 2, 0), ("b2_v", 2, 0), ("b2_pin", 1, 0), ("b2_cc", 1, 0),
              ("b2_cx", 1, 0), ("b2_cb", 1, 0), ("b2_out", 0, 4), ("mem_k", 4, 0),
              ("b2_ffn",) + ffn[1:], ("mem_v", 4, 0), ("l0_ffn1",) + ffn[1:],
              ("rw_r", 4, 0), ("rw_k", 4, 0), ("rw_v", 4, 0), ("rw_out", 0, 4),
              ("l0_xq", 4, 0), ("l0_xo", 0, 4), ("l0_ffn2",) + ffn[1:],
              ("l1_ffn1",) + ffn[1:], ("gm_u", 8, 0), ("gm_v", 8, 0), ("gm_out", 0, 8),
              ("l1_xq", 4, 0), ("l1_xo", 0, 4), ("l1_ffn2",) + ffn[1:]]
    unit, bank, out = 0, 0, {}
    for name, np_, nd in stages:
        out[name] = (unit, bank)
        unit, bank = unit + np_ + nd, bank + np_
    out["end"] = (unit, bank)
    return out


PLAN = plan()
N_UNITS = -(-PLAN["end"][0] // UNITS) * UNITS


PARAMS = [("norm_in_g", 8), ("conv_w", 32), ("conv_b", 8), ("gate_a_b", 8), ("gate_x_b", 8),
          ("lru_lambda", 8), ("norm_out_g", 8),
          ("conv_w_2", 6), ("pool_scale_2", 2), ("ln1_g_2", 8), ("ln1_b_2", 8), ("ffn_conv_w_2", 132),
          ("ffn_conv_b_2", 44), ("ln2_g_2", 8), ("ln2_b_2", 8),
          ("mem_norm_3", 8), ("ffn1_norm_3", 16), ("mix_norm_3", 16), ("xattn_norm_3", 16),
          ("ffn2_norm_3", 16), ("rwkv_mu_3", 48), ("rwkv_w0_3", 8), ("rwkv_a0_3", 8), ("rwkv_k_k_3", 8),
          ("rwkv_k_a_3", 8), ("rwkv_r_k_3", 8), ("rwkv_ln_w_3", 8), ("rwkv_ln_b_3", 8),
          ("gmlp_v_norm_3", 16), ("final_norm_3", 8)]
PCOL, _n = {}, 0
for _name, _w in PARAMS:
    PCOL[_name] = _n
    _n += _w
N_PARAMS = _n


def constants():
    f = np.float32
    i = np.arange(P)
    out = {}
    out["ident"] = np.eye(P, dtype=f)
    out["mean_c"] = np.full((P, P), 1.0 / C, f)
    out["mean_p"] = np.full((P, P), 1.0 / P, f)
    half = (i[:, None] // 64 == i[None, :] // 64)
    out["sum_h"] = half.astype(f)
    out["mean_h"] = (half / 64.0).astype(f)
    rot = np.zeros((P, P), f)
    for d in range(64):
        rot[d + 64, d] = -1.0
        rot[d, d + 64] = 1.0
    out["rot"] = rot
    inv = (f(10000.0) ** (-np.arange(0, P, 2, dtype=f) / f(P))).astype(f)
    ang = np.arange(T, dtype=f)[None, :] * inv[:, None]
    ang = np.concatenate([ang, ang], 0)
    out["cos"] = np.tile(np.cos(ang).astype(f), (1, 2))
    out["sin"] = np.tile(np.sin(ang).astype(f), (1, 2))
    logg = np.log1p(-np.exp2(-5.0 - np.arange(8)))
    rel = np.arange(T)[None, :] - i[:, None]
    dec = np.where(rel[None] >= 0, np.exp(np.maximum(rel, 0)[None] * logg[:, None, None]), 0.0) * P ** -0.5
    dec = np.concatenate([dec, dec[:, :, :P]], 2)
    out["decay"] = dec.transpose(1, 0, 2).reshape(P, -1).astype(f)
    pos = np.arange(1, T + 1)
    win = np.repeat(np.array([2, 4, 8, 16]), 64).reshape(2, P)
    out["pool_inv"] = (1.0 / np.minimum(pos, win[:, :, None])).transpose(1, 0, 2).reshape(P, -1).astype(f)
    n = np.maximum(255 - np.arange(384), 0)
    nf = np.maximum(n, 1).astype(f)
    large = 16 + (np.log(nf / f(16)) / f(math.log(64.0)) * f(16)).astype(np.int32)
    bucket = np.where(n < 16, n, np.minimum(large, 31))
    hot = np.zeros((P, 384), f)
    hot[bucket[:256], np.arange(256)] = 1.0
    out["bucket_hot"] = hot
    out["future"] = np.tile(np.where(np.arange(384) > 255, f(-1e30), f(0)).astype(f), (P, 1))
    s_, t_ = i[:, None], i[None, :]
    same = s_ // CHUNK == t_ // CHUNK
    out["before"] = (same & (s_ < t_)).astype(f)
    out["upto"] = (same & (s_ <= t_)).astype(f)
    for m in LEVELS:
        out[f"level{m}"] = ((s_ // (2 * m) == t_ // (2 * m)) & (s_ % (2 * m) < m) & (t_ % (2 * m) >= m)).astype(f)
    reset = np.ones((P, T), f)
    reset[:, ::CHUNK] = 0.0
    out["reset"] = reset
    out["causal"] = (s_ <= t_).astype(f)
    return out


CHUNK = 64
LEVELS = (1, 2, 4, 8, 16, 32)
CONSTS = constants()
DECAY = CONSTS.pop("decay")
COMMON = ("ident", "mean_c")
EARLY = ("mean_p", "rot", "cos", "sin", "pool_inv", "bucket_hot", "future")
LATE = tuple(n for n in CONSTS if n not in COMMON + EARLY)
CCOL, N_COMMON = {}, 0
for _name in COMMON:
    CCOL[_name] = (N_COMMON, N_COMMON + CONSTS[_name].shape[1])
    N_COMMON += CONSTS[_name].shape[1]
N_CONSTS = 0
for _set in (EARLY, LATE):
    _n = N_COMMON
    for _name in _set:
        CCOL[_name] = (_n, _n + CONSTS[_name].shape[1])
        _n += CONSTS[_name].shape[1]
    N_CONSTS = max(N_CONSTS, _n)
N_LATE = _n - N_COMMON


class Sems(dict):

    def __init__(self, nc, ctx):
        self.nc, self.ctx = nc, ctx

    def __missing__(self, name):
        self[name] = self.ctx.enter_context(self.nc.semaphore(name))
        return self[name]


class Chain:

    def __init__(self, eng, sem):
        self.eng, self.sem, self.n = eng, sem, 0

    def step(self, ins):
        self.n += 1
        ins.then_inc(self.sem, 1)
        self.eng.wait_ge(self.sem, self.n)


class Ctx:

    def __init__(self, nc, ctx, io):
        self.nc, self.io = nc, io
        self.S = Sems(nc, ctx)

        def sb(name, shape):
            return ctx.enter_context(nc.sbuf_tensor("sb_" + name, shape, F32))

        self.ring = sb("ring", [P, UNITS, UNIT])
        self.par = sb("par", [P, N_PARAMS])
        self.con = sb("con", [P, N_CONSTS])
        self.h = sb("h", [P, KB, T])
        self.xn = sb("xn", [P, KB, T])
        self.sq = sb("sq", [P, KB, T])
        self.rstd = sb("rstd", [P, 512])
        self.std = sb("std", [P, 512])
        self.eps = sb("eps", [P, 4])
        self.th = sb("th", [P, 2, 512])
        self.t1 = sb("t1", [P, 2, 512])
        self.hid = sb("hid", [P, 2, 512])
        self.work = [sb(f"work{i}", [P, KB, T]) for i in range(NWORK)]
        self.small = sb("small", [P, 256])
        self.xg = self.work[6]
        self.gates = self.work[9][:, :, :].rearrange("p a b -> p (a b)")\
            .rearrange("p (g n o) -> p g n o", g=2, n=8)
        self.pad = sb("pad", [P, KB, T + 4])
        self.relb = sb("relb", [P, 8])
        self.relg = sb("relg", [8, 384])
        self.table = sb("table", [P, 8, 384])
        self.wpool = sb("wpool", [P, 2, P])
        self.ps = ctx.enter_context(nc.psum_tensor("ps", [P, 8, 512], F32))

    def p(self, name, j=0, n=1):
        return self.par[:, PCOL[name] + j:PCOL[name] + j + n]

    def c(self, name):
        a, b = CCOL[name]
        return self.con[:, a:b]

    def wait_loaded(self, eng, n, j=None):
        v = 16 * (n // UNITS + 1)
        eng.wait_ge(self.S[f"unit_loaded{n % UNITS}"], v if j is None else j * 16 + v)

    def wait_done(self, eng, n, j=None):
        v = n // UNITS + 1
        eng.wait_ge(self.S[f"unit_done{n % UNITS}"], v if j is None else j + v)

    def wait_read(self, eng, q, j=None):
        v = q // BANKS + 1
        eng.wait_ge(self.S[f"bank_read{q % BANKS}"], v if j is None else j + v)

    def bank(self, q):
        return self.ps[:, q % BANKS, :]

    def read(self, ins, q):
        ins.then_inc(self.S[f"bank_read{q % BANKS}"], 1)


NWORK = 10


def p_unit(c, pe, n, q, x, j=None, token_major=False):
    c.wait_loaded(pe, n, j)
    if q >= BANKS:
        c.wait_read(pe, q - BANKS, j)
    w = c.ring[:, n % UNITS, :].rearrange("p (k n) -> p k n", k=KB)
    out = c.bank(q).rearrange("p (m t) -> p m t", m=2)
    for m in range(2):
        for k in range(KB):
            if token_major:
                mm = c.nc.tensor.matmul(out[:, m, :], x[:, k, m * P:m * P + P], w[:, k, :],
                                        start=k == 0, stop=k == KB - 1)
            else:
                mm = c.nc.tensor.matmul(out[:, m, :], w[:, k, m * P:m * P + P], x[:, k, :],
                                        start=k == 0, stop=k == KB - 1)
    mm.then_inc(c.S[f"unit_done{n % UNITS}"], 1)


def first_unit(c, pe, n, q, x, sem, v):
    c.wait_loaded(pe, n)
    if q >= BANKS:
        c.wait_read(pe, q - BANKS)
    w = c.ring[:, n % UNITS, :].rearrange("p (k n) -> p k n", k=KB)
    for k in range(KB):
        pe.wait_ge(sem, v + k + 1)
        for m in range(2):
            mm = c.nc.tensor.matmul(c.bank(q)[:, m * T:m * T + T], w[:, k, m * P:m * P + P], x[:, k, :],
                                    start=k == 0 and m == 0, stop=k == KB - 1, skip_group_check=True)
    mm.then_inc(c.S[f"unit_done{n % UNITS}"], 1)


def norm_units(c, pe, name, k):
    n0, q0 = PLAN[name]
    first_unit(c, pe, n0, q0, c.xg, c.S["xg_ready"], 8 * GAINED.index(k))
    rms_tensor(c, pe, NK[k])
    p_unit(c, pe, n0 + 1, q0 + 1, c.xg)
    pe.wait_ge(c.S["xn_ready"], 8 * NK[k] + 8)


def d_unit(c, pe, n, x2, first, last, j=None):
    c.wait_loaded(pe, n, j)
    w = c.ring[:, n % UNITS, :].rearrange("p (k n) -> p k n", k=2)
    for m in range(KB):
        for k in range(2):
            mm = c.nc.tensor.matmul(c.ps[:, 4 + m // 2, (m % 2) * T:(m % 2) * T + T],
                                    w[:, k, m * P:m * P + P], x2(k),
                                    start=first and k == 0 and m % 2 == 0, stop=last and k == 1,
                                    skip_group_check=True)
        if last and m in (1, 3, 5):
            mm.then_inc(c.S["bank_complete"], 1)
    mm.then_inc(c.S[f"unit_done{n % UNITS}"], 1)


def rms_scalar(c, act, k, r):
    for b in range(4):
        act.wait_ge(c.S["h_ready"], 4 * r + b + 1)
        squares(c, k, b, c.h)
    rms_root(c, act, k)


def squares(c, k, b, src):
    c.nc.scalar.activation(c.sq[:, 2 * b:2 * b + 2, :], src[:, 2 * b:2 * b + 2, :], ACT.Square)\
        .then_inc(c.S["sq_ready"], 1)


def rms_root(c, act, k):
    act.wait_ge(c.S["mean_sq_ready"], k + 1)
    c.nc.scalar.activation(c.std[:, 0:T], c.ps[:, 4, 0:T], ACT.Sqrt, bias=c.eps[:, 0:1])\
        .then_inc(c.S["std_ready"], 1)


def rms_tensor(c, pe, k):
    for b in range(KB):
        if b % 2 == 0:
            pe.wait_ge(c.S["sq_ready"], 4 * k + b // 2 + 1)
        mm = c.nc.tensor.matmul(c.ps[:, 4, 0:T], c.c("mean_c"), c.sq[:, b, :], start=b == 0, stop=b == KB - 1)
    mm.then_inc(c.S["mean_sq_ready"], 1)


def gain_blocks(c, b, gain, src):
    for m in (2 * b, 2 * b + 1):
        c.nc.vector.tensor_scalar(c.xg[:, m, :], src[:, m, :], c.p(*gain(m)), None, ALU.mult)\
            .then_inc(c.S["xg_ready"], 1)


def rms_recip(c, dve, k):
    dve.wait_ge(c.S["std_ready"], k + 1)
    c.nc.vector.reciprocal(c.rstd[:, 0:T], c.std[:, 0:T]).then_inc(c.S["rstd_ready"], 1)
    dve.wait_ge(c.S["rstd_ready"], k + 1)


def rms_vector(c, dve, name, out):
    rms_recip(c, dve, NK[name])
    dve.wait_ge(c.S["xg_ready"], 8 * GAINED.index(name) + 8)
    for b in range(KB):
        c.nc.vector.tensor_tensor(out[:, b, :], c.xg[:, b, :], c.rstd[:, 0:T], ALU.mult)\
            .then_inc(c.S["xn_ready"], 1)


def rms_vector_gain(c, dve, k, gain, out, src):
    rms_recip(c, dve, k)
    for b in range(KB):
        c.nc.vector.scalar_tensor_tensor(out=out[:, b, :], in0=src[:, b, :], scalar=c.p(*gain(b)),
                                         in1=c.rstd[:, 0:T], op0=ALU.mult, op1=ALU.mult)\
            .then_inc(c.S["xn_ready"], 1)


def rescaled(c, dve, name, u, out):
    n0, q0 = PLAN[name]
    c.wait_done(dve, n0 + u)
    rstd = c.rstd[:, 0:T].rearrange("p (a t) -> p a t", a=1).to_broadcast([P, 2, T])
    c.read(c.nc.vector.tensor_tensor(out, c.bank(q0 + u).rearrange("p (m t) -> p m t", m=2), rstd, ALU.mult),
           q0 + u)


def wait_bank(c, dve, name, n, b):
    if b < 3:
        dve.wait_ge(c.S["bank_complete"], 3 * DPROJ.index(name) + b + 1)
    else:
        c.wait_done(dve, n)


def add_residual(c, dve, name, n, scale, gain=None):
    r = RESID.index(name)
    for b in range(4):
        wait_bank(c, dve, name, n, b)
        c.nc.vector.scalar_tensor_tensor(
            out=c.h[:, 2 * b:2 * b + 2, :], in0=c.ps[:, 4 + b, :].rearrange("p (m t) -> p m t", m=2),
            scalar=scale, in1=c.h[:, 2 * b:2 * b + 2, :], op0=ALU.mult, op1=ALU.add)\
            .then_inc(c.S["h_ready"], 1)
        dve.wait_ge(c.S["h_ready"], 4 * r + b + 1)
        if gain:
            gain_blocks(c, b, gain, c.h)


def gu_unit(n0, i):
    if i < 2:
        return n0 + 2 * i
    return n0 + 5 + 6 * ((i - 2) // 2) + 3 * (i % 2)


def d_unit_of(n0, i):
    if i == 0:
        return n0 + 4
    if i == FFI - 1:
        return n0 + 3 * FFI - 1
    return n0 + 7 + 6 * ((i - 1) // 2) + 3 * ((i - 1) % 2)


def ffn_tensor(c, pe, name, x, norm=None):
    n0, q0 = PLAN[name]

    def gu(i, j=None):
        n = gu_unit(n0, i)
        p_unit(c, pe, n, q0 + 2 * i, x, j)
        p_unit(c, pe, n + 1, q0 + 2 * i + 1, x, j)

    def d(i, j=None):
        c.wait_read(pe, q0 + 2 * i + 1, j)
        x = c.hid[:, i % 2, :].rearrange("p (m t) -> p m t", m=2)
        d_unit(c, pe, d_unit_of(n0, i), lambda k: x[:, k, :], i == 0, i == FFI - 1, j)

    if norm:
        norm_units(c, pe, name, norm)
    else:
        gu(0)
    gu(1)
    d(0)
    with pe.Fori(0, (FFI - 3) // 2) as j:
        gu(2, j)
        d(1, j)
        gu(3, j)
        d(2, j)
    gu(FFI - 1)
    d(FFI - 2)
    d(FFI - 1)


def ffn_loop(eng, body):
    body(0, None)
    body(1, None)
    with eng.Fori(0, (FFI - 3) // 2) as j:
        body(2, j)
        body(3, j)
    body(FFI - 1, None)


def swiglu_scalar(c, act, name, f):
    n0, q0 = PLAN[name]

    def body(i, j):
        if i == 0:
            c.wait_read(act, q0)
            src = c.t1[:, 0, :]
        else:
            c.wait_done(act, gu_unit(n0, i), j)
            src = c.bank(q0 + 2 * i)
        if i >= 2:
            c.wait_read(act, q0 + 2 * (i - 2) + 1, j)
        c.nc.scalar.activation(c.th[:, i % 2, :], src, ACT.Tanh, scale=0.5)\
            .then_inc(c.S[f"tanh_ready{i % 2}"], 1)
    ffn_loop(act, body)


def tanh_count(f, i):
    return f * ((FFI + 1) // 2 if i % 2 == 0 else FFI // 2) + i // 2 + 1


def swiglu_vector(c, dve, name, f, ch):
    n0, q0 = PLAN[name]

    def first(v):
        rescaled(c, dve, name, 0, c.t1[:, 0, :].rearrange("p (m t) -> p m t", m=2))
        c.wait_done(dve, n0 + 1)
        rstd = c.rstd[:, 0:T].rearrange("p (a t) -> p a t", a=1).to_broadcast([P, 2, T])
        ch.step(c.nc.vector.tensor_tensor(c.hid[:, 0, :].rearrange("p (m t) -> p m t", m=2),
                                          c.bank(q0 + 1).rearrange("p (m t) -> p m t", m=2), rstd, ALU.mult))
        dve.wait_ge(c.S["tanh_ready0"], v)
        ch.step(c.nc.vector.scalar_tensor_tensor(out=c.t1[:, 0, :], in0=c.th[:, 0, :], scalar=1.0,
                                                 in1=c.t1[:, 0, :], op0=ALU.add, op1=ALU.mult))
        c.read(c.nc.vector.scalar_tensor_tensor(out=c.hid[:, 0, :], in0=c.t1[:, 0, :], scalar=0.5,
                                                in1=c.hid[:, 0, :], op0=ALU.mult, op1=ALU.mult), q0 + 1)

    def body(i, j):
        v = tanh_count(f, i)
        if i == 0:
            first(v)
            return
        dve.wait_ge(c.S[f"tanh_ready{i % 2}"], v if j is None else j + v)
        c.read(c.nc.vector.scalar_tensor_tensor(
            out=c.t1[:, i % 2, :], in0=c.th[:, i % 2, :], scalar=1.0, in1=c.bank(q0 + 2 * i),
            op0=ALU.add, op1=ALU.mult), q0 + 2 * i)
        c.wait_done(dve, gu_unit(n0, i) + 1, j)
        if i >= 2:
            c.wait_done(dve, d_unit_of(n0, i - 2), j)
        c.wait_read(dve, q0 + 2 * i, j)
        c.read(c.nc.vector.scalar_tensor_tensor(
            out=c.hid[:, i % 2, :], in0=c.t1[:, i % 2, :], scalar=0.5, in1=c.bank(q0 + 2 * i + 1),
            op0=ALU.mult, op1=ALU.mult), q0 + 2 * i + 1)
    ffn_loop(dve, body)


NORMS = ["b1_in", "b1_out", "mem", "l0_ffn1", "l0_mix", "l0_x", "l0_ffn2",
         "l1_ffn1", "l1_mix", "l1_x", "l1_ffn2", "final"]
NK = {name: i for i, name in enumerate(NORMS)}
GAINED = [n for n in NORMS if n not in ("mem", "final")]
RESID = ["b1_out", "l0_ffn1", "rw_out", "l0_xo", "l0_ffn2",
         "l1_ffn1", "gm_out", "l1_xo", "l1_ffn2"]
HR = {name: 4 * i + 4 for i, name in enumerate(RESID)}
DPROJ = ["b1_out", "b2_out", "b2_ffn"] + RESID[1:]


def b1_scalar(c, act):
    S, nc, W = c.S, c.nc, c.work
    act.wait_ge(S["x_loaded"], 16)
    for b in range(4):
        squares(c, NK["b1_in"], b, c.h)
    rms_root(c, act, NK["b1_in"])
    n0, q0 = PLAN["b1_xlru"]
    act.wait_ge(S["b1_pad"], 1)
    for u in range(2, 4):
        c.wait_done(act, n0 + u)
        c.read(nc.scalar.activation(c.pad[:, 2 * u:2 * u + 2, 3:3 + T],
                                    c.bank(q0 + u).rearrange("p (m t) -> p m t", m=2), ACT.Copy), q0 + u)
    act.wait_ge(S["b1_abs"], 1)
    nc.scalar.activation(c.small[:, 8:16], c.small[:, 0:8], ACT.Exp, scale=-1.0).then_inc(S["b1_exp"], 1)
    def lru_gates(n):
        tmp = c.sq if n % 2 == 0 else W[8]
        act.wait_ge(S["b1_gate_mm"], n + 1)
        if n >= 2:
            act.wait_ge(S["b1_gate_used"], n - 1)
        bank = c.ps[:, 6 + n % 2, :]
        nc.scalar.activation(tmp[:, 0, :], bank[:, 0:T], ACT.Tanh, scale=0.5,
                             bias=c.small[:, 64 + n:65 + n]).then_inc(S["b1_gate_r"], 1)
        nc.scalar.activation(tmp[:, 1, :], bank[:, T:2 * T], ACT.Tanh, scale=0.5,
                             bias=c.small[:, 72 + n:73 + n]).then_inc(S["b1_gate_i"], 1)
        act.wait_ge(S["b1_gate_r"], n + 1)
        for s, (col, f) in enumerate(((80, ACT.Exp), (88, ACT.Tanh), (80, ACT.Tanh), (96, ACT.Exp))):
            nc.scalar.activation(tmp[:, 2 + s, :], tmp[:, 0, :], f, scale=c.small[:, col + n:col + n + 1],
                                 bias=c.small[:, col + n:col + n + 1]).then_inc(S["b1_gate_ready"], 1)

    n0, q0 = PLAN["b1_q"]
    for u in range(8):
        c.wait_done(act, n0 + u)
        if u >= 2:
            act.wait_ge(S["b1_rotated"], u - 1)
        c.read(nc.scalar.activation(c.hid[:, u % 2, :], c.bank(q0 + u), ACT.Copy), q0 + u)
        if u >= 5:
            lru_gates(u - 5)
    n0, q0 = PLAN["b1_v"]
    v = W[2][:, :, :].rearrange("p a b -> p (a b)").rearrange("p (m n) -> p m n", m=2)
    for u in range(4):
        c.wait_done(act, n0 + u)
        c.read(nc.scalar.activation(v[:, :, u * 256:u * 256 + 256],
                                    c.bank(q0 + u).rearrange("p (m n) -> p m n", m=2), ACT.Copy), q0 + u)
        lru_gates(u + 3)
    lru_gates(7)
    ng, qg = PLAN["b1_gret"]

    def gate(u):
        c.wait_done(act, ng + u)
        if u >= 2:
            c.wait_read(act, qg + u - 2)
        nc.scalar.activation(c.th[:, u % 2, :], c.bank(qg + u), ACT.Tanh, scale=0.5)\
            .then_inc(S["b1_gate_tanh"], 1)

    act.wait_ge(S["b1_m_ready"], 8)
    nc.scalar.activation(W[7][:, :, :], W[7][:, :, :], ACT.Sqrt).then_inc(S["b1_mult"], 1)
    for p in range(5):
        gate(2 * p if p < 4 else 7)
        if p > 0:
            act.wait_ge(S["b1_var"], p)
            nc.scalar.activation(W[9][:, 2 * p - 2:2 * p, :],
                                 c.ps[:, 6, :].rearrange("p (m t) -> p m t", m=2), ACT.Sqrt,
                                 bias=c.eps[:, 0:1]).then_inc(S["b1_var_read"], 1)
        if p < 3:
            gate(2 * p + 1)
        if p < 4:
            act.wait_ge(S["b1_o"], p + 1)
            nc.scalar.activation(c.t1[:, 0, :], c.ps[:, 6, :], ACT.Copy).then_inc(S["b1_o_read"], 1)
            act.wait_ge(S["b1_cen"], p + 1)
            nc.scalar.activation(c.t1[:, 1, :], W[0][:, 2 * p:2 * p + 2, :].rearrange("p a b -> p (a b)"),
                                 ACT.Square).then_inc(S["b1_cen_sq"], 1)
    rms_scalar(c, act, NK["b1_out"], 0)


def b1_tensor(c, pe):
    S, nc, W = c.S, c.nc, c.work
    pe.wait_ge(S["common_loaded"], 16)
    norm_units(c, pe, "b1_xlru", "b1_in")
    for u in range(2, 4):
        n0, q0 = PLAN["b1_xlru"]
        p_unit(c, pe, n0 + u, q0 + u, c.xn)
    n0, q0 = PLAN["b1_q"]
    pe.wait_ge(S["con_loaded"], 16)

    def rotate(u):
        c.wait_read(pe, q0 + u)
        if u >= 2:
            pe.wait_ge(S["b1_rot_read"], u - 1)
        nc.tensor.matmul(c.ps[:, 4 + u % 2, :], c.c("rot"), c.hid[:, u % 2, :], start=True, stop=True)\
            .then_inc(S["b1_rot_mm"], 1)

    def lru_gates(n):
        if n == 0:
            pe.wait_ge(S["gates_loaded"], 16)
        pe.wait_ge(S["b1_conv"], n + 1)
        if n >= 2:
            pe.wait_ge(S["b1_gate_i"], n - 1)
        for g in range(2):
            mm = nc.tensor.matmul(c.ps[:, 6 + n % 2, g * T:g * T + T], c.gates[:, g, n, :], W[5][:, n, :],
                                  start=True, stop=True)
        mm.then_inc(S["b1_gate_mm"], 1)

    for u in range(8):
        p_unit(c, pe, n0 + u, q0 + u, c.xn)
        if u > 0:
            rotate(u - 1)
        if u >= 5:
            lru_gates(u - 5)
    n0, q1 = PLAN["b1_v"]
    for u in range(4):
        p_unit(c, pe, n0 + u, q1 + u, c.xn, token_major=True)
        if u == 0:
            rotate(7)
        lru_gates(u + 3)
    lru_gates(7)
    ng, qg = PLAN["b1_gret"]
    v = W[2][:, :, :].rearrange("p a b -> p (a b)").rearrange("p (m n) -> p m n", m=2)
    prob = c.hid[:, :, :].rearrange("p a b -> p (a b)").rearrange("p (a b) -> p a b", a=2)
    pe.wait_ge(S["b1_rotated"], 8)
    pe.wait_ge(S["b1_gate_i"], 8)
    for p in range(5):
        if p < 4:
            if p > 0:
                pe.wait_ge(S["b1_prob"], 2 * p)
            for e in range(2):
                hd = 2 * p + e
                nc.tensor.matmul(c.ps[:, 4 + e, 0:T], W[1][:, hd, 0:P], W[0][:, hd, :], start=True, stop=True)
                nc.tensor.matmul(c.ps[:, 4 + e, T:T + P], W[1][:, hd, P:T], W[0][:, hd, P:T],
                                 start=True, stop=True).then_inc(S["b1_scores"], 1)
        u = 2 * p if p < 4 else 7
        p_unit(c, pe, ng + u, qg + u, c.xn)
        if p > 0:
            pe.wait_ge(S["b1_cen_sq"], p)
            nc.tensor.matmul(c.ps[:, 6, :], c.c("mean_p"), c.t1[:, 1, :], start=True, stop=True)\
                .then_inc(S["b1_var"], 1)
        if p < 3:
            p_unit(c, pe, ng + 2 * p + 1, qg + 2 * p + 1, c.xn)
        if p < 4:
            if p == 0:
                c.wait_read(pe, q1 + 3)
                c.wait_read(pe, q1 + 2)
            else:
                pe.wait_ge(S["b1_var_read"], p)
            for e in range(2):
                hd = 2 * p + e
                pe.wait_ge(S["b1_prob"], hd + 1)
                nc.tensor.matmul(c.ps[:, 6, e * T:e * T + T], v[:, 0, hd * P:hd * P + P],
                                 prob[:, e, 0:T], start=True, stop=False, skip_group_check=True)
                mm = nc.tensor.matmul(c.ps[:, 6, e * T + P:e * T + T], v[:, 1, hd * P:hd * P + P],
                                      prob[:, e, T:T + P], start=False, stop=True, skip_group_check=True)
            mm.then_inc(S["b1_o"], 1)
            pe.wait_ge(S["b1_o_read"], p + 1)
            if p > 0:
                pe.wait_ge(S["b1_cen"], p)
            nc.tensor.matmul(c.ps[:, 7, :], c.c("mean_p"), c.t1[:, 0, :], start=True, stop=True)\
                .then_inc(S["b1_mean"], 1)
    n0, _ = PLAN["b1_out"]
    pe.wait_ge(S["b1_cen"], 4)
    pe.wait_ge(S["b1_var_read"], 4)
    for u in range(8):
        pe.wait_ge(S["b1_y"] if u < 4 else S["b1_y_lru"], u % 4 + 1)
        src = W[0] if u < 4 else W[7]
        d_unit(c, pe, n0 + u, lambda k: src[:, 2 * (u % 4) + k, :], u == 0, u == 7)


def b1_vector(c, dve, ch):
    S, nc, W = c.S, c.nc, c.work
    v = nc.vector
    for i, e in enumerate((EPS, 1e-5, 64e-5)):
        ch.step(v.memset(c.eps[:, i:i + 1], e))
    v.memset(c.pad[:, :, 0:4], 0.0).then_inc(S["b1_pad"], 1)
    dve.wait_ge(S["b1_pad"], 1)
    dve.wait_ge(S["par_loaded"], 16)
    dve.wait_ge(S["x_loaded"], 16)
    for b in range(4):
        gain_blocks(c, b, lambda m: ("norm_in_g", m), c.h)
    rms_vector(c, dve, "b1_in", c.xn)
    for u in range(2):
        rescaled(c, dve, "b1_xlru", u, c.pad[:, 2 * u:2 * u + 2, 3:3 + T])
    s = c.small
    ch.step(v.tensor_scalar(s[:, 16:24], c.p("lru_lambda", 0, 8), -1.0, None, ALU.mult))
    v.tensor_tensor(s[:, 0:8], s[:, 16:24], c.p("lru_lambda", 0, 8), ALU.max).then_inc(S["b1_abs"], 1)
    ch.step(v.tensor_scalar(s[:, 16:24], s[:, 16:24], 0.0, None, ALU.max))
    dve.wait_ge(S["b1_exp"], 1)
    ch.step(v.tensor_scalar(s[:, 24:32], s[:, 8:16], 2.0, None, ALU.add))
    ch.step(v.reciprocal(s[:, 24:32], s[:, 24:32]))
    ch.step(v.tensor_tensor(s[:, 24:32], s[:, 24:32], s[:, 8:16], ALU.mult))
    ch.step(v.tensor_tensor(s[:, 32:40], s[:, 24:32], s[:, 24:32], ALU.mult))
    ch.step(v.tensor_scalar(s[:, 40:48], s[:, 32:40], 1 / 17, 1 / 15, ALU.mult, ALU.add))
    for d in (13, 11, 9, 7, 5, 3, 1):
        ch.step(v.tensor_tensor(s[:, 40:48], s[:, 40:48], s[:, 32:40], ALU.mult))
        ch.step(v.tensor_scalar(s[:, 40:48], s[:, 40:48], 1 / d, None, ALU.add))
    ch.step(v.tensor_tensor(s[:, 40:48], s[:, 40:48], s[:, 24:32], ALU.mult))
    ch.step(v.scalar_tensor_tensor(out=s[:, 40:48], in0=s[:, 40:48], scalar=2.0, in1=s[:, 16:24],
                                   op0=ALU.mult, op1=ALU.add))
    ch.step(v.tensor_scalar(s[:, 80:88], s[:, 40:48], -4.0, None, ALU.mult))
    ch.step(v.tensor_scalar(s[:, 88:96], s[:, 40:48], -2.0, None, ALU.mult))
    ch.step(v.tensor_scalar(s[:, 96:104], s[:, 40:48], -8.0, None, ALU.mult))
    ch.step(v.tensor_scalar(s[:, 64:72], c.p("gate_a_b", 0, 8), 0.5, None, ALU.mult))
    ch.step(v.tensor_scalar(s[:, 72:80], c.p("gate_x_b", 0, 8), 0.5, None, ALU.mult))
    dve.wait_ge(S["con_loaded"], 16)

    def conv(b):
        _, q0 = PLAN["b1_xlru"]
        c.wait_read(dve, q0 + b // 2)
        ch.step(v.tensor_scalar(W[5][:, b, :], c.pad[:, b, 0:T], c.p("conv_w", b), c.p("conv_b", b),
                                ALU.mult, ALU.add))
        for tap in range(1, 4):
            ins = v.scalar_tensor_tensor(out=W[5][:, b, :], in0=c.pad[:, b, tap:tap + T],
                                         scalar=c.p("conv_w", 8 * tap + b), in1=W[5][:, b, :],
                                         op0=ALU.mult, op1=ALU.add)
            if tap < 3:
                ch.step(ins)
        ins.then_inc(S["b1_conv"], 1)

    def rotate(u):
        _, q0 = PLAN["b1_q"]
        dst = W[u // 4][:, 2 * (u % 4):2 * (u % 4) + 2, :].rearrange("p a b -> p (a b)")
        c.wait_read(dve, q0 + u)
        ch.step(v.tensor_tensor(dst, c.hid[:, u % 2, :], c.c("cos"), ALU.mult))
        dve.wait_ge(S["b1_rot_mm"], u + 1)
        v.tensor_tensor(c.t1[:, u % 2, :], c.ps[:, 4 + u % 2, :], c.c("sin"), ALU.mult)\
            .then_inc(S["b1_rot_read"], 1)
        dve.wait_ge(S["b1_rot_read"], u + 1)
        v.tensor_tensor(dst, dst, c.t1[:, u % 2, :], ALU.add).then_inc(S["b1_rotated"], 1)

    def decay(n):
        tmp = c.sq if n % 2 == 0 else W[8]
        e1, th, tf, e2 = (tmp[:, 2 + k, :] for k in range(4))
        dve.wait_ge(S["b1_gate_i"], n + 1)
        v.scalar_tensor_tensor(out=W[5][:, n, :], in0=tmp[:, 1, :], scalar=1.0, in1=W[5][:, n, :],
                               op0=ALU.add, op1=ALU.mult).then_inc(S["b1_ix"], 1)
        dve.wait_ge(S["b1_gate_ready"], 4 * n + 4)
        ch.step(v.scalar_tensor_tensor(out=W[6][:, n, :], in0=e1, scalar=1.0, in1=th,
                                       op0=ALU.add, op1=ALU.mult))
        ch.step(v.tensor_scalar(W[6][:, n, :], W[6][:, n, :], 1.0, None, ALU.add))
        v.scalar_tensor_tensor(out=W[7][:, n, :], in0=e2, scalar=1.0, in1=tf,
                               op0=ALU.add, op1=ALU.mult).then_inc(S["b1_gate_used"], 1)
        dve.wait_ge(S["b1_gate_used"], n + 1)
        v.tensor_scalar(W[7][:, n, :], W[7][:, n, :], -1.0, 0.0, ALU.mult, ALU.max)\
            .then_inc(S["b1_m_ready"], 1)

    for b in range(8):
        conv(b)
    for u in range(8):
        rotate(u)
        if u >= 5:
            decay(u - 5)
    for n in range(3, 8):
        decay(n)
    prob = c.hid[:, :, :].rearrange("p a b -> p (a b)").rearrange("p (a b) -> p a b", a=2)
    dec = c.table
    dve.wait_ge(S["decay_loaded"], 16)
    _, qg = PLAN["b1_gret"]

    def gate(u):
        dst = W[3 + u // 4][:, 2 * (u % 4):2 * (u % 4) + 2, :].rearrange("p a b -> p (a b)")
        dve.wait_ge(S["b1_gate_tanh"], u + 1)
        c.read(v.scalar_tensor_tensor(out=dst, in0=c.th[:, u % 2, :], scalar=1.0, in1=c.bank(qg + u),
                                      op0=ALU.add, op1=ALU.mult), qg + u)

    def retention_out(p):
        sl = (slice(None), slice(2 * p, 2 * p + 2), slice(None))
        dve.wait_ge(S["b1_var_read"], p + 1)
        ch.step(v.reciprocal(W[9][sl], W[9][sl]))
        dve.wait_ge(S["b1_cen_sq"], p + 1)
        c.wait_read(dve, qg + p)
        ch.step(v.scalar_tensor_tensor(out=W[0][sl], in0=W[0][sl], scalar=0.5, in1=W[9][sl],
                                       op0=ALU.mult, op1=ALU.mult))
        v.tensor_tensor(W[0][sl], W[0][sl], W[3][sl], ALU.mult).then_inc(S["b1_y"], 1)

    def recurrence(p):
        if p == 0:
            dve.wait_ge(S["b1_mult"], 1)
            dve.wait_ge(S["b1_ix"], 8)
        for n in (2 * p, 2 * p + 1):
            ch.step(v.scalar_tensor_tensor(out=W[7][:, n, :], in0=W[7][:, n, :], scalar=0.5,
                                           in1=W[5][:, n, :], op0=ALU.mult, op1=ALU.mult))
            ch.step(v.tensor_tensor_scan(W[5][:, n, :], W[6][:, n, :], W[7][:, n, :], 0.0,
                                         ALU.mult, ALU.add))

    def lru_out(p):
        sl = (slice(None), slice(2 * p, 2 * p + 2), slice(None))
        c.wait_read(dve, qg + 4 + p)
        v.scalar_tensor_tensor(out=W[7][sl], in0=W[5][sl], scalar=0.5, in1=W[4][sl],
                               op0=ALU.mult, op1=ALU.mult).then_inc(S["b1_y_lru"], 1)

    for p in range(5):
        if p < 4:
            for e in range(2):
                hd = 2 * p + e
                dve.wait_ge(S["b1_scores"], hd + 1)
                if p > 0:
                    dve.wait_ge(S["b1_o"], p)
                v.tensor_tensor(prob[:, e, 0:T + P], c.ps[:, 4 + e, 0:T + P], dec[:, hd, :], ALU.mult)\
                    .then_inc(S["b1_prob"], 1)
            recurrence(p)
        gate(2 * p if p < 4 else 7)
        if p < 3:
            gate(2 * p + 1)
        if p < 4:
            dve.wait_ge(S["b1_mean"], p + 1)
            v.tensor_tensor(W[0][:, 2 * p:2 * p + 2, :].rearrange("p a b -> p (a b)"), c.t1[:, 0, :],
                            c.ps[:, 7, :], ALU.subtract).then_inc(S["b1_cen"], 1)
        if p > 0:
            retention_out(p - 1)
        if p == 3:
            lru_out(0)
            lru_out(1)
    lru_out(2)
    lru_out(3)
    add_residual(c, dve, "b1_out", PLAN["b1_out"][0] + 7, 1.0, lambda b: ("norm_out_g", b))
    rms_vector(c, dve, "b1_out", c.h)


ALPHA = 2.0 ** 0.25


def at(v, step, j):
    return v if j is None else j * step + v


def ln_tensor(c, pe, k):
    S, mm = c.S, c.nc.tensor.matmul
    mem_unit(c, pe, 4 * k)
    pe.wait_ge(S["ln_x"], 4 * k + 4)
    for b in range(KB):
        ins = mm(c.ps[:, 4, 0:T], c.c("mean_c"), c.h[:, b, :], start=b == 0, stop=b == KB - 1)
    ins.then_inc(S["ln_mean"], 1)
    mem_unit(c, pe, 4 * k + 1)
    pe.wait_ge(S["ln_sq"], k + 1)
    for b in range(KB):
        ins = mm(c.ps[:, 5, 0:T], c.c("mean_c"), c.sq[:, b, :], start=b == 0, stop=b == KB - 1)
    ins.then_inc(S["ln_var"], 1)
    mem_unit(c, pe, 4 * k + 2)
    mem_unit(c, pe, 4 * k + 3)


def ln_scalar(c, act, k):
    S = c.S
    act.wait_ge(S["ln_centred"], 8 * k + 8)
    c.nc.scalar.activation(c.sq[:, :, :], c.h[:, :, :], ACT.Square).then_inc(S["ln_sq"], 1)
    act.wait_ge(S["ln_var"], k + 1)
    c.nc.scalar.activation(c.std[:, 0:T], c.ps[:, 5, 0:T], ACT.Sqrt, bias=c.eps[:, 1:2])\
        .then_inc(S["ln_std"], 1)
    n0, q0 = PLAN[("mem_k", "mem_v")[k]]
    for u in range(4):
        c.wait_done(act, n0 + u)
        dst = c.work[8][:, 2 * u:2 * u + 2, :] if k == 0 else \
            token_view(c.work[9])[:, :, u * 256:u * 256 + 256]
        c.read(c.nc.scalar.activation(dst, c.bank(q0 + u).rearrange("p (m t) -> p m t", m=2), ACT.Copy), q0 + u)


def ln_vector(c, dve, k, n, gain, bias, ch):
    S, v = c.S, c.nc.vector
    for b in range(4):
        wait_bank(c, dve, ("b2_out", "b2_ffn")[k], n, b)
        v.scalar_tensor_tensor(
            out=c.h[:, 2 * b:2 * b + 2, :], in0=c.h[:, 2 * b:2 * b + 2, :], scalar=ALPHA,
            in1=c.ps[:, 4 + b, :].rearrange("p (m t) -> p m t", m=2), op0=ALU.mult, op1=ALU.add)\
            .then_inc(S["ln_x"], 1)
    dve.wait_ge(S["ln_x"], 4 * k + 4)
    dve.wait_ge(S["ln_mean"], k + 1)
    for b in range(KB):
        v.tensor_tensor(c.h[:, b, :], c.h[:, b, :], c.ps[:, 4, 0:T], ALU.subtract)\
            .then_inc(S["ln_centred"], 1)
    dve.wait_ge(S["ln_std"], k + 1)
    ch.step(v.reciprocal(c.rstd[:, 0:T], c.std[:, 0:T]))
    for b in range(KB):
        dve.wait_ge(S["ln_sq"], k + 1)
        ch.step(v.scalar_tensor_tensor(out=c.h[:, b, :], in0=c.h[:, b, :], scalar=c.p(gain, b),
                                       in1=c.rstd[:, 0:T], op0=ALU.mult, op1=ALU.mult))
        v.tensor_scalar(c.h[:, b, :], c.h[:, b, :], c.p(bias, b), None, ALU.add).then_inc(S["ln_out"], 1)


def b2_views(c):
    W = c.work

    class V:
        q = W[0][:, 0:4, :]
        k = W[0][:, 4:8, :]
        v = W[1][:, 0:4, :].rearrange("p a b -> p (a b)").rearrange("p (m n) -> p m n", m=2)
        cb, cc, cx, pin = (W[2][:, i:i + 2, :] for i in (0, 2, 4, 6))
        mix = W[3]
        logit = [W[6][:, 2 * i:2 * i + 2, :].rearrange("p a b -> p (a b)")[:, 0:384] for i in range(4)]
        pt = [W[8][:, 2 * i:2 * i + 2, :].rearrange("p a b -> p (a b)")[:, 0:384] for i in range(2)]
        sums = [W[5][:, 2 * i:2 * i + 2, :] for i in range(4)]
        pooled = W[1][:, 4:6, :]
        conv = W[1][:, 6:8, :]
        cv = [W[4][:, 2 * i:2 * i + 2, :] for i in range(4)]
    return V


B2_UNITS = {1: "b2_pin", 2: "b2_cc", 4: "b2_cx", 6: "b2_cb"}


def b2_tensor(c, pe):
    S, nc, V, mm = c.S, c.nc, b2_views(c), c.nc.tensor.matmul
    norm_units(c, pe, "b2_q", "b1_out")
    pe.wait_ge(S["relb_loaded"], 16)
    pe.wait_ge(S["rstd_ready"], NK["b1_out"] + 1)
    mm(c.ps[0:8, 5, 0:384], c.relb[0:32, :], c.c("bucket_hot")[0:32, :], start=True, stop=True)\
        .then_inc(S["b2_bias_mm"], 1)
    for name in ("b2_k", "b2_v"):
        n0, q0 = PLAN[name]
        for u in range(2):
            p_unit(c, pe, n0 + u, q0 + u, c.h, token_major=name == "b2_v")
        if name == "b2_k":
            rms_tensor(c, pe, NK["mem"])
    pe.wait_ge(S["std_ready"], NK["mem"] + 1)
    _, qq = PLAN["b2_q"]
    pe.wait_ge(S["b2_bias_read"], 1)
    for s in range(11):
        if s < 8:
            b, e = s // 2, 64 * (s % 2)
            if s == 0:
                for u in range(4):
                    c.wait_read(pe, qq + u)
            if s >= 2:
                pe.wait_ge(S["b2_logit"], s - 1)
            mm(c.ps[:, 4 + s % 2, 0:P], V.q[e:e + 64, b, 0:P], V.k[e:e + 64, b, 0:P], start=True, stop=True)
            mm(c.ps[:, 4 + s % 2, P:P + T], V.q[e:e + 64, b, P:T], V.k[e:e + 64, b, :],
               start=True, stop=True).then_inc(S["b2_scores"], 1)
        if s in B2_UNITS:
            n0, q0 = PLAN[B2_UNITS[s]]
            p_unit(c, pe, n0, q0, c.h)
        if 2 <= s < 10:
            hd = s - 2
            pr = V.logit[hd % 4]
            pe.wait_ge(S["b2_prob"], hd + 1)
            if hd >= 1:
                pe.wait_ge(S["b2_pt"], hd)
            for k in range(3):
                ins = nc.tensor.transpose(c.ps[:, 6, k * P:k * P + P], pr[:, k * P:k * P + P], c.c("ident"))
            ins.then_inc(S["b2_turned"], 1)
        if s >= 3:
            hd = s - 3
            e = 64 * (hd % 2)
            col = 256 * (hd // 2 % 2)
            pe.wait_ge(S["b2_pt"], hd + 1)
            if hd == 0:
                for u in range(4, 6):
                    c.wait_read(pe, qq + u)
            if hd >= 2 and hd % 2 == 0:
                pe.wait_ge(S["b2_o_read"], hd // 2)
            pt = V.pt[hd % 2]
            mm(c.ps[e:e + 64, 7, col:col + T], V.v[:, 0, 64 * hd:64 * hd + 64], pt[:, 0:T],
               start=True, stop=False, skip_group_check=True)
            mm(c.ps[e:e + 64, 7, col + P:col + T], V.v[:, 1, 64 * hd:64 * hd + 64], pt[:, T:T + P],
               start=False, stop=True, skip_group_check=True).then_inc(S["b2_o"], 1)
    pe.wait_ge(S["wpool_loaded"], 16)
    pe.wait_ge(S["b2_pooled"], 1)
    for b in range(2):
        ins = mm(c.ps[:, 5, b * T:b * T + T], c.wpool[:, b, :], V.pooled[:, b, :], start=True, stop=True)
    ins.then_inc(S["b2_pool_mm"], 1)
    n0, _ = PLAN["b2_out"]
    pe.wait_ge(S["b2_o_read"], 4)
    pe.wait_ge(S["b2_conv"], 1)
    pe.wait_ge(S["b2_pool"], 1)
    for u in range(4):
        d_unit(c, pe, n0 + u, lambda k: V.mix[:, 2 * u + k, :], u == 0, u == 3)
    ln_tensor(c, pe, 0)
    pe.wait_ge(S["ln_out"], 8)
    ffn_tensor(c, pe, "b2_ffn", c.h)
    ln_tensor(c, pe, 1)


def mem_unit(c, pe, u):
    n0, q0 = PLAN["mem_k" if u < 4 else "mem_v"]
    if u == 0:
        pe.wait_ge(c.S["xn_ready"], 8 * NK["mem"] + 8)
    p_unit(c, pe, n0 + u % 4, q0 + u % 4, c.work[7], token_major=u >= 4)


def b2_scalar(c, act):
    S, nc, V = c.S, c.nc, b2_views(c)
    act.wait_ge(S["mem_loaded"], 16)
    for b in range(4):
        squares(c, NK["mem"], b, c.work[7])
    n0, q0 = PLAN["b2_q"]
    for u in range(2, 6):
        if u == 4:
            rms_root(c, act, NK["mem"])
        c.wait_done(act, n0 + u)
        if u < 4:
            dst = (V.q if u < 2 else V.k)[:, 2 * (u % 2):2 * (u % 2) + 2, :]
            src = c.bank(q0 + u).rearrange("p (m t) -> p m t", m=2)
        else:
            dst = V.v[:, :, (u - 4) * 256:(u - 4) * 256 + 256]
            src = c.bank(q0 + u).rearrange("p (m n) -> p m n", m=2)
        c.read(nc.scalar.activation(dst, src, ACT.Copy), q0 + u)
    for s in range(11):
        if s < 8:
            act.wait_ge(S["b2_max"], s + 1)
            lg = V.logit[s % 4]
            nc.scalar.activation(lg[:, 0:P], lg[:, 0:P], ACT.Exp, bias=c.small[:, 2 * s:2 * s + 1],
                                 accum_out=c.small[:, 32 + 2 * s:33 + 2 * s]).then_inc(S["b2_exp"], 1)
            nc.scalar.activation(lg[:, P:384], lg[:, P:384], ACT.Exp, bias=c.small[:, 2 * s + 1:2 * s + 2],
                                 accum_out=c.small[:, 33 + 2 * s:34 + 2 * s]).then_inc(S["b2_exp"], 1)
        if s in B2_UNITS:
            n, q = PLAN[B2_UNITS[s]]
            dst = {1: V.pin, 2: V.cc, 4: V.cx, 6: V.cb}[s]
            c.wait_done(act, n)
            c.read(nc.scalar.activation(dst, c.bank(q).rearrange("p (m t) -> p m t", m=2), ACT.Copy), q)
        if 2 <= s < 10:
            hd = s - 2
            act.wait_ge(S["b2_turned"], hd + 1)
            if hd >= 2:
                act.wait_ge(S["b2_o"], hd - 1)
            nc.scalar.activation(V.pt[hd % 2], c.ps[:, 6, 0:384], ACT.Copy).then_inc(S["b2_pt"], 1)
        if s >= 4 and s % 2 == 0:
            b = s // 2 - 2
            act.wait_ge(S["b2_o"], 2 * b + 2)
            nc.scalar.activation(V.mix[:, b, :], c.ps[:, 7, 256 * (b % 2):256 * (b % 2) + 256], ACT.Copy)\
                .then_inc(S["b2_o_read"], 1)
    ln_scalar(c, act, 0)
    n0, q0 = PLAN["b2_ffn"]

    def body(i, j):
        for g in range(2):
            q = q0 + 2 * i + g
            c.wait_done(act, gu_unit(n0, i) + g, j)
            if i >= 2 and g == 0:
                c.wait_read(act, q0 + 2 * (i - 2) + 1, j)
            for m in range(2):
                blk = 2 * i + m + (22 if g == 0 else 0)
                col = lambda name, k: c.par[:, at(PCOL[name] + k, 4, j):at(PCOL[name] + k, 4, j) + 1] \
                    if j is None else c.par[:, bass.ds(at(PCOL[name] + k, 4, j), 1)]
                nc.scalar.activation(V.cv[2 * g + i % 2][:, m, :],
                                     c.bank(q)[:, m * T:m * T + T], ACT.Identity,
                                     scale=col("ffn_conv_w_2", 88 + blk), bias=col("ffn_conv_b_2", blk))\
                    .then_inc(S["b2_tap0"], 1)
        c.wait_read(act, q0 + 2 * i, j)
        nc.scalar.activation(c.th[:, i % 2, :], V.cv[i % 2].rearrange("p m t -> p (m t)"),
                             ACT.Tanh, scale=0.5).then_inc(S["b2_tanh"], 1)
    ffn_loop(act, body)
    ln_scalar(c, act, 1)


def b2_vector(c, dve, ch):
    S, nc, V = c.S, c.nc, b2_views(c)
    v = nc.vector
    for u in range(2):
        rescaled(c, dve, "b2_q", u, V.q[:, 2 * u:2 * u + 2, :])
    dve.wait_ge(S["b2_bias_mm"], 1)
    v.tensor_tensor(c.relg[0:8, :], c.ps[0:8, 5, 0:384], c.c("future")[0:8, :], ALU.add)\
        .then_inc(S["b2_bias_read"], 1)
    c.wait_read(dve, PLAN["b2_q"][1] + 1)
    rms_vector_gain(c, dve, NK["mem"], lambda b: ("mem_norm_3", b), c.work[7], c.work[7])
    bias = c.table
    dve.wait_ge(S["bias_loaded"], 32)
    m = c.small

    def moving_sum(i):
        sh, src = 2 ** i, V.sums[i - 1] if i else V.pin
        if i == 0:
            c.wait_read(dve, PLAN["b2_pin"][1])
        ch.step(v.tensor_copy(V.sums[i][:, :, 0:sh], src[:, :, 0:sh]))
        ch.step(v.tensor_tensor(V.sums[i][:, :, sh:T], src[:, :, sh:T], src[:, :, 0:T - sh], ALU.add))

    def pool_mixer():
        inv = c.c("pool_inv").rearrange("p (m t) -> p m t", m=2)
        for i in range(4):
            e = 64 * (i % 2)
            ch.step(v.tensor_tensor(V.pooled[e:e + 64, i // 2, :], V.sums[i][e:e + 64, i // 2, :],
                                    inv[e:e + 64, i // 2, :], ALU.mult))
        v.tensor_tensor(V.pooled, V.pooled, V.pin, ALU.subtract).then_inc(S["b2_pooled"], 1)

    def conv_mixer(b):
        if b == 0:
            c.wait_read(dve, PLAN["b2_cc"][1])
            c.wait_read(dve, PLAN["b2_cx"][1])
            ch.step(v.tensor_tensor(c.pad[:, 0:2, 3:3 + T], V.cc, V.cx, ALU.mult))
        ch.step(v.tensor_scalar(V.conv[:, b, :], c.pad[:, b, 1:1 + T], c.p("conv_w_2", b), None, ALU.mult))
        for tap in (1, 2):
            ch.step(v.scalar_tensor_tensor(out=V.conv[:, b, :], in0=c.pad[:, b, 1 + tap:1 + tap + T],
                                           scalar=c.p("conv_w_2", 2 * tap + b), in1=V.conv[:, b, :],
                                           op0=ALU.mult, op1=ALU.add))

    def conv_out():
        c.wait_read(dve, PLAN["b2_cb"][1])
        v.tensor_tensor(V.mix[:, 4:6, :], V.conv, V.cb, ALU.mult).then_inc(S["b2_conv"], 1)

    for s in range(9):
        if s == 3:
            moving_sum(0)
            moving_sum(1)
        if s == 4:
            moving_sum(2)
            moving_sum(3)
        if s == 5:
            pool_mixer()
        if s == 6:
            conv_mixer(0)
        if s == 7:
            conv_mixer(1)
        if s == 8:
            conv_out()
        if s < 8:
            lg = V.logit[s % 4]
            dve.wait_ge(S["b2_scores"], s + 1)
            if s >= 4:
                dve.wait_ge(S["b2_turned"], s - 3)
            v.scalar_tensor_tensor(out=lg, in0=c.ps[:, 4 + s % 2, 0:384], scalar=0.125, in1=bias[:, s, :],
                                   op0=ALU.mult, op1=ALU.add).then_inc(S["b2_logit"], 1)
            dve.wait_ge(S["b2_logit"], s + 1)
            v.tensor_reduce(m[:, 64:65], lg[:, 0:P], AX.X, ALU.max).then_inc(S["b2_rowmax"], 1)
            v.tensor_reduce(m[:, 65:66], lg[:, P:384], AX.X, ALU.max).then_inc(S["b2_rowmax"], 1)
            dve.wait_ge(S["b2_rowmax"], 2 * s + 2)
            v.tensor_scalar(m[:, 2 * s:2 * s + 2], m[:, 64:66], -1.0, None, ALU.mult).then_inc(S["b2_max"], 1)
            dve.wait_ge(S["b2_max"], s + 1)
        if s >= 1:
            hd = s - 1
            lg = V.logit[hd % 4]
            dve.wait_ge(S["b2_exp"], 2 * hd + 2)
            ch.step(v.reciprocal(m[:, 66:68], m[:, 32 + 2 * hd:34 + 2 * hd]))
            ch.step(v.tensor_scalar(lg[:, 0:P], lg[:, 0:P], m[:, 66:67], None, ALU.mult))
            v.tensor_scalar(lg[:, P:384], lg[:, P:384], m[:, 67:68], None, ALU.mult)\
                .then_inc(S["b2_prob"], 1)
            dve.wait_ge(S["b2_prob"], hd + 1)
    dve.wait_ge(S["b2_pool_mm"], 1)
    for b in range(2):
        ins = v.tensor_scalar(V.mix[:, 6 + b, :], c.ps[:, 5, b * T:b * T + T], c.p("pool_scale_2", b), None,
                              ALU.mult)
        ch.step(ins) if b == 0 else ins.then_inc(S["b2_pool"], 1)
    ln_vector(c, dve, 0, PLAN["b2_out"][0] + 3, "ln1_g_2", "ln1_b_2", ch)

    n0, q0 = PLAN["b2_ffn"]

    def body(i, j):
        for g in range(2):
            q = q0 + 2 * i + g
            for tap in (1, 2):
                for m in range(2):
                    blk = 2 * i + m + (22 if g == 0 else 0)
                    k = PCOL["ffn_conv_w_2"] + 44 * (2 - tap) + blk
                    w = c.par[:, k:k + 1] if j is None else c.par[:, bass.ds(at(k, 4, j), 1)]
                    cv = V.cv[2 * g + i % 2][:, m, tap:T]
                    if tap == 1:
                        dve.wait_ge(S["b2_tap0"], at(4 * i + 2 * g + 2, 8, j))
                    else:
                        dve.wait_ge(S["b2_tap"], at(7 * i + (4 if g else 0) + m + 1, 14, j))
                    ins = v.scalar_tensor_tensor(out=cv, in0=c.bank(q)[:, m * T:m * T + T - tap], scalar=w,
                                                 in1=cv, op0=ALU.mult, op1=ALU.add)
                    if g == 0 and tap == 2 and m == 1:
                        c.read(ins, q)
                    else:
                        ins.then_inc(S["b2_tap"], 1)
        dve.wait_ge(S["b2_tanh"], at(i + 1, 2, j))
        c.wait_read(dve, q0 + 2 * i, j)
        v.scalar_tensor_tensor(out=c.t1[:, i % 2, :], in0=c.th[:, i % 2, :], scalar=1.0,
                               in1=V.cv[i % 2].rearrange("p m t -> p (m t)"), op0=ALU.add, op1=ALU.mult)\
            .then_inc(S["b2_half"], 1)
        if i >= 2:
            c.wait_done(dve, d_unit_of(n0, i - 2), j)
        dve.wait_ge(S["b2_tap"], at(7 * i + 7, 14, j))
        dve.wait_ge(S["b2_half"], at(i + 1, 2, j))
        c.read(v.scalar_tensor_tensor(out=c.hid[:, i % 2, :], in0=c.t1[:, i % 2, :], scalar=0.5,
                                      in1=V.cv[2 + i % 2].rearrange("p m t -> p (m t)"),
                                      op0=ALU.mult, op1=ALU.mult), q0 + 2 * i + 1)
    dve.wait_ge(S["b2_o_read"], 4)
    ffn_loop(dve, body)
    ln_vector(c, dve, 1, PLAN["b2_ffn"][0] + 3 * FFI - 1, "ln2_g_2", "ln2_b_2", ch)


def token_view(w):
    return w[:, :, :].rearrange("p a b -> p (a b)").rearrange("p (m n) -> p m n", m=2)


def ffn3(c, name, f):
    k = NK[name]
    last = PLAN[name][0] + 3 * FFI - 1

    def scalar(act, r):
        rms_scalar(c, act, k, r)
        swiglu_scalar(c, act, name, f)

    def tensor(pe):
        ffn_tensor(c, pe, name, c.xn, name)

    def vector(dve, ch, gain):
        rms_vector(c, dve, name, c.xn)
        swiglu_vector(c, dve, name, f, ch)
        add_residual(c, dve, name, last, 0.5, gain)
    return scalar, tensor, vector


def xattn_tensor(c, pe, i):
    S, nc, W, mm = c.S, c.nc, c.work, c.nc.tensor.matmul
    norm_units(c, pe, f"l{i}_xq", f"l{i}_x")
    n0, q0 = PLAN[f"l{i}_xq"]
    for u in range(2, 4):
        p_unit(c, pe, n0 + u, q0 + u, c.xn)
    if i == 0:
        for u in range(4):
            c.wait_read(pe, PLAN["mem_k"][1] + u)
            c.wait_read(pe, PLAN["mem_v"][1] + u)
    v = token_view(W[9])
    for s in range(7):
        if s < 4:
            c.wait_read(pe, q0 + s)
            for n in range(2):
                for k in range(2):
                    ins = mm(c.bank(q0 + s)[:, n * T:n * T + T], W[0][:, 2 * s + k, n * P:n * P + P],
                             W[8][:, 2 * s + k, :], start=k == 0, stop=k == 1)
            ins.then_inc(S["x_scores"], 1)
        if 2 <= s < 6:
            hd = s - 2
            pe.wait_ge(S["x_prob"], 4 * i + hd + 1)
            if hd >= 2:
                pe.wait_ge(S["x_pt"], 4 * i + hd - 1)
            for k in range(2):
                for n in range(2):
                    col = (2 * k + n) * P
                    ins = nc.tensor.transpose(c.ps[:, 6 - hd % 2, col:col + P],
                                              W[2][:, 2 * hd + n, k * P:k * P + P], c.c("ident"))
            ins.then_inc(S["x_turned"], 1)
        if s >= 3:
            hd = s - 3
            pe.wait_ge(S["x_pt"], 4 * i + hd + 1)
            if hd >= 2:
                pe.wait_ge(S["x_o_read"], 4 * i + hd - 1)
            for d in range(2):
                for k in range(2):
                    ins = mm(c.ps[:, 7 - 3 * (hd % 2), d * T:d * T + T],
                             v[:, k, (2 * hd + d) * P:(2 * hd + d) * P + P],
                             W[4][:, 2 * (hd % 2) + k, :], start=k == 0, stop=k == 1)
            ins.then_inc(S["x_o"], 1)
    n0, _ = PLAN[f"l{i}_xo"]
    pe.wait_ge(S["x_o_read"], 4 * i + 4)
    for u in range(4):
        d_unit(c, pe, n0 + u, lambda k: W[1][:, 2 * u + k, :], u == 0, u == 3)


def xattn_scalar(c, act, i, r):
    S, nc, W = c.S, c.nc, c.work
    rms_scalar(c, act, NK[f"l{i}_x"], r)
    n0, q0 = PLAN[f"l{i}_xq"]
    for u in range(2, 4):
        c.wait_done(act, n0 + u)
        c.read(nc.scalar.activation(W[0][:, 2 * u:2 * u + 2, :],
                                    c.bank(q0 + u).rearrange("p (m t) -> p m t", m=2), ACT.Copy), q0 + u)
    for s in range(7):
        if s < 4:
            act.wait_ge(S["x_max"], 4 * i + s + 1)
            for n in range(2):
                nc.scalar.activation(W[2][:, 2 * s + n, :], c.bank(q0 + s)[:, n * T:n * T + T], ACT.Exp,
                                     scale=1.0 / 16, bias=c.small[:, 4 * s + n:4 * s + n + 1],
                                     accum_out=c.small[:, 32 + 4 * s + n:33 + 4 * s + n])\
                    .then_inc(S["x_exp"], 1)
        if 2 <= s < 6:
            hd = s - 2
            act.wait_ge(S["x_turned"], 4 * i + hd + 1)
            if hd >= 2:
                act.wait_ge(S["x_o"], 4 * i + hd - 1)
            nc.scalar.activation(W[4][:, 2 * (hd % 2):2 * (hd % 2) + 2, :],
                                 c.ps[:, 6 - hd % 2, :].rearrange("p (k q) -> p k q", k=2), ACT.Copy)\
                .then_inc(S["x_pt"], 1)
        if s >= 3:
            hd = s - 3
            act.wait_ge(S["x_o"], 4 * i + hd + 1)
            nc.scalar.activation(W[1][:, 2 * hd:2 * hd + 2, :],
                                 c.ps[:, 7 - 3 * (hd % 2), :].rearrange("p (d q) -> p d q", d=2), ACT.Copy)\
                .then_inc(S["x_o_read"], 1)


def xattn_vector(c, dve, i, ch, gain):
    S, W, v, m = c.S, c.work, c.nc.vector, c.small
    rms_vector(c, dve, f"l{i}_x", c.xn)
    for u in range(2):
        rescaled(c, dve, f"l{i}_xq", u, W[0][:, 2 * u:2 * u + 2, :])
    _, q0 = PLAN[f"l{i}_xq"]
    for s in range(5):
        if s < 4:
            dve.wait_ge(S["x_scores"], 4 * i + s + 1)
            ch.step(v.tensor_reduce(m[:, 64:66], c.bank(q0 + s).rearrange("p (n k) -> p n k", n=2),
                                    AX.X, ALU.max))
            v.tensor_scalar(m[:, 4 * s:4 * s + 2], m[:, 64:66], -1.0 / 16, None, ALU.mult)\
                .then_inc(S["x_max"], 1)
            dve.wait_ge(S["x_max"], 4 * i + s + 1)
        if s >= 1:
            hd = s - 1
            dve.wait_ge(S["x_exp"], 8 * i + 2 * hd + 2)
            ch.step(v.reciprocal(m[:, 66:68], m[:, 32 + 4 * hd:34 + 4 * hd]))
            pr = W[2][:, 2 * hd:2 * hd + 2, :]
            ch.step(v.tensor_scalar(pr[:, 0, :], pr[:, 0, :], m[:, 66:67], None, ALU.mult))
            v.tensor_scalar(pr[:, 1, :], pr[:, 1, :], m[:, 67:68], None, ALU.mult).then_inc(S["x_prob"], 1)
            dve.wait_ge(S["x_prob"], 4 * i + hd + 1)
    add_residual(c, dve, f"l{i}_xo", PLAN[f"l{i}_xo"][0] + 3, 1.0, gain)


def gmlp_tensor(c, pe):
    S, W, mm = c.S, c.work, c.nc.tensor.matmul
    norm_units(c, pe, "gm_u", "l1_mix")
    n1, _ = PLAN["gm_u"]
    for u in range(2, 8):
        p_unit(c, pe, n1 + u, PLAN["gm_u"][1] + u, c.xn)
    n0, q1 = PLAN["gm_v"]
    for u in range(8):
        p_unit(c, pe, n0 + u, q1 + u, c.xn, token_major=True)
    pe.wait_ge(S["gm_ws"], 1)
    for g in range(16):
        if g % 4 == 0:
            pe.wait_ge(S["gm_vn"], g // 2 + 2)
        if g == 8:
            for u in range(4, 8):
                c.wait_read(pe, q1 + u)
        for n in range(2):
            mm(c.ps[:, (g // 2 + 4) % 8, 256 * (g % 2) + n * P:256 * (g % 2) + n * P + P],
               W[n][:, :, :].rearrange("p a b -> p (a b)")[:, g * P:g * P + P],
               W[2][:, :, :].rearrange("p a b -> p (a b)")[:, g * P:g * P + P],
               start=True, stop=True).then_inc(S["gm_sv"], 1)
    n0, _ = PLAN["gm_out"]
    pe.wait_ge(S["gm_sv_read"], 8)
    for u in range(8):
        pe.wait_ge(S["gm_y"], 2 * u + 2)
        d_unit(c, pe, n0 + u, lambda k: W[4 + u // 4][:, 2 * (u % 4) + k, :], u == 0, u == 7)


def gmlp_scalar(c, act, r):
    S, nc, W = c.S, c.nc, c.work
    rms_scalar(c, act, NK["l1_mix"], r)
    n1, q1 = PLAN["gm_u"]
    for u in range(8):
        dst = W[4 + u // 4][:, 2 * (u % 4):2 * (u % 4) + 2, :]
        if u < 2:
            c.wait_read(act, q1 + u)
            nc.scalar.activation(dst, dst, ACT.Gelu_apprx_tanh).then_inc(S["gm_u_first"], 1)
        else:
            c.wait_done(act, n1 + u)
            c.read(nc.scalar.activation(dst, c.bank(q1 + u).rearrange("p (m t) -> p m t", m=2),
                                        ACT.Gelu_apprx_tanh), q1 + u)
    n0, q0 = PLAN["gm_v"]
    for u in range(8):
        c.wait_done(act, n0 + u)
        bank = c.bank(q0 + u).rearrange("p (m n) -> p m n", m=2)
        dst = [W[n][:, :, :].rearrange("p a b -> p (a b)")[:, u * 256:u * 256 + 256] for n in range(2)]
        nc.scalar.activation(dst[0], bank[:, 0, :], ACT.Gelu_apprx_tanh).then_inc(S["gm_v0"], 1)
        c.read(nc.scalar.activation(dst[1], bank[:, 1, :], ACT.Gelu_apprx_tanh), q0 + u)
        act.wait_ge(S["gm_v0"], u + 1)
        c.wait_read(act, q0 + u)
        for n in range(2):
            nc.scalar.activation(W[6 + n][:, u, :], dst[n], ACT.Square,
                                 accum_out=c.small[:, 16 + 8 * n + u:17 + 8 * n + u]).then_inc(S["gm_sq"], 1)
    act.wait_ge(S["gm_ms"], 1)
    nc.scalar.activation(c.small[:, 4:6], c.small[:, 2:4], ACT.Sqrt).then_inc(S["gm_std"], 1)


def gmlp_vector(c, dve, ch, gain):
    S, W, v, m = c.S, c.work, c.nc.vector, c.small
    rms_vector(c, dve, "l1_mix", c.xn)
    for u in range(2):
        rescaled(c, dve, "gm_u", u, W[4][:, 2 * u:2 * u + 2, :])
    dve.wait_ge(S["gm_loaded"], 32)
    ws = W[2][:, :, :].rearrange("p a b -> p (a b)").rearrange("p (g t) -> p g t", g=16)
    causal = c.c("causal").rearrange("p (a t) -> p a t", a=1).to_broadcast([P, 16, P])
    v.tensor_tensor(ws, ws, causal, ALU.mult).then_inc(S["gm_ws"], 1)
    dve.wait_ge(S["gm_sq"], 16)
    ch.step(v.tensor_reduce(m[:, 0:2], m[:, 16:32].rearrange("p (n u) -> p n u", n=2), AX.X, ALU.add))
    v.tensor_scalar(m[:, 2:4], m[:, 0:2], 1.0 / 2048, EPS, ALU.mult, ALU.add).then_inc(S["gm_ms"], 1)
    dve.wait_ge(S["gm_std"], 1)
    ch.step(v.reciprocal(m[:, 6:8], m[:, 4:6]))
    for part in range(4):
        for n in range(2):
            sl = (slice(None), slice(2 * part, 2 * part + 2), slice(None))
            v.tensor_scalar(W[n][sl], W[n][sl], m[:, 6 + n:7 + n], None, ALU.mult).then_inc(S["gm_vn"], 1)
    bs = W[3][:, :, :].rearrange("p a b -> p (a b)").rearrange("p (g t) -> p g t", g=16)
    for g in range(16):
        dve.wait_ge(S["gm_sv"], 2 * (g // 2 * 2 + 2))
        if g == 0:
            dve.wait_ge(S["gm_u_first"], 2)
        if g >= 4:
            c.wait_read(dve, PLAN["gm_u"][1] + g // 2)
        sv = W[6 + g // 8][:, g % 8, :]
        v.scalar_tensor_tensor(out=sv.rearrange("p (n t) -> p n t", n=2),
                               in0=c.ps[:, (g // 2 + 4) % 8, 256 * (g % 2):256 * (g % 2) + 256]
                               .rearrange("p (n t) -> p n t", n=2),
                               scalar=c.p("gmlp_v_norm_3", g),
                               in1=bs[:, g:g + 1, :].to_broadcast([P, 2, P]),
                               op0=ALU.mult, op1=ALU.add).then_inc(S["gm_sv_read"], 1)
        dve.wait_ge(S["gm_sv_read"], g + 1)
        v.tensor_tensor(W[4 + g // 8][:, g % 8, :], W[4 + g // 8][:, g % 8, :], sv, ALU.mult)\
            .then_inc(S["gm_y"], 1)
    add_residual(c, dve, "gm_out", PLAN["gm_out"][0] + 7, 1.0, gain)


DECAY_SCALE = math.exp(-0.5)


def rw_views(c):
    W = c.work

    class V:
        bonus = c.pad[:, :, 0:T]
        vt, kt, bt = (token_view(w) for w in (c.sq, c.xn, W[3]))
        lora1 = c.table[:, :, 0:288]
        lora_wa = c.t1[:, :, :].rearrange("p a b -> p (a b)")
        lora_g = c.hid[:, :, :].rearrange("p a b -> p (a b)")
        lora_gt = c.th[:, :, :].rearrange("p a b -> p (a b)")[0:32, :]
        low = W[2][:, :, :].rearrange("p a b -> p (a b)").rearrange("p (i t) -> p i t", i=16)
        inv = W[6][:, :, :].rearrange("p a b -> p (a b)").rearrange("p (i t) -> p i t", i=16)
        tab = c.table[:, :, :].rearrange("p a b -> p (a b)")
        grow = tab[:, 0:2048].rearrange("p (a b) -> p a b", a=KB)
        invt = tab[:, 0:2048].rearrange("p (i t) -> p i t", i=16)
        x0 = tab[:, 2048:3072].rearrange("p (h n) -> p h n", h=2)
        zed = [c.th[:, :, :].rearrange("p a b -> p (a b)").rearrange("p (i t) -> p i t", i=8),
               c.t1[:, :, :].rearrange("p a b -> p (a b)").rearrange("p (i t) -> p i t", i=8)]
        sa = [c.std, c.rstd]
        state = c.hid[:, 0, :].rearrange("p (b i) -> p b i", b=8)
        pend = c.small[:, 160:192].rearrange("p (b n) -> p b n", b=8)
        gk = low
        rb = invt
        rk = zed
    return V


def rw_head(i):
    g, r = i // 4, i % 4
    half, blk = g % 2, 4 * (g // 2) + r
    return 2 * blk + half, half, blk


RW_PROBLEM = {rw_head(i)[0]: i for i in range(16)}


def rw_z(V, i):
    return V.zed[i // 8][:, i % 8, :]


def rw_z4(V, g):
    return V.zed[g // 2][:, 4 * (g % 2):4 * (g % 2) + 4, :]


RW_PE, RW_VEC = 64, 68


def pe_step(n, kind, l, g):
    if l == 0:
        k = {"z": g, "zt": 4 + g}[kind]
    elif l < 5:
        k = 8 + 12 * (l - 1) + {"z": g, "q": 4 + 2 * g, "x": 5 + 2 * g}[kind]
    else:
        k = 8 + 12 * 4 + {"z": g, "q": 4 + g}[kind]
    return RW_PE * n + k + 1


def vec_step(n, kind, l, g):
    if l == 0:
        k = {"z": g, "q": 4 + g, "x": 8 + g}[kind]
    elif l < 5:
        k = 12 + 12 * (l - 1) + {"z": g, "q": 4 + 2 * g, "x": 5 + 2 * g}[kind]
    else:
        k = 12 + 12 * 4 + {"z": g, "q": 4 + g}[kind]
    return RW_VEC * n + k + 1


def rw_tensor(c, pe):
    S, nc, W, V, mm = c.S, c.nc, c.work, rw_views(c), c.nc.tensor.matmul
    tr = nc.tensor.transpose
    rms_tensor(c, pe, NK["l0_mix"])
    for i, name in enumerate(("rw_r", "rw_k", "rw_v")):
        n0, q0 = PLAN[name]
        for u in range(4):
            if u == 0:
                first_unit(c, pe, n0, q0, W[1 + i], S["rw_mix"], 8 * i)
            else:
                p_unit(c, pe, n0 + u, q0 + u, W[1 + i])
            if i == 2 and u == 1:
                pe.wait_ge(S["rw_kk_sq"], 1)
                for b in range(KB):
                    ins = mm(c.ps[:, 4 + b // 2, (b % 2) * T:(b % 2) * T + T], c.c("sum_h"), c.xn[:, b, :],
                             start=True, stop=True)
                ins.then_inc(S["rw_kk_sum"], 1)
    pe.wait_ge(S["lora_loaded"], 64)
    pe.wait_ge(S["rw_mix"], 48)
    pe.wait_ge(S["rw_norm"], 4)
    for k in range(KB):
        for half, x in ((slice(0, 64), W[4]), (slice(64, 128), W[5])):
            mm(c.ps[half, 4, 0:T], V.lora1[:, k, half], x[:, k, :], start=k == 0, stop=k == KB - 1,
               skip_group_check=True)
    for out, cols, x in ((c.ps[:, 5, 0:T], (128, 256), W[6]), (c.ps[0:32, 6, 0:T], (256, 288), W[6])):
        for k in range(KB):
            ins = mm(out, V.lora1[:, k, cols[0]:cols[1]], x[:, k, :], start=k == 0, stop=k == KB - 1)
    ins.then_inc(S["rw_lora_mm"], 1)
    pe.wait_ge(S["rw_lora_act"], 4)
    for u in range(4):
        c.wait_read(pe, PLAN["rw_v"][1] + u)
    for b in range(KB):
        o = slice(b * P, b * P + P)
        b0 = 4 * (1 - b % 2)
        if b > 1:
            pe.wait_ge(S["rw_z_read"], 3 * b - 3)
        mm(c.ps[:, b0 + 0, 0:T], V.lora_wa[0:64, o], c.sq[0:64, 0, :], start=True, stop=True)
        mm(c.ps[:, b0 + 1, 0:T], V.lora_wa[64:128, o], c.sq[64:128, 0, :], start=True, stop=True)
        mm(c.ps[:, b0 + 2, 0:T], V.lora_g[:, o], c.sq[:, 1, :], start=True, stop=False)
        mm(c.ps[:, b0 + 2, 0:T], V.lora_gt[:, o], c.sq[0:32, 2, :], start=False, stop=True)\
            .then_inc(S["rw_z_mm"], 1)
    pe.wait_ge(S["rw_z_read"], 24)
    _, qv = PLAN["rw_v"]
    for u in range(4):
        c.wait_read(pe, qv + u)
    turn = 0
    for src, ready in ((W[2], ("rw_z_read", 24)), (W[4], ("rw_tilde", 2)), (W[1], ("rw_pool", 1))):
        if turn == 4:
            for b in range(KB):
                pe.wait_ge(S["rw_rk"], b + 1)
                ins = mm(c.ps[:, 4 + b // 2, (b % 2) * T:(b % 2) * T + T], c.c("sum_h"), W[6][:, b, :],
                         start=True, stop=True)
            ins.then_inc(S["rw_rk_sum"], 1)
        pe.wait_ge(S[ready[0]], ready[1])
        for g in range(4):
            if turn >= 4:
                pe.wait_ge(S["rw_turn_read"], turn - 3)
            for r in range(4):
                b, n = 4 * (g % 2) + r, g // 2
                ins = tr(c.ps[:, turn % 4, r * P:r * P + P], src[:, b, n * P:n * P + P], c.c("ident"))
            ins.then_inc(S["rw_turned"], 1)
            turn += 1
    pe.wait_ge(S["rw_turn_read"], 12)
    pe.wait_ge(S["rw_tilde"], 3)
    for n in range(2):
        tok = slice(n * P, n * P + P)
        if n:
            pe.wait_ge(S["rw_x0_read"], 2)
            pe.wait_ge(S["rw_sa_read"], 4)
            pe.wait_ge(S["rw_y_add"], 4)
            pe.wait_ge(S["rw_y_read"], 2)
            pe.wait_ge(S["rw_state"], 2)
        for g in range(4):
            for r in range(4):
                _, e, b = rw_head(4 * g + r)
                rows = slice(64 * e, 64 * e + 64)
                ins = mm(c.ps[:, g, r * P:r * P + P], W[0][rows, b, tok], W[4][rows, b, tok],
                         start=True, stop=True)
            ins.then_inc(S["rw_low_mm"], 1)
        pe.wait_ge(S["rw_bonus"], 4)
        for g in range(4):
            pe.wait_ge(S["rw_low"], 4 * n + g + 1)
            for r in range(4):
                ins = tr(c.ps[:, 4 + g, r * P:r * P + P], V.low[:, 4 * g + r, :], c.c("ident"))
            ins.then_inc(S["rw_inv_mm"], 1)
        for g in range(4):
            pe.wait_ge(S["rw_inv"], vec_step(n, "z", 0, g))
            for r in range(4):
                ins = tr(c.ps[:, g, r * P:r * P + P], rw_z(V, 4 * g + r), c.c("ident"))
            ins.then_inc(S["rw_inv_mm"], 1)
        for l in range(1, 6):
            for g in range(4):
                pe.wait_ge(S["rw_inv"], vec_step(n, "x", l - 1, g))
                for r in range(4):
                    ins = mm(c.ps[:, 4 + g, r * P:r * P + P], V.low[:, 4 * g + r, :], V.inv[:, 4 * g + r, :],
                             start=True, stop=True)
                ins.then_inc(S["rw_inv_mm"], 1)
            for g in range(4):
                pe.wait_ge(S["rw_inv"], vec_step(n, "z", l, g))
                for r in range(4):
                    ins = mm(c.ps[:, g, r * P:r * P + P], V.invt[:, 4 * g + r, :], rw_z(V, 4 * g + r),
                             start=True, stop=True)
                ins.then_inc(S["rw_inv_mm"], 1)
                if l < 5:
                    for r in range(4):
                        ins = mm(c.ps[:, 4 + g, r * P:r * P + P], rw_z(V, 4 * g + r),
                                 V.invt[:, 4 * g + r, :], start=True, stop=True)
                    ins.then_inc(S["rw_inv_mm"], 1)
        pe.wait_ge(S["rw_pool"], 2)
        for j, (x, y) in enumerate(((1, 0), (4, 7), (1, 7))):
            for g in range(4):
                bank = (4 + g) if j == 1 else g
                if j == 0:
                    pe.wait_ge(S["rw_inv"], vec_step(n, "q", 5, g))
                elif j == 1:
                    pe.wait_ge(S["rw_inv"], vec_step(n, "z", 5, g))
                else:
                    pe.wait_ge(S["rw_mat"], 12 * n + g + 1)
                for r in range(4):
                    _, e, b = rw_head(4 * g + r)
                    rows = slice(64 * e, 64 * e + 64)
                    ins = mm(c.ps[:, bank, r * P:r * P + P], W[x][rows, b, tok], W[y][rows, b, tok],
                             start=True, stop=True)
                ins.then_inc(S["rw_mat_mm"], 1)
        pe.wait_ge(S["rw_mat"], 12 * n + 12)
        for i in range(16):
            hd, e, b = rw_head(i)
            mm(c.ps[:, e, b * 64:b * 64 + 64], V.gk[:, i, :], V.vt[:, n, hd * 64:hd * 64 + 64],
               start=b == 0, stop=False, skip_group_check=True)
        for cc in range(2):
            ci = 2 * n + cc
            rows = slice(64 * cc, 64 * cc + 64)
            tk = slice(ci * 64, ci * 64 + 64)

            def half(e):
                return slice(64 * e, 64 * e + 64)

            def cols(hd):
                return slice(hd // 2 * 64, hd // 2 * 64 + 64)

            def y_intra(hd):
                i = RW_PROBLEM[hd]
                return mm(c.ps[half(hd % 2), 4, cols(hd)], V.vt[rows, n, hd * 64:hd * 64 + 64],
                          V.rk[i // 8][rows, i % 8, rows], start=hd < 2, stop=False, skip_group_check=True)

            def y_sa(hd):
                return mm(c.ps[half(hd % 2), 4, cols(hd)], V.sa[hd % 2][rows, cols(hd)],
                          V.rb[rows, RW_PROBLEM[hd], rows], start=False, stop=True, skip_group_check=True)

            def y_state(hd):
                e = hd % 2
                return mm(c.ps[half(e), 7 - 2 * e, cols(hd)], V.state[half(e), hd // 2, :],
                          W[7][half(e), hd // 2, tk], start=True, stop=True)

            def rhs(hd):
                e = hd % 2
                return mm(c.ps[rows, e, cols(hd)], W[0][half(e), hd // 2, tk], V.state[half(e), hd // 2, :],
                          start=False, stop=True, skip_group_check=True)

            def solve(hd):
                e = hd % 2
                return mm(c.ps[rows, 2 + e, cols(hd)], V.inv[rows, RW_PROBLEM[hd], rows],
                          V.x0[rows, e, cols(hd)], start=True, stop=True)

            def s_kv(hd):
                return mm(c.ps[half(hd % 2), 6, cols(hd)], V.kt[rows, n, hd * 64:hd * 64 + 64],
                          V.vt[rows, n, hd * 64:hd * 64 + 64], start=hd < 2, stop=False, skip_group_check=True)

            def s_sa(hd):
                return mm(c.ps[half(hd % 2), 6, cols(hd)], V.bt[rows, n, hd * 64:hd * 64 + 64],
                          V.sa[hd % 2][rows, cols(hd)], start=False, stop=True, skip_group_check=True)

            if ci:
                pe.wait_ge(S["rw_y_read"], ci)
            for hd in range(16):
                y_intra(hd)
            if ci:
                pe.wait_ge(S["rw_state"], ci)
                pe.wait_ge(S["rw_y_add"], 2 * ci)
            if cc:
                pe.wait_ge(S["rw_x0_read"], ci)
            for b in range(8):
                other = 2 * b + 1 - cc
                rhs(2 * b)
                y_state(other)
                ins = rhs(2 * b + 1)
                if ci < 3:
                    s_kv(other)
            ins.then_inc(S["rw_x0"], 1)
            for b in range(8):
                y_state(2 * b + cc)
            pe.wait_ge(S["rw_x0_read"], ci + 1)
            if ci:
                pe.wait_ge(S["rw_sa_read"], 2 * ci)
            for hd in range(16):
                ins = solve(hd)
            ins.then_inc(S["rw_sa"], 1)
            if ci < 3:
                for b in range(8):
                    s_kv(2 * b + cc)
            pe.wait_ge(S["rw_sa_read"], 2 * ci + 2)
            if ci < 3:
                for hd in range(16):
                    ins = s_sa(hd)
                ins.then_inc(S["rw_s"], 1)
            for hd in range(16):
                ins = y_sa(hd)
            ins.then_inc(S["rw_y"], 1)
    pe.wait_ge(S["rw_y_add"], 8)
    pe.wait_ge(S["rw_sa_read"], 8)
    pe.wait_ge(S["rw_x0_read"], 4)
    for b in range(KB):
        ins = mm(c.ps[:, b // 2, (b % 2) * T:(b % 2) * T + T], c.c("mean_h"), W[7][:, b, :],
                 start=True, stop=True)
        if b % 2:
            ins.then_inc(S["rw_mean"], 1)
    pe.wait_ge(S["rw_y_read"], 4)
    for b in range(KB):
        pe.wait_ge(S["rw_cen_sq"], b // 2 + 1)
        ins = mm(c.ps[:, 4 + b // 2, (b % 2) * T:(b % 2) * T + T], c.c("mean_h"), W[6][:, b, :],
                 start=True, stop=True)
        if b % 2:
            ins.then_inc(S["rw_var"], 1)
    n0, _ = PLAN["rw_out"]
    pe.wait_ge(S["rw_gn_std"], 4)
    for u in range(4):
        pe.wait_ge(S["rw_out"], u + 1)
        d_unit(c, pe, n0 + u, lambda k: W[7][:, 2 * u + k, :], u == 0, u == 3)


def rw_scalar(c, act, r):
    S, nc, W, V = c.S, c.nc, c.work, rw_views(c)
    A = nc.scalar.activation
    rms_scalar(c, act, NK["l0_mix"], r)
    for i, name in enumerate(("rw_r", "rw_k", "rw_v")):
        n0, q0 = PLAN[name]
        dst = (W[7], W[1], W[2])[i]
        for u in range(4):
            c.wait_done(act, n0 + u)
            if i and u == 0:
                for k in range(4):
                    c.wait_done(act, PLAN[("rw_r", "rw_k")[i - 1]][0] + k)
            c.read(A(dst[:, 2 * u:2 * u + 2, :], c.bank(q0 + u).rearrange("p (m t) -> p m t", m=2),
                     ACT.Copy), q0 + u)
            if i == 2 and u == 0:
                act.wait_ge(S["rw_kk"], 8)
                A(c.xn[:, :, :], W[0][:, :, :], ACT.Square).then_inc(S["rw_kk_sq"], 1)
            if i == 2 and u == 2:
                act.wait_ge(S["rw_kk_sum"], 1)
                for g in range(4):
                    A(c.xn[:, 2 * g:2 * g + 2, :], c.ps[:, 4 + g, :].rearrange("p (m t) -> p m t", m=2),
                      ACT.Sqrt).then_inc(S["rw_norm"], 1)
    act.wait_ge(S["rw_lora_mm"], 1)
    A(c.sq[0:64, 0, :], c.ps[0:64, 4, 0:T], ACT.Tanh).then_inc(S["rw_lora_act"], 1)
    A(c.sq[64:128, 0, :], c.ps[64:128, 4, 0:T], ACT.Copy).then_inc(S["rw_lora_act"], 1)
    A(c.sq[:, 3, :], c.ps[:, 5, 0:T], ACT.Tanh, scale=0.5).then_inc(S["rw_lora_g"], 1)
    A(c.sq[0:32, 4, :], c.ps[0:32, 6, 0:T], ACT.Tanh, scale=0.5).then_inc(S["rw_lora_g"], 1)
    for b in range(KB):
        b0 = 4 * (1 - b % 2)
        act.wait_ge(S["rw_z_mm"], b + 1)
        A(W[3][:, b, :], c.ps[:, b0, 0:T], ACT.Sigmoid, bias=c.p("rwkv_w0_3", b)).then_inc(S["rw_z_read"], 1)
        A(W[4][:, b, :], c.ps[:, b0 + 1, 0:T], ACT.Sigmoid, bias=c.p("rwkv_a0_3", b)).then_inc(S["rw_z_read"], 1)
        A(W[5][:, b, :], c.ps[:, b0 + 2, 0:T], ACT.Copy).then_inc(S["rw_z_read"], 1)
    for turn in range(12):
        if turn == 4:
            act.wait_ge(S["rw_before"], 1)
            A(W[3][:, :, :], W[3][:, :, :], ACT.Exp, scale=-DECAY_SCALE).then_inc(S["rw_exp"], 1)
            A(V.grow, c.xn[:, :, :], ACT.Exp, scale=DECAY_SCALE).then_inc(S["rw_exp"], 1)
            act.wait_ge(S["rw_rk_sum"], 1)
            A(W[6][:, :, :], c.xn[:, :, :], ACT.Exp, scale=-DECAY_SCALE).then_inc(S["rw_exp"], 1)
        n, h = turn // 2 % 2, turn % 2
        dst = (V.vt, V.bt, V.kt)[turn // 4]
        act.wait_ge(S["rw_turned"], turn + 1)
        if turn == 4:
            act.wait_ge(S["rw_tilde"], 2)
        if turn == 8:
            act.wait_ge(S["rw_exp"], 3)
        A(dst[:, n, h * 512:h * 512 + 512], c.ps[:, turn % 4, :], ACT.Copy).then_inc(S["rw_turn_read"], 1)
    for n in range(2):
        for g in range(4):
            act.wait_ge(S["rw_bonus"], g + 1)
            act.wait_ge(S["rw_low_mm"], 4 * n + g + 1)
            A(V.low[:, 4 * g:4 * g + 4, :], c.ps[:, g, :].rearrange("p (r t) -> p r t", r=4), ACT.Copy)\
                .then_inc(S["rw_low"], 1)
        for cc in range(2):
            ci = 2 * n + cc
            rows = slice(64 * cc, 64 * cc + 64)
            act.wait_ge(S["rw_x0"], ci + 1)
            A(V.x0[rows, :, :], c.ps[rows, 0:2, :], ACT.Copy).then_inc(S["rw_x0_read"], 1)
            act.wait_ge(S["rw_sa"], ci + 1)
            for e in range(2):
                A(V.sa[e][rows, :], c.ps[rows, 2 + e, :], ACT.Copy, scale=-1.0).then_inc(S["rw_sa_read"], 1)
            act.wait_ge(S["rw_y"], ci + 1)
            A(W[7][:, :, ci * 64:ci * 64 + 64], c.ps[:, 4, :].rearrange("p (b t) -> p b t", b=8), ACT.Copy)\
                .then_inc(S["rw_y_read"], 1)
    for g in range(4):
        act.wait_ge(S["rw_cen"], g + 1)
        A(W[6][:, 2 * g:2 * g + 2, :], W[7][:, 2 * g:2 * g + 2, :], ACT.Square).then_inc(S["rw_cen_sq"], 1)
    for g in range(4):
        act.wait_ge(S["rw_var"], g + 1)
        A(W[2][:, 2 * g:2 * g + 2, :], c.ps[:, 4 + g, :].rearrange("p (m t) -> p m t", m=2), ACT.Sqrt,
          bias=c.eps[:, 2:3]).then_inc(S["rw_gn_std"], 1)


def rw_vector(c, dve, ch, gain):
    S, W, V, v = c.S, c.work, rw_views(c), c.nc.vector
    def mix(i, m, b):
        v.scalar_tensor_tensor(out=W[1 + i][:, b, :], in0=W[0][:, b, :],
                               scalar=c.p("rwkv_mu_3", 8 * m + b), in1=c.xn[:, b, :],
                               op0=ALU.mult, op1=ALU.add).then_inc(S["rw_mix"], 1)

    rms_recip(c, dve, NK["l0_mix"])
    dve.wait_ge(S["xg_ready"], 8 * GAINED.index("l0_mix") + 8)
    for b in range(KB):
        v.tensor_tensor(c.xn[:, b, :], c.xg[:, b, :], c.rstd[:, 0:T], ALU.mult).then_inc(S["xn_ready"], 1)
        dve.wait_ge(S["xn_ready"], 8 * NK["l0_mix"] + b + 1)
        ch.step(v.tensor_scalar(W[0][:, b, 0:1], c.xn[:, b, 0:1], -1.0, None, ALU.mult))
        ch.step(v.tensor_tensor(W[0][:, b, 1:T], c.xn[:, b, 0:T - 1], c.xn[:, b, 1:T], ALU.subtract))
        mix(0, 0, b)
    for i, m in ((1, 2), (2, 3), (3, 1), (4, 4), (5, 5)):
        for b in range(KB):
            mix(i, m, b)
    _, qk = PLAN["rw_k"]
    for u in range(4):
        c.wait_read(dve, qk + u)
    dve.wait_ge(S["rw_mix"], 48)
    for b in range(KB):
        v.tensor_scalar(W[0][:, b, :], W[1][:, b, :], c.p("rwkv_k_k_3", b), None, ALU.mult)\
            .then_inc(S["rw_kk"], 1)
    for g in range(4):
        sl = (slice(None), slice(2 * g, 2 * g + 2), slice(None))
        dve.wait_ge(S["rw_norm"], g + 1)
        ch.step(v.tensor_scalar(c.xn[sl], c.xn[sl], 1e-12, None, ALU.max))
        ch.step(v.reciprocal(c.xn[sl], c.xn[sl]))
        ch.step(v.tensor_tensor(W[0][sl], W[0][sl], c.xn[sl], ALU.mult))
    dve.wait_ge(S["rw_lora_g"], 2)
    v.tensor_scalar(c.sq[:, 1, :], c.sq[:, 3, :], 1.0, 0.5, ALU.add, ALU.mult).then_inc(S["rw_lora_act"], 1)
    v.tensor_scalar(c.sq[0:32, 2, :], c.sq[0:32, 4, :], 1.0, 0.5, ALU.add, ALU.mult)\
        .then_inc(S["rw_lora_act"], 1)
    _, qr = PLAN["rw_r"]
    for u in range(4):
        c.wait_read(dve, qr + u)
    for b in range(KB):
        dve.wait_ge(S["rw_z_read"], 3 * b + 2)
        ch.step(v.tensor_tensor_scan(c.xn[:, b, :], c.c("reset"), W[3][:, b, :], 0.0, ALU.mult, ALU.add))
        ins = v.tensor_tensor(W[3][:, b, :], c.xn[:, b, :], W[3][:, b, :], ALU.subtract)
        if b < KB - 1:
            ch.step(ins)
        else:
            ins.then_inc(S["rw_before"], 1)
        ch.step(v.tensor_scalar(W[6][:, b, :], W[4][:, b, :], -1.0, c.p("rwkv_k_a_3", b), ALU.add, ALU.mult))
        ch.step(v.scalar_tensor_tensor(out=W[1][:, b, :], in0=W[6][:, b, :], scalar=1.0,
                                       in1=W[1][:, b, :], op0=ALU.add, op1=ALU.mult))
        ch.step(v.tensor_tensor(W[4][:, b, :], W[4][:, b, :], W[0][:, b, :], ALU.mult))
        v.scalar_tensor_tensor(out=W[6][:, b, :], in0=W[7][:, b, :], scalar=c.p("rwkv_r_k_3", b),
                               in1=W[1][:, b, :], op0=ALU.mult, op1=ALU.mult).then_inc(S["rw_rk"], 1)
    dve.wait_ge(S["rw_exp"], 1)
    v.tensor_tensor(W[0][:, :, :], W[0][:, :, :], W[3][:, :, :], ALU.mult).then_inc(S["rw_tilde"], 1)
    dve.wait_ge(S["rw_exp"], 2)
    v.tensor_tensor(W[4][:, :, :], W[4][:, :, :], V.grow, ALU.mult).then_inc(S["rw_tilde"], 1)
    v.memset(V.state, 0.0).then_inc(S["rw_tilde"], 1)
    dve.wait_ge(S["rw_exp"], 3)
    ch.step(v.tensor_copy(V.pend, W[6][:, :, CHUNK - 1:T:CHUNK]))
    _, qv = PLAN["rw_v"]
    for u in range(4):
        c.wait_read(dve, qv + u)
    dve.wait_ge(S["rw_rk_sum"], 1)
    for g in range(4):
        v.tensor_tensor(V.bonus[:, 2 * g:2 * g + 2, :], c.ps[:, 4 + g, :].rearrange("p (m t) -> p m t", m=2),
                        W[2][:, 2 * g:2 * g + 2, :], ALU.mult).then_inc(S["rw_bonus"], 1)

    def four(name):
        return c.c(name).rearrange("p (a t) -> p a t", a=1).to_broadcast([P, 4, P])

    def bank(g):
        return c.ps[:, g, :].rearrange("p (r t) -> p r t", r=4)

    dve.wait_ge(S["rw_turn_read"], 12)
    dve.wait_ge(S["rw_tilde"], 3)
    dve.wait_ge(S["rw_pool"], 2)
    for n in range(2):
        if n:
            dve.wait_ge(S["rw_y"], 2)
        for g in range(4):
            dve.wait_ge(S["rw_inv_mm"], pe_step(n, "z", 0, g))
            v.tensor_tensor(rw_z4(V, g), bank(4 + g), four("level1"), ALU.mult).then_inc(S["rw_inv"], 1)
        for g in range(4):
            dve.wait_ge(S["rw_inv"], vec_step(n, "z", 0, g))
            v.tensor_tensor(V.inv[:, 4 * g:4 * g + 4, :], four("ident"), rw_z4(V, g), ALU.subtract)\
                .then_inc(S["rw_inv"], 1)
        for g in range(4):
            dve.wait_ge(S["rw_inv_mm"], pe_step(n, "zt", 0, g))
            v.tensor_tensor(V.invt[:, 4 * g:4 * g + 4, :], four("ident"), bank(g), ALU.subtract)\
                .then_inc(S["rw_inv"], 1)
        for l in range(1, 6):
            for g in range(4):
                dve.wait_ge(S["rw_inv_mm"], pe_step(n, "z", l, g))
                v.tensor_tensor(rw_z4(V, g), bank(4 + g), four(f"level{LEVELS[l]}"), ALU.mult)\
                    .then_inc(S["rw_inv"], 1)
            for g in range(4):
                q4, x4 = V.inv[:, 4 * g:4 * g + 4, :], V.invt[:, 4 * g:4 * g + 4, :]
                dve.wait_ge(S["rw_inv_mm"], pe_step(n, "q", l, g))
                v.tensor_tensor(q4, q4, bank(g), ALU.subtract).then_inc(S["rw_inv"], 1)
                if l < 5:
                    dve.wait_ge(S["rw_inv_mm"], pe_step(n, "x", l, g))
                    v.tensor_tensor(x4, x4, bank(4 + g), ALU.subtract).then_inc(S["rw_inv"], 1)
        dve.wait_ge(S["rw_inv_mm"], pe_step(n, "q", 5, 3))
        for j, (mask, dst) in enumerate((("before", None), ("upto", None), ("upto", None))):
            for g in range(4):
                dve.wait_ge(S["rw_mat_mm"], 12 * n + 4 * j + g + 1)
                dst = (V.gk[:, 4 * g:4 * g + 4, :], V.rb[:, 4 * g:4 * g + 4, :], rw_z4(V, g))[j]
                v.tensor_tensor(dst, bank((4 + g) if j == 1 else g), four(mask), ALU.mult)\
                    .then_inc(S["rw_mat"], 1)
        if n:
            for b in range(KB):
                ch.step(v.scalar_tensor_tensor(out=V.bonus[:, b, :], in0=V.bonus[:, b, :],
                                               scalar=c.p("rwkv_ln_b_3", b), in1=W[5][:, b, :],
                                               op0=ALU.add, op1=ALU.mult))
                ch.step(v.tensor_scalar(W[5][:, b, :], W[5][:, b, :], c.p("rwkv_ln_w_3", b), None, ALU.mult))
        for cc in range(2):
            ci = 2 * n + cc
            if ci < 3:
                dve.wait_ge(S["rw_s"], ci + 1)
                end = V.pend[:, :, ci:ci + 1].to_broadcast([P, 8, 64])
                ch.step(v.tensor_tensor(V.state, V.state, c.ps[:, 6, :].rearrange("p (b i) -> p b i", b=8),
                                        ALU.add))
                v.tensor_tensor(V.state, V.state, end, ALU.mult).then_inc(S["rw_state"], 1)
                dve.wait_ge(S["rw_state"], ci + 1)
            dve.wait_ge(S["rw_y_read"], ci + 1)
            for e in range(2):
                half = slice(64 * e, 64 * e + 64)
                y = W[7][half, :, ci * 64:ci * 64 + 64]
                v.tensor_tensor(y, y, c.ps[half, 7 - 2 * e, :].rearrange("p (b t) -> p b t", b=8), ALU.add)\
                    .then_inc(S["rw_y_add"], 1)
    dve.wait_ge(S["rw_y_add"], 8)
    for g in range(4):
        dve.wait_ge(S["rw_mean"], g + 1)
        y = W[7][:, 2 * g:2 * g + 2, :]
        v.tensor_tensor(y, y, c.ps[:, g, :].rearrange("p (m t) -> p m t", m=2), ALU.subtract)\
            .then_inc(S["rw_cen"], 1)
    dve.wait_ge(S["rw_cen"], 4)
    for g in range(4):
        sl = (slice(None), slice(2 * g, 2 * g + 2), slice(None))
        ch.step(v.tensor_tensor(W[5][sl], W[5][sl], W[7][sl], ALU.mult))
        dve.wait_ge(S["rw_cen_sq"], g + 1)
        dve.wait_ge(S["rw_gn_std"], g + 1)
        ch.step(v.reciprocal(W[2][sl], W[2][sl]))
        ch.step(v.tensor_tensor(W[5][sl], W[5][sl], W[2][sl], ALU.mult))
        v.tensor_tensor(W[7][sl], W[5][sl], V.bonus[sl], ALU.add).then_inc(S["rw_out"], 1)
    add_residual(c, dve, "rw_out", PLAN["rw_out"][0] + 3, 1.0, gain)


def b3_scalar(c, act):
    for b in range(4):
        act.wait_ge(c.S["ln_out"], 8 + 2 * b + 2)
        squares(c, NK["l0_ffn1"], b, c.h)
    rms_root(c, act, NK["l0_ffn1"])
    swiglu_scalar(c, act, "l0_ffn1", 0)
    rw_scalar(c, act, RESID.index("l0_ffn1"))
    xattn_scalar(c, act, 0, RESID.index("rw_out"))
    ffn3(c, "l0_ffn2", 1)[0](act, RESID.index("l0_xo"))
    ffn3(c, "l1_ffn1", 2)[0](act, RESID.index("l0_ffn2"))
    gmlp_scalar(c, act, RESID.index("l1_ffn1"))
    xattn_scalar(c, act, 1, RESID.index("gm_out"))
    ffn3(c, "l1_ffn2", 3)[0](act, RESID.index("l1_xo"))
    rms_scalar(c, act, NK["final"], RESID.index("l1_ffn2"))


def b3_tensor(c, pe):
    ffn3(c, "l0_ffn1", 0)[1](pe)
    pe.wait_ge(c.S["late_loaded"], 16)
    rw_tensor(c, pe)
    xattn_tensor(c, pe, 0)
    ffn3(c, "l0_ffn2", 1)[1](pe)
    ffn3(c, "l1_ffn1", 2)[1](pe)
    gmlp_tensor(c, pe)
    xattn_tensor(c, pe, 1)
    ffn3(c, "l1_ffn2", 3)[1](pe)
    rms_tensor(c, pe, NK["final"])


def gain_of(name, layer):
    return lambda b: (name, 8 * layer + b)


def b3_vector(c, dve, ch):
    dve.wait_ge(c.S["late_loaded"], 16)
    dve.wait_ge(c.S["ln_out"], 16)
    for b in range(4):
        gain_blocks(c, b, gain_of("ffn1_norm_3", 0), c.h)
    ffn3(c, "l0_ffn1", 0)[2](dve, ch, gain_of("mix_norm_3", 0))
    rw_vector(c, dve, ch, gain_of("xattn_norm_3", 0))
    xattn_vector(c, dve, 0, ch, gain_of("ffn2_norm_3", 0))
    ffn3(c, "l0_ffn2", 1)[2](dve, ch, gain_of("ffn1_norm_3", 1))
    ffn3(c, "l1_ffn1", 2)[2](dve, ch, gain_of("mix_norm_3", 1))
    gmlp_vector(c, dve, ch, gain_of("xattn_norm_3", 1))
    xattn_vector(c, dve, 1, ch, gain_of("ffn2_norm_3", 1))
    ffn3(c, "l1_ffn2", 3)[2](dve, ch, None)
    rms_vector_gain(c, dve, NK["final"], gain_of("final_norm_3", 0), c.h, c.h)


def skewed(flat, offset, n):
    return bass.AP(tensor=flat.tensor, offset=flat.offset + offset,
                   ap=[[383, P], [P * 384, 8], [1, n]])


def build(nc, x, params, consts, late_consts, stream, decay, gates, rel_bias, w_pool, bias_rows, mem, lora1,
          lora_wa, lora_g, spatial, spatial_b, out):
    with ExitStack() as ctx:
        c = Ctx(nc, ctx, None)
        S = c.S
        block = ctx.enter_context(nc.Block())

        @block.sync
        def _(sp):
            sp.dma_start(c.h[:, :, :], x).then_inc(S["x_loaded"], 16)
            sp.dma_start(c.par[:, :], params).then_inc(S["par_loaded"], 16)
            for s in range(UNITS):
                sp.dma_start(c.ring[:, s, :], stream[s]).then_inc(S[f"unit_loaded{s}"], 16)
            with sp.Fori(1, N_UNITS // UNITS) as r:
                for s in range(UNITS):
                    unit = sp.snap(r * UNITS + s)
                    sp.wait_ge(S[f"unit_done{s}"], r)
                    sp.dma_start(c.ring[:, s, :], stream[bass.ds(unit, 1)].rearrange("a p n -> (a p) n"))\
                        .then_inc(S[f"unit_loaded{s}"], 16)
            for i in range(2):
                sp.wait_ge(S["xn_ready"], 8 * len(NORMS) - 4 + 4 * i)
                sp.dma_start(out[:, 4 * i:4 * i + 4, :], c.h[:, 4 * i:4 * i + 4, :]).then_inc(S["out_stored"], 16)
            sp.wait_ge(S["out_stored"], 32)

        @block.scalar
        def _(act):
            act.dma_start(c.con[:, 0:N_COMMON], consts[:, 0:N_COMMON]).then_inc(S["common_loaded"], 16)
            act.dma_start(c.con[:, N_COMMON:consts.shape[1]], consts[:, N_COMMON:]).then_inc(S["con_loaded"], 16)
            act.dma_start(c.table[:, :, :], decay).then_inc(S["decay_loaded"], 16)
            act.dma_start(c.gates[:, :, :, :], gates).then_inc(S["gates_loaded"], 16)
            act.wait_ge(S["b1_pad"], 1)
            b1_scalar(c, act)
            b2_scalar(c, act)
            b3_scalar(c, act)

        @block.tensor
        def _(pe):
            b1_tensor(c, pe)
            b2_tensor(c, pe)
            b3_tensor(c, pe)

        @block.vector
        def _(dve):
            ch = Chain(dve, S["vector_step"])
            b1_vector(c, dve, ch)
            b2_vector(c, dve, ch)
            b3_vector(c, dve, ch)

        @block.gpsimd
        def _(pool):
            pool.dma_start(c.relb[0:32, :], rel_bias).then_inc(S["relb_loaded"], 16)
            pool.dma_start(c.wpool[:, :, :], w_pool).then_inc(S["wpool_loaded"], 16)
            pool.wait_ge(S["h_ready"], HR["b1_out"])
            pool.dma_start(c.work[7][:, :, :], mem).then_inc(S["mem_loaded"], 16)
            pool.wait_ge(S["b2_bias_read"], 1)
            pool.dma_start(bias_rows.rearrange("h p y -> h p y"),
                           c.relg[0:8, :].rearrange("h (a y) -> h a y", a=1).to_broadcast([8, P, 384]))\
                .then_inc(S["bias_stored"], 16)
            pool.wait_ge(S["bias_stored"], 16)
            pool.wait_ge(S["b1_prob"], 8)
            flat = bias_rows.rearrange("h p y -> (h p y)")
            pool.dma_start(c.table[:, :, P:384], skewed(flat, 127, T)).then_inc(S["bias_loaded"], 16)
            pool.dma_start(c.table[:, :, 0:P], skewed(flat, 127 + P, P)).then_inc(S["bias_loaded"], 16)
            pool.wait_ge(S["b2_bias_read"], 1)
            pool.wait_ge(S["b2_pooled"], 1)
            pool.dma_start(c.con[:, N_COMMON:N_COMMON + N_LATE], late_consts).then_inc(S["late_loaded"], 16)
            V = rw_views(c)
            pool.wait_ge(S["h_ready"], HR["l0_ffn1"])
            pool.dma_start(V.lora1, lora1).then_inc(S["lora_loaded"], 16)
            pool.dma_start(V.lora_wa, lora_wa).then_inc(S["lora_loaded"], 16)
            pool.dma_start(V.lora_g, lora_g[0:P, :]).then_inc(S["lora_loaded"], 16)
            pool.dma_start(V.lora_gt, lora_g[P:160, :]).then_inc(S["lora_loaded"], 16)
            W = c.work
            pool.wait_ge(S["rw_rk"], 8)
            pool.wait_ge(S["rw_exp"], 2)
            nc.gpsimd.tensor_tensor(W[1][:, :, :], W[1][:, :, :], V.grow, ALU.mult).then_inc(S["rw_pool"], 1)
            pool.wait_ge(S["rw_exp"], 3)
            nc.gpsimd.tensor_tensor(W[7][:, :, :], W[7][:, :, :], W[6][:, :, :], ALU.mult)\
                .then_inc(S["rw_pool"], 1)
            pool.wait_ge(S["h_ready"], HR["l0_xo"])
            pool.dma_start(c.work[2][:, :, :], spatial).then_inc(S["gm_loaded"], 16)
            pool.dma_start(c.work[3][:, :, :].rearrange("p a b -> p (a b)"),
                           spatial_b.rearrange("(a n) -> a n", a=1).to_broadcast([P, 2048]))\
                .then_inc(S["gm_loaded"], 16)


def p_units(w):
    n = w.shape[1] // 256
    return [u for u in w.reshape(KB, P, n, 256).transpose(2, 1, 0, 3).reshape(n, P, UNIT)]


def d_units(w):
    n = w.shape[0] // 256
    return [u for u in w.reshape(n, 2, P, C).transpose(0, 2, 1, 3).reshape(n, P, UNIT)]


def ffn_units(w_in, w_out, gate_first=True):
    g, u, d = p_units(w_in[:, :FF]), p_units(w_in[:, FF:]), d_units(w_out)
    if not gate_first:
        g, u = u, g
    out = [g[0], u[0], g[1], u[1], d[0]]
    for j in range((FFI - 3) // 2):
        i = 2 * j + 2
        out += [g[i], u[i], d[i - 1], g[i + 1], u[i + 1], d[i]]
    return out + [g[FFI - 1], u[FFI - 1], d[FFI - 2], d[FFI - 1]]


def kernel(**inputs):
    import concourse.bacc as bacc
    from concourse.bass_utils import run_bass_kernel_spmd as run

    a = {k: np.asarray(v) for k, v in inputs.items()}
    w1 = a["w_in"]
    cut = [w1[:, i * C:(i + 1) * C] for i in range(6)]
    units = []
    for i in (4, 0, 1, 2, 3, 5):
        units += p_units(cut[i])
    units += d_units(a["w_out"])
    w2 = a["w_in_2"][0]
    mixers = p_units(w2)
    units += mixers[:6] + [mixers[9], mixers[7], mixers[8], mixers[6]] + d_units(a["w_out_2"][0])
    mem_units = p_units(a["mem_w_kv_3"])
    units += mem_units[:4] + ffn_units(a["w_up_2"][0], a["w_down_2"][0], False) + mem_units[4:]
    for i in range(2):
        units += ffn_units(a["ffn1_w_in_3"][i], a["ffn1_w_out_3"][i])
        if i == 0:
            units += p_units(a["rwkv_w_rkv_3"][0]) + d_units(a["rwkv_w_o_3"][0])
        else:
            uv = a["gmlp_w_uv_3"][0]
            units += p_units(uv) + d_units(a["gmlp_w_o_3"][0])
        units += p_units(a["xattn_wq_3"][i]) + d_units(a["xattn_wo_3"][i])
        units += ffn_units(a["ffn2_w_in_3"][i], a["ffn2_w_out_3"][i])
    while len(units) < N_UNITS:
        units.append(np.zeros((P, UNIT), np.float32))
    arrays = {"stream": np.stack(units)}
    cols = []
    for name, width in PARAMS:
        v = a[name].reshape(-1, P)
        assert v.shape[0] == width, name
        cols.append(v.T)
    arrays["params"] = np.ascontiguousarray(np.concatenate(cols, 1))
    arrays["consts"] = np.concatenate([CONSTS[n] for n in COMMON + EARLY], 1)
    arrays["late_consts"] = np.concatenate([CONSTS[n] for n in LATE], 1)
    arrays["decay"] = DECAY.reshape(P, 8, 384)
    arrays["x"] = np.ascontiguousarray(a["x"][0].T.reshape(KB, P, T).transpose(1, 0, 2))
    arrays["gates"] = np.ascontiguousarray(
        np.stack([a["gate_a_w"], a["gate_x_w"]]).transpose(2, 0, 1, 3))
    arrays["rel_bias"] = np.ascontiguousarray(a["rel_bias_2"].T)
    pool = np.zeros((P, 2, P), np.float32)
    for g in range(4):
        e = 64 * (g % 2)
        pool[e:e + 64, g // 2, e:e + 64] = a["w_pool_2"][0, g]
    arrays["w_pool"] = pool
    arrays["mem"] = np.ascontiguousarray(a["mem_3"][0].T.reshape(KB, P, T).transpose(1, 0, 2))
    lora = np.concatenate([a["rwkv_w1_3"][0], a["rwkv_a1_3"][0], a["rwkv_g1_3"][0]], 1)
    arrays["lora1"] = np.ascontiguousarray(lora.reshape(KB, P, -1).transpose(1, 0, 2))
    arrays["lora_wa"] = np.concatenate([a["rwkv_w2_3"][0], a["rwkv_a2_3"][0]], 0)
    arrays["lora_g"] = np.ascontiguousarray(a["rwkv_g2_3"][0])
    arrays["spatial"] = np.ascontiguousarray(a["gmlp_w_s_3"][0].transpose(2, 0, 1)).reshape(P, KB, T)
    arrays["spatial_b"] = a["gmlp_b_s_3"].reshape(-1)
    nc = bacc.Bacc("TRN2", target_bir_lowering=False, num_devices=1)
    args = {n: nc.dram_tensor(n, v.shape, F32, kind="ExternalInput").ap() for n, v in arrays.items()}
    args["bias_rows"] = nc.dram_tensor("bias_rows", (8, P, 384), F32, kind="Internal").ap()
    args["out"] = nc.dram_tensor("out", (P, KB, T), F32, kind="ExternalOutput").ap()
    build(nc, **args)
    r = run(nc, [arrays], core_ids=[0])
    o = np.asarray(r.results[0]["out"])
    return np.ascontiguousarray(o.transpose(1, 0, 2).reshape(C, T).T)[None]
```
